# Optimizing a Trainium2 kernel written in Bass

```python
import jax, jax.numpy as jnp
from jax import lax
import numpy as np
import math

D_MODEL = 1024
BATCH = 1
SEQ = 512
DEPTH = 2

HEAD_DIM = 64
BLOCK = 128
A_Q_HEADS = 8
A_KV_HEADS = 2
A_GROUP = A_Q_HEADS // A_KV_HEADS
A_WINDOW = 128
B_HEADS = 8
C_HEADS = 16
C_PATTERNS = ((128, 1), (512, 4), (2048, 16))
MEM_LEN = 256
X_HEADS = 4
X_HEAD_DIM = D_MODEL // X_HEADS
D_FF = 2816
RMS_EPS = 1e-6

A_Q_W = A_Q_HEADS * HEAD_DIM
A_KV_W = A_KV_HEADS * HEAD_DIM
B_W = B_HEADS * HEAD_DIM
EVEN_IN = A_Q_W + 2 * A_KV_W + 3 * B_W
EVEN_MIX = A_Q_W + B_W
ODD_IN = 3 * C_HEADS * HEAD_DIM
ODD_MIX = C_HEADS * HEAD_DIM


def rms_norm(x, g):
    xf = x.astype(jnp.float32)
    y = xf * lax.rsqrt(jnp.mean(xf * xf, axis=-1, keepdims=True) + RMS_EPS)
    return (y * g.astype(jnp.float32)).astype(x.dtype)

def alibi_slopes(n_heads):
    return jnp.asarray(2.0 ** (-8.0 * np.arange(1, n_heads + 1) / n_heads), dtype=jnp.float32)

def swiglu_ffn(x, w_gu, w_down):
    gate, up = jnp.split(x @ w_gu, 2, axis=-1)
    return (jax.nn.silu(gate) * up) @ w_down

def banded_attention(q, k, v, slopes, max_dist, step, sinks=None):
    b, l, hkv, g, dh = q.shape
    nb = -(-l // BLOCK)
    lp = nb * BLOCK
    pad = lp - l
    qb = jnp.pad(q, ((0, 0), (0, pad), (0, 0), (0, 0), (0, 0))).reshape(b, nb, BLOCK, hkv, g, dh)
    kv_pad = ((0, 0), (BLOCK, pad), (0, 0), (0, 0))
    k = jnp.pad(k, kv_pad).reshape(b, nb + 1, BLOCK, hkv, dh)
    v = jnp.pad(v, kv_pad).reshape(b, nb + 1, BLOCK, hkv, dh)
    kb = jnp.concatenate([k[:, :-1], k[:, 1:]], axis=2)
    vb = jnp.concatenate([v[:, :-1], v[:, 1:]], axis=2)
    s = jnp.einsum('bnqhgd,bnkhd->bnhgqk', qb, kb).astype(jnp.float32) * (dh ** -0.5)
    dist = jnp.arange(BLOCK)[:, None] + BLOCK - jnp.arange(2 * BLOCK)[None, :]
    kpos = jnp.arange(nb)[:, None] * BLOCK - BLOCK + jnp.arange(2 * BLOCK)[None, :]
    valid = (dist >= 0) & (dist <= max_dist) & (kpos[:, None, :] >= 0)
    bias = -(slopes.astype(jnp.float32) * step)[:, :, None, None] * dist.astype(jnp.float32)
    s = jnp.where(valid[None, :, None, None], s + bias[None, None], -jnp.inf)
    m = jnp.max(s, axis=-1)
    if sinks is not None:
        sk = sinks.astype(jnp.float32)[..., None]
        m = jnp.maximum(m, sk)
    p = jnp.exp(s - m[..., None])
    denom = jnp.sum(p, axis=-1)
    if sinks is not None:
        denom = denom + jnp.exp(sk - m)
    o = jnp.einsum('bnhgqk,bnkhd->bnqhgd', (p / denom[..., None]).astype(v.dtype), vb)
    lse = m + jnp.log(denom)
    o = o.reshape(b, lp, hkv, g, dh)[:, :l]
    lse = jnp.moveaxis(lse, -1, 2).reshape(b, lp, hkv, g)[:, :l]
    return o, lse

def stick_breaking_attention(q, k, v):
    b, s, h, dh = q.shape
    nb = s // BLOCK
    qb = q.reshape(b, nb, BLOCK, h, dh).transpose(1, 0, 2, 3, 4)
    spos = jnp.arange(s)
    scale = dh ** -0.5

    def one_block(args):
        i, qi = args
        z = jnp.einsum('bqhd,bkhd->bhqk', qi, k).astype(jnp.float32) * scale
        tpos = i * BLOCK + jnp.arange(BLOCK)
        strict = spos[None, :] < tpos[:, None]
        log_keep = jnp.where(strict, jax.nn.log_sigmoid(-z), 0.0)
        log_after = lax.cumsum(log_keep, axis=3, reverse=True) - log_keep
        a = jnp.where(strict, jnp.exp(jax.nn.log_sigmoid(z) + log_after), 0.0)
        return jnp.einsum('bhqk,bkhd->bqhd', a.astype(v.dtype), v)

    o = lax.map(one_block, (jnp.arange(nb), qb))
    return o.transpose(1, 0, 2, 3, 4).reshape(b, s, h, dh)

def dilated_attention(q, k, v, slopes):
    b, s, h, dh = q.shape
    outs, lses = [], []
    for window, dil in C_PATTERNS:
        sp = -(-s // dil) * dil
        ls = sp // dil

        def strided(t):
            t = jnp.pad(t, ((0, 0), (0, sp - s), (0, 0), (0, 0)))
            return t.reshape(b, ls, dil, h, dh).transpose(0, 2, 1, 3, 4).reshape(b * dil, ls, h, dh)

        o, lse = banded_attention(strided(q)[:, :, :, None], strided(k), strided(v),
                                  slopes[:, None], window // dil, dil)
        o = o[:, :, :, 0].reshape(b, dil, ls, h, dh).transpose(0, 2, 1, 3, 4).reshape(b, sp, h, dh)[:, :s]
        lse = lse[..., 0].reshape(b, dil, ls, h).transpose(0, 2, 1, 3).reshape(b, sp, h)[:, :s]
        outs.append(o)
        lses.append(lse)
    w = jax.nn.softmax(jnp.stack(lses), axis=0)
    o = jnp.sum(w[..., None] * jnp.stack(outs).astype(jnp.float32), axis=0)
    return o.astype(q.dtype)

def even_mixer(h, w_in, q_gain, k_gain, sinks, w_out):
    b, s, _ = h.shape
    cuts = np.cumsum([A_Q_W, A_KV_W, A_KV_W, B_W, B_W]).tolist()
    qa, ka, va, qb, kb, vb = jnp.split(h @ w_in, cuts, axis=-1)
    qa = rms_norm(qa.reshape(b, s, A_KV_HEADS, A_GROUP, HEAD_DIM), q_gain)
    ka = rms_norm(ka.reshape(b, s, A_KV_HEADS, HEAD_DIM), k_gain)
    va = va.reshape(b, s, A_KV_HEADS, HEAD_DIM)
    slopes_a = alibi_slopes(A_Q_HEADS).reshape(A_KV_HEADS, A_GROUP)
    o_a, _ = banded_attention(qa, ka, va, slopes_a, A_WINDOW - 1, 1,
                              sinks.reshape(A_KV_HEADS, A_GROUP))
    o_b = stick_breaking_attention(qb.reshape(b, s, B_HEADS, HEAD_DIM),
                                   kb.reshape(b, s, B_HEADS, HEAD_DIM),
                                   vb.reshape(b, s, B_HEADS, HEAD_DIM))
    o = jnp.concatenate([o_a.reshape(b, s, A_Q_W), o_b.reshape(b, s, B_W)], axis=-1)
    return o @ w_out

def odd_mixer(h, w_in, q_gain, k_gain, w_out):
    b, s, _ = h.shape
    qkv = (h @ w_in).reshape(b, s, 3, C_HEADS, HEAD_DIM)
    q = rms_norm(qkv[:, :, 0], q_gain)
    k = rms_norm(qkv[:, :, 1], k_gain)
    o = dilated_attention(q, k, qkv[:, :, 2], alibi_slopes(C_HEADS))
    return o.reshape(b, s, ODD_MIX) @ w_out

def memory_cross_attention(h, m, w_q, w_kv, q_gain, k_gain, w_o):
    b, s, _ = h.shape
    q = rms_norm((h @ w_q).reshape(b, s, X_HEADS, X_HEAD_DIM), q_gain)
    kv = (m @ w_kv).reshape(b, m.shape[1], 2, X_HEADS, X_HEAD_DIM)
    k = rms_norm(kv[:, :, 0], k_gain)
    v = kv[:, :, 1]
    sc = jnp.einsum('bqhd,bkhd->bhqk', q, k).astype(jnp.float32) * (X_HEAD_DIM ** -0.5)
    p = jax.nn.softmax(sc, axis=-1).astype(v.dtype)
    o = jnp.einsum('bhqk,bkhd->bqhd', p, v).reshape(b, s, X_HEADS * X_HEAD_DIM)
    return o @ w_o

def first_inputs(seed: int = 0) -> dict:
    key = jax.random.key(seed)
    k = jax.random.split(key, 25)
    n_even = (DEPTH + 1) // 2
    n_odd = DEPTH // 2
    f32 = jnp.float32

    def dense(kk, shape, fan_in):
        return jax.random.normal(kk, shape, f32) * (fan_in ** -0.5)

    def gain(kk, shape):
        return 1.0 + 0.02 * jax.random.normal(kk, shape, f32)

    return {
        'x': jax.random.normal(k[0], (BATCH, SEQ, D_MODEL), f32),
        'mem': jax.random.normal(k[1], (BATCH, MEM_LEN, D_MODEL), f32),
        'ffn1_norm': gain(k[2], (DEPTH, D_MODEL)),
        'ffn1_w_gu': dense(k[3], (DEPTH, D_MODEL, 2 * D_FF), D_MODEL),
        'ffn1_w_down': dense(k[4], (DEPTH, D_FF, D_MODEL), D_FF),
        'mix_norm': gain(k[5], (DEPTH, D_MODEL)),
        'ev_w_in': dense(k[6], (n_even, D_MODEL, EVEN_IN), D_MODEL),
        'ev_q_gain': gain(k[7], (n_even, HEAD_DIM)),
        'ev_k_gain': gain(k[8], (n_even, HEAD_DIM)),
        'ev_sinks': 0.5 * jax.random.normal(k[9], (n_even, A_Q_HEADS), f32),
        'ev_w_out': dense(k[10], (n_even, EVEN_MIX, D_MODEL), EVEN_MIX),
        'od_w_in': dense(k[11], (n_odd, D_MODEL, ODD_IN), D_MODEL),
        'od_q_gain': gain(k[12], (n_odd, HEAD_DIM)),
        'od_k_gain': gain(k[13], (n_odd, HEAD_DIM)),
        'od_w_out': dense(k[14], (n_odd, ODD_MIX, D_MODEL), ODD_MIX),
        'xa_norm': gain(k[15], (DEPTH, D_MODEL)),
        'xa_mem_norm': gain(k[16], (DEPTH, D_MODEL)),
        'xa_w_q': dense(k[17], (DEPTH, D_MODEL, X_HEADS * X_HEAD_DIM), D_MODEL),
        'xa_w_kv': dense(k[18], (DEPTH, D_MODEL, 2 * X_HEADS * X_HEAD_DIM), D_MODEL),
        'xa_q_gain': gain(k[19], (DEPTH, X_HEAD_DIM)),
        'xa_k_gain': gain(k[20], (DEPTH, X_HEAD_DIM)),
        'xa_w_o': dense(k[21], (DEPTH, X_HEADS * X_HEAD_DIM, D_MODEL), X_HEADS * X_HEAD_DIM),
        'ffn2_norm': gain(k[22], (DEPTH, D_MODEL)),
        'ffn2_w_gu': dense(k[23], (DEPTH, D_MODEL, 2 * D_FF), D_MODEL),
        'ffn2_w_down': dense(k[24], (DEPTH, D_FF, D_MODEL), D_FF),
    }

def first_block(x, mem, ffn1_norm, ffn1_w_gu, ffn1_w_down, mix_norm,
              ev_w_in, ev_q_gain, ev_k_gain, ev_sinks, ev_w_out,
              od_w_in, od_q_gain, od_k_gain, od_w_out,
              xa_norm, xa_mem_norm, xa_w_q, xa_w_kv, xa_q_gain, xa_k_gain, xa_w_o,
              ffn2_norm, ffn2_w_gu, ffn2_w_down):
    for layer in range(DEPTH):
        x = x + 0.5 * swiglu_ffn(rms_norm(x, ffn1_norm[layer]), ffn1_w_gu[layer], ffn1_w_down[layer])
        h = rms_norm(x, mix_norm[layer])
        if layer % 2 == 0:
            j = layer // 2
            x = x + even_mixer(h, ev_w_in[j], ev_q_gain[j], ev_k_gain[j], ev_sinks[j], ev_w_out[j])
        else:
            j = layer // 2
            x = x + odd_mixer(h, od_w_in[j], od_q_gain[j], od_k_gain[j], od_w_out[j])
        x = x + memory_cross_attention(rms_norm(x, xa_norm[layer]), rms_norm(mem, xa_mem_norm[layer]),
                                       xa_w_q[layer], xa_w_kv[layer], xa_q_gain[layer],
                                       xa_k_gain[layer], xa_w_o[layer])
        x = x + 0.5 * swiglu_ffn(rms_norm(x, ffn2_norm[layer]), ffn2_w_gu[layer], ffn2_w_down[layer])
    return x


DEPTH_2 = 1

D_RNN = 1024
N_RNN_BLOCKS = 16
RNN_BLOCK = D_RNN // N_RNN_BLOCKS
CONV_WIDTH = 4
LRU_C = 8.0
N_HEADS = 16
N_KV_HEADS = 4
ROT_DIM = HEAD_DIM // 4
ROPE_THETA = 500000.0
N_IDX_HEADS = 8
IDX_DIM = 64
IDX_ROT_DIM = IDX_DIM // 4
TOPK_MAX = 256
Q_BLOCK = 128
D_FF_2 = -(-8 * D_MODEL // (3 * 256)) * 256
EPS = 1e-6

IN_SPLITS = (D_RNN, D_RNN, N_HEADS * HEAD_DIM, N_KV_HEADS * HEAD_DIM, N_KV_HEADS * HEAD_DIM,
             N_IDX_HEADS * IDX_DIM, IDX_DIM, N_IDX_HEADS, D_MODEL, D_MODEL)
D_IN = sum(IN_SPLITS)


def rms_norm_2(x, g):
    x32 = x.astype(jnp.float32)
    y = x32 * lax.rsqrt(jnp.mean(x32 * x32, axis=-1, keepdims=True) + EPS)
    return (y * g.astype(jnp.float32)).astype(x.dtype)

def layer_norm(x, g, b):
    x32 = x.astype(jnp.float32)
    mu = jnp.mean(x32, axis=-1, keepdims=True)
    var = jnp.mean(jnp.square(x32 - mu), axis=-1, keepdims=True)
    y = (x32 - mu) * lax.rsqrt(var + EPS)
    return (y * g.astype(jnp.float32) + b.astype(jnp.float32)).astype(x.dtype)

def partial_rope(x, rot_dim):
    s = x.shape[1]
    half = rot_dim // 2
    inv_freq = ROPE_THETA ** (-jnp.arange(half, dtype=jnp.float32) / half)
    ang = jnp.arange(s, dtype=jnp.float32)[:, None] * inv_freq[None, :]
    cos = jnp.cos(ang)[None, :, None, :]
    sin = jnp.sin(ang)[None, :, None, :]
    xr = x[..., :rot_dim].astype(jnp.float32)
    x1, x2 = xr[..., :half], xr[..., half:]
    rot = jnp.concatenate([x1 * cos - x2 * sin, x2 * cos + x1 * sin], axis=-1).astype(x.dtype)
    return jnp.concatenate([rot, x[..., rot_dim:]], axis=-1)

def causal_depthwise_conv(x, w, b):
    s = x.shape[1]
    xp = jnp.pad(x, ((0, 0), (CONV_WIDTH - 1, 0), (0, 0)))
    out = b
    for k in range(CONV_WIDTH):
        out = out + xp[:, k:k + s] * w[k]
    return out

def rg_lru(x, w_a, b_a, w_x, b_x, lam):
    bsz, s, _ = x.shape
    xb = x.reshape(bsz, s, N_RNN_BLOCKS, RNN_BLOCK)
    r = jax.nn.sigmoid(jnp.einsum('bshi,hij->bshj', xb, w_a).reshape(bsz, s, D_RNN) + b_a)
    i = jax.nn.sigmoid(jnp.einsum('bshi,hij->bshj', xb, w_x).reshape(bsz, s, D_RNN) + b_x)
    log_a = (-LRU_C * r.astype(jnp.float32)) * jax.nn.softplus(-lam.astype(jnp.float32))
    a = jnp.exp(log_a)
    u = jnp.sqrt(-jnp.expm1(2.0 * log_a)) * (i * x).astype(jnp.float32)

    def combine(left, right):
        a_l, b_l = left
        a_r, b_r = right
        return a_r * a_l, a_r * b_l + b_r

    _, h = lax.associative_scan(combine, (a, u), axis=1)
    return h.astype(x.dtype)

def dsa_sparse_attention(q, k, v, iq, ik, iw):
    bsz, s = q.shape[0], q.shape[1]
    topk = min(TOPK_MAX, s // 4)
    n_blk = s // Q_BLOCK
    rep = N_HEADS // N_KV_HEADS
    key_pos = jnp.arange(s)
    gather = jax.vmap(lambda t, idx: t[idx])

    def to_blocks(t):
        return jnp.moveaxis(t.reshape(bsz, n_blk, Q_BLOCK, *t.shape[2:]), 1, 0)

    def one_block(args):
        blk, qb, iqb, iwb = args
        q_pos = blk * Q_BLOCK + jnp.arange(Q_BLOCK)
        causal = key_pos[None, :] <= q_pos[:, None]
        logits = jnp.einsum('bqhd,bsd->bqhs', iqb, ik, preferred_element_type=jnp.float32)
        score = jnp.einsum('bqhs,bqh->bqs', jax.nn.relu(logits), iwb.astype(jnp.float32))
        score = jnp.where(causal[None], score, -jnp.inf)
        _, idx = lax.top_k(score, topk)
        valid = idx <= q_pos[None, :, None]
        k_sel = gather(k, idx)
        v_sel = gather(v, idx)
        qg = qb.reshape(bsz, Q_BLOCK, N_KV_HEADS, rep, HEAD_DIM)
        att = jnp.einsum('bqgrd,bqkgd->bqgrk', qg, k_sel,
                         preferred_element_type=jnp.float32) * (HEAD_DIM ** -0.5)
        att = jnp.where(valid[:, :, None, None, :], att, -jnp.inf)
        p = jax.nn.softmax(att, axis=-1).astype(v.dtype)
        o = jnp.einsum('bqgrk,bqkgd->bqgrd', p, v_sel)
        return o.reshape(bsz, Q_BLOCK, N_HEADS * HEAD_DIM)

    out = lax.map(one_block, (jnp.arange(n_blk), to_blocks(q), to_blocks(iq), to_blocks(iw)))
    return jnp.moveaxis(out, 0, 1).reshape(bsz, s, N_HEADS * HEAD_DIM)

def second_inputs(seed: int = 0) -> dict:
    key = jax.random.key(seed)
    ks = jax.random.split(key, 24)
    f32 = jnp.float32

    def nrm(k, shape, fan_in):
        return jax.random.normal(k, shape, f32) * (fan_in ** -0.5)

    def gain(k, shape):
        return 1.0 + 0.05 * jax.random.normal(k, shape, f32)

    L = DEPTH_2
    u = jax.random.uniform(ks[9], (L, D_RNN), f32, 0.9, 0.999)
    s_lam = u ** (1.0 / LRU_C)
    rg_lambda = jnp.log(s_lam) - jnp.log1p(-s_lam)
    return {
        "x": jax.random.normal(ks[0], (BATCH, SEQ, D_MODEL), f32),
        "norm_mix_pre": gain(ks[1], (L, D_MODEL)),
        "w_in": nrm(ks[2], (L, D_MODEL, D_IN), D_MODEL),
        "conv_w": nrm(ks[3], (L, CONV_WIDTH, D_RNN), CONV_WIDTH),
        "conv_b": 0.02 * jax.random.normal(ks[4], (L, D_RNN), f32),
        "rg_w_a": nrm(ks[5], (L, N_RNN_BLOCKS, RNN_BLOCK, RNN_BLOCK), RNN_BLOCK),
        "rg_b_a": 0.02 * jax.random.normal(ks[6], (L, D_RNN), f32),
        "rg_w_x": nrm(ks[7], (L, N_RNN_BLOCKS, RNN_BLOCK, RNN_BLOCK), RNN_BLOCK),
        "rg_b_x": 0.02 * jax.random.normal(ks[8], (L, D_RNN), f32),
        "rg_lambda": rg_lambda,
        "idx_k_ln_g": gain(ks[10], (L, IDX_DIM)),
        "idx_k_ln_b": 0.02 * jax.random.normal(ks[11], (L, IDX_DIM), f32),
        "w_rnn_out": nrm(ks[12], (L, D_RNN, D_MODEL), D_RNN),
        "w_att_out": nrm(ks[13], (L, N_HEADS * HEAD_DIM, D_MODEL), N_HEADS * HEAD_DIM),
        "w_o": nrm(ks[14], (L, D_MODEL, D_MODEL), D_MODEL),
        "norm_mix_post": gain(ks[15], (L, D_MODEL)),
        "norm_ffn_pre": gain(ks[16], (L, D_MODEL)),
        "w_ffn_gate": nrm(ks[17], (L, D_MODEL, D_FF_2), D_MODEL),
        "w_ffn_up": nrm(ks[18], (L, D_MODEL, D_FF_2), D_MODEL),
        "w_ffn_down": nrm(ks[19], (L, D_FF_2, D_MODEL), D_FF_2),
        "norm_ffn_post": gain(ks[20], (L, D_MODEL)),
    }

def second_block(x, norm_mix_pre, w_in, conv_w, conv_b, rg_w_a, rg_b_a, rg_w_x, rg_b_x, rg_lambda,
              idx_k_ln_g, idx_k_ln_b, w_rnn_out, w_att_out, w_o, norm_mix_post,
              norm_ffn_pre, w_ffn_gate, w_ffn_up, w_ffn_down, norm_ffn_post):
    bsz, s, _ = x.shape
    idx_w_scale = (N_IDX_HEADS ** -0.5) * (IDX_DIM ** -0.5)
    for l in range(DEPTH_2):
        h = rms_norm_2(x, norm_mix_pre[l])
        proj = h @ w_in[l]
        parts = []
        start = 0
        for width in IN_SPLITS:
            parts.append(proj[..., start:start + width])
            start += width
        xr, gr, q, k, v, iq, ik, iw, g_a, g_b = parts

        xc = causal_depthwise_conv(xr, conv_w[l], conv_b[l])
        y_rnn = rg_lru(xc, rg_w_a[l], rg_b_a[l], rg_w_x[l], rg_b_x[l], rg_lambda[l]) * jax.nn.gelu(gr)
        y_a = y_rnn @ w_rnn_out[l]

        q = partial_rope(q.reshape(bsz, s, N_HEADS, HEAD_DIM), ROT_DIM)
        k = partial_rope(k.reshape(bsz, s, N_KV_HEADS, HEAD_DIM), ROT_DIM)
        v = v.reshape(bsz, s, N_KV_HEADS, HEAD_DIM)
        iq = partial_rope(iq.reshape(bsz, s, N_IDX_HEADS, IDX_DIM), IDX_ROT_DIM)
        ik = layer_norm(ik, idx_k_ln_g[l], idx_k_ln_b[l])
        ik = partial_rope(ik[:, :, None, :], IDX_ROT_DIM)[:, :, 0, :]
        iw = iw * idx_w_scale
        y_att = dsa_sparse_attention(q, k, v, iq, ik, iw)
        y_b = y_att @ w_att_out[l]

        merged = jax.nn.sigmoid(g_a) * y_a + jax.nn.sigmoid(g_b) * y_b
        mix = merged @ w_o[l]
        x = x + rms_norm_2(mix, norm_mix_post[l])

        h = rms_norm_2(x, norm_ffn_pre[l])
        f = (jax.nn.silu(h @ w_ffn_gate[l]) * (h @ w_ffn_up[l])) @ w_ffn_down[l]
        x = x + rms_norm_2(f, norm_ffn_post[l])
    return x


def setup_inputs(seed=0):
    out = dict(first_inputs(seed))
    for name, value in second_inputs(seed + 1).items():
        if name != "x":
            out[name + "_2"] = value
    return out


def reference(
    x, mem, ffn1_norm, ffn1_w_gu, ffn1_w_down, mix_norm, ev_w_in, ev_q_gain, ev_k_gain,
    ev_sinks, ev_w_out, od_w_in, od_q_gain, od_k_gain, od_w_out, xa_norm, xa_mem_norm, xa_w_q,
    xa_w_kv, xa_q_gain, xa_k_gain, xa_w_o, ffn2_norm, ffn2_w_gu, ffn2_w_down, norm_mix_pre_2,
    w_in_2, conv_w_2, conv_b_2, rg_w_a_2, rg_b_a_2, rg_w_x_2, rg_b_x_2, rg_lambda_2,
    idx_k_ln_g_2, idx_k_ln_b_2, w_rnn_out_2, w_att_out_2, w_o_2, norm_mix_post_2,
    norm_ffn_pre_2, w_ffn_gate_2, w_ffn_up_2, w_ffn_down_2, norm_ffn_post_2,
):
    x = first_block(
        x, mem, ffn1_norm, ffn1_w_gu, ffn1_w_down, mix_norm, ev_w_in, ev_q_gain, ev_k_gain,
        ev_sinks, ev_w_out, od_w_in, od_q_gain, od_k_gain, od_w_out, xa_norm, xa_mem_norm,
        xa_w_q, xa_w_kv, xa_q_gain, xa_k_gain, xa_w_o, ffn2_norm, ffn2_w_gu, ffn2_w_down,
    )
    return second_block(
        x, norm_mix_pre_2, w_in_2, conv_w_2, conv_b_2, rg_w_a_2, rg_b_a_2, rg_w_x_2, rg_b_x_2,
        rg_lambda_2, idx_k_ln_g_2, idx_k_ln_b_2, w_rnn_out_2, w_att_out_2, w_o_2,
        norm_mix_post_2, norm_ffn_pre_2, w_ffn_gate_2, w_ffn_up_2, w_ffn_down_2,
        norm_ffn_post_2,
    )


_drawn_inputs = setup_inputs


def setup_inputs(seed=0):
    import zlib

    import numpy as np

    out = dict(_drawn_inputs(seed))
    spreads = {}
    factors = {'ev_q_gain': 6.151,
     'ev_k_gain': 6.383,
     'od_q_gain': 5.528,
     'od_k_gain': 5.283,
     'xa_norm': 6.424,
     'xa_mem_norm': 4.963,
     'xa_q_gain': 6.896,
     'xa_k_gain': 6.875,
     'ffn2_norm': 2.851,
     'rg_b_a_2': 64.0,
     'rg_b_x_2': 64.0,
     'idx_k_ln_b_2': 31.0,
     'norm_mix_pre_2': 4.854,
     'conv_b_2': 3.711,
     'idx_k_ln_g_2': 8.0,
     'norm_mix_post_2': 8.0,
     'norm_ffn_pre_2': 6.181,
     'norm_ffn_post_2': 8.0}
    for name, (base, spread) in spreads.items():
        noise = np.random.default_rng([zlib.crc32(name.encode()), seed]).standard_normal(out[name].shape)
        drawn = base * np.exp(spread * noise) if base else spread * noise
        out[name] = __import__('jax').numpy.asarray(drawn.astype(out[name].dtype))
    for name, factor in factors.items():
        out[name] = (out[name] * factor).astype(out[name].dtype)
    return out
```

```python
from contextlib import ExitStack

import numpy as np

import concourse.bass as bass
from concourse import mybir

F32 = mybir.dt.float32
F32R = mybir.dt.float32r
ALU = mybir.AluOpType
AF = mybir.ActivationFunctionType
AX = mybir.AxisListType.X

P = 128
S = 512
NT = S // P
D = 1024
KD = D // P
FF = 2816
KF = FF // P
MEM = 256
EPS = 1e-6
NEG = -1.0e30
FLOOR = -3.0e38
TAKEN = -3.3e38
NRAW = 4
NW = 4
AHEAD = 3


class Sem:

    def __init__(self, handle):
        self.handle = handle
        self.count = 0


class Queue:

    def __init__(self, sem):
        self.sem = sem
        self.items = []
        self.met = {}

    def wait(self, *tokens):
        for t in tokens:
            if t is None:
                continue
            if isinstance(t, list):
                self.wait(*t)
                continue
            sem, value = t
            if self.met.get(sem, 0) < value:
                self.met[sem] = value
                self.items.append(lambda e, h=sem.handle, v=value: e.wait_ge(h, v))

    def do(self, fn, *tokens, mark=True):
        self.wait(*tokens)
        if not mark:
            self.items.append(fn)
            return None
        self.sem.count += 1
        self.items.append(lambda e, h=self.sem.handle: fn(e).then_inc(h, 1))
        return (self.sem, self.sem.count)

    def dma(self, out, in_, sem, *tokens):
        self.wait(*tokens)
        sem.count += 16
        self.items.append(lambda e, h=sem.handle: e.dma_start(out, in_).then_inc(h, 16))
        return (sem, sem.count)

    def now(self):
        return (self.sem, self.sem.count) if self.sem.count else None

    def play(self, engine):
        for item in self.items:
            item(engine)


class Bank:
    def __init__(self, ap):
        self.ap = ap
        self.free = []


class Area:

    def __init__(self, at):
        self.at = at

    def take(self, nc, name, shape, dt):
        n = 4 * int(np.prod(shape[1:]))
        t = nc.alloc_sbuf_tensor_at(name, shape, dt, offset=self.at)
        self.at += -(-n // 32) * 32
        return t

    def sub(self, skip=0):
        return Area(self.at + skip)


class Act:

    def __init__(self, hi, lo, n):
        self.hi, self.lo, self.n = hi, lo, n
        self.tok = {}
        self.free = []


def params_layout():
    names = []
    for l in range(2):
        names += [(f"ffn1_norm{l}", 8), (f"mix_norm{l}", 8), (f"xa_norm{l}", 8), (f"xa_mem_norm{l}", 8),
                  (f"ffn2_norm{l}", 8), (f"xa_q_gain{l}", 2), (f"xa_k_gain{l}", 2)]
    names += [("ev_q_gain", 1), ("ev_k_gain", 1), ("od_q_gain", 1), ("od_k_gain", 1), ("ev_sinks", 8),
              ("norm_mix_pre", 8), ("norm_ffn_pre", 8), ("conv_b", 8), ("rg_b_a", 8), ("rg_b_x", 8),
              ("rg_lambda", 8), ("conv_w", 32)]
    at, off = {}, 0
    for n, w in names:
        at[n] = (off, w)
        off += w
    return at, off


PRM, NPRM = params_layout()
MISC = {"ident": (0, 128), "strict": (128, 128), "causal": (256, 128), "cos": (384, 32), "sin": (416, 32)}
NMISC = 448


def program(nc, T, out, stop=None):
    ctx = ExitStack()

    def sb(name, shape, dt=F32, area=None):
        if area is None:
            return ctx.enter_context(nc.sbuf_tensor(name, shape, dt))
        return area.take(nc, name, shape, dt)

    def sem(name):
        return Sem(ctx.enter_context(nc.semaphore(name)))

    pe, act, dve, pool, sp = (Queue(sem("s_" + n)) for n in ("pe", "act", "dve", "pool", "sp"))
    s_st = sem("s_st")
    s_cst = sem("s_cst")
    banks = [Bank(ctx.enter_context(nc.psum_tensor(f"ps{i}", [P, 512], F32))) for i in range(8)]

    x = sb("x", [P, NT, D])
    hTh = sb("hTh", [P, KD, S], F32R)
    hTl = sb("hTl", [P, KD, S], F32R)
    hT = Act(hTh, hTl, S)
    raw = [sb(f"raw{i}", [P, 2, 512]) for i in range(NRAW)]
    wh = [sb(f"wh{i}", [P, 2, 512], F32R) for i in range(NW)]
    wl = [sb(f"wl{i}", [P, 2, 512], F32R) for i in range(NW)]
    s_raw = [sem(f"s_raw{i}") for i in range(NRAW)]
    xn = [sb(f"xn{i}", [P, D]) for i in range(2)]
    xn_free = [[], []]
    prm = sb("prm", [P, NPRM])
    misc = sb("misc", [P, NMISC])
    half = sb("half", [P, 64])
    stat = sb("stat", [P, 16])
    ident = misc[:, 0:128]
    base = -(-nc.sbuf_base // 64) * 64

    def par(name):
        o, w = PRM[name]
        return prm[:, o:o + w]

    def mis(name):
        o, w = MISC[name]
        return misc[:, o:o + w]

    t_cst = [sp.dma(prm[:, :], T["prm"], s_cst), sp.dma(misc[:, :], T["misc"], s_cst)][-1]
    s_x = [sem(f"s_x{t}") for t in range(NT)]
    xtok = [[sp.dma(x[:, t, :], T["x"][0, t * P:(t + 1) * P, :], s_x[t])] for t in range(NT)]
    t_half = pool.do(lambda e: e.memset(half[:, :], -0.5))

    def gate_up(name, wg, wu, a="h"):
        return (name, KD, [[(wg, c, 256, a, "A"), (wu, c, 256, a, "A")] for c in range(0, FF, 256)])

    def rows(name, w, K, widths, a="h", form="B", c0=0):
        groups = []
        for n in widths:
            groups.append([(w, c0, n, a, form)])
            c0 += n
        return (name, K, groups)

    GEMMS = []
    for l in range(2):
        wgu, wd = T["ffn1_w_gu"][l], T["ffn1_w_down"][l]
        GEMMS.append(gate_up(f"f1u{l}", wgu[:, 0:FF], wgu[:, FF:2 * FF]))
        GEMMS.append(rows(f"f1d{l}", wd, KF, [512, 512], "f"))
        if l == 0:
            w = T["ev_w_in"][0]
            GEMMS.append((f"in{l}", KD, [[(w, 0, 512, "h", "B")], [(w, 512, 256, "h", "B")], [(w, 1792, 512, "h", "B")],
                                         [(w, 768, 512, "h", "A")], [(w, 1280, 512, "h", "A")]]))
            GEMMS.append(rows(f"out{l}", T["ev_w_out"][0], KD, [512, 512]))
        else:
            w = T["od_w_in"][0]
            GEMMS.append(rows(f"in{l}", w, KD, [512] * 6))
            GEMMS.append(rows(f"out{l}", T["od_w_out"][0], KD, [512, 512]))
        GEMMS.append(rows(f"kv{l}", T["xa_w_kv"][l], KD, [512] * 4, "m"))
        GEMMS.append(rows(f"xq{l}", T["xa_w_q"][l], KD, [512] * 2))
        GEMMS.append(rows(f"xo{l}", T["xa_w_o"][l], KD, [512] * 2))
        wgu, wd = T["ffn2_w_gu"][l], T["ffn2_w_down"][l]
        GEMMS.append(gate_up(f"f2u{l}", wgu[:, 0:FF], wgu[:, FF:2 * FF]))
        GEMMS.append(rows(f"f2d{l}", wd, KF, [512, 512], "f"))
    w = T["w_in_2"][0]
    GEMMS.append(("idx", KD, [[(w, 3584, 512, "h", "B")], [(w, 4096, 72, "h", "B")]]))
    GEMMS.append(rows("qkv", w, KD, [512] * 3, c0=2048))
    GEMMS.append(("rnn", KD, [[(w, c, 256, "h", "A"), (w, 1024 + c, 256, "h", "A")] for c in range(0, 1024, 256)]))
    GEMMS.append(("ya", KD, [[(w, 4168 + c, 256, "h", "A"), (T["w_rnn_out_2"][0], c, 256, "y", "A")]
                             for c in range(0, 1024, 256)]))
    GEMMS.append(rows("gb", w, KD, [512] * 2, form="A", c0=5192))
    GEMMS.append(rows("yb", T["w_att_out_2"][0], KD, [512] * 2, form="A"))
    GEMMS.append(rows("wo", T["w_o_2"][0], KD, [512] * 2, "y"))
    GEMMS.append(gate_up("f3u", T["w_ffn_gate_2"][0], T["w_ffn_up_2"][0]))
    GEMMS.append(rows("f3d", T["w_ffn_down_2"][0], KF, [512, 512], "f"))

    stream = [(segs, kp) for _, K, groups in GEMMS for segs in groups for kp in range(K // 2)]
    first = {}
    n = 0
    for name, K, groups in GEMMS:
        first[name] = n
        n += len(groups) * K // 2
    spec = {g[0]: g for g in GEMMS}
    t_raw, t_hi, t_lo, t_used = {}, {}, {}, {}
    done = {"load": 0, "split": 0}

    def load(n):
        if n >= len(stream):
            return
        segs, kp = stream[n]
        r = n % NRAW
        old = n - NRAW
        o = 0
        for w, c, width, _, _ in segs:
            t_raw[n] = sp.dma(raw[r][:, :, o:o + width],
                              w[kp * 256:(kp + 1) * 256, c:c + width].rearrange("(c p) n -> p c n", p=P),
                              s_raw[r], t_hi.get(old), t_lo.get(old))
            o += width

    def split(n):
        if n >= len(stream):
            return
        W = sum(s[2] for s in stream[n][0])
        r, i = n % NRAW, n % NW
        src, hi, lo = raw[r][:, :, 0:W], wh[i][:, :, 0:W], wl[i][:, :, 0:W]
        t_hi[n] = act.do(lambda e: e.activation(hi, src, AF.Copy), t_raw[n], t_used.get(n - NW))
        t_lo[n] = dve.do(lambda e: e.tensor_tensor(lo, src, hi.bitcast(F32), ALU.subtract),
                         t_raw[n], t_hi[n], t_used.get(n - NW))

    def advance(n):
        while done["split"] <= n + AHEAD:
            while done["load"] < done["split"] + NRAW:
                load(done["load"])
                done["load"] += 1
            split(done["split"])
            done["split"] += 1

    later = []
    background = []
    side = [0]

    def flush():
        while later:
            later.pop(0)()

    def take_half():
        side[0] ^= 1
        return banks[4 * side[0]:4 * side[0] + 4]

    def gemm(name, acts, on_group, background_per_chunk=0):
        _, K, groups = spec[name]
        n = first[name]
        for g, segs in enumerate(groups):
            bk = take_half()
            jobs, o, b = [], 0, 0
            for _, _, width, a, form in segs:
                A = acts[a]
                if form == "A":
                    for j in range(width // P):
                        jobs.append((bk[b], A, "A", slice(o + j * P, o + (j + 1) * P), slice(0, A.n)))
                        b += 1
                else:
                    for t in range(A.n // P):
                        jobs.append((bk[b], A, "B", slice(o, o + width), slice(t * P, (t + 1) * P)))
                        b += 1
                o += width
            toks = []
            for kp in range(K // 2):
                advance(n)
                i = n % NW
                pe.wait(t_hi[n], t_lo[n])
                for kk in range(2):
                    k = 2 * kp + kk
                    for bank, A, form, wc, tc in jobs:
                        pe.wait(A.tok[k])
                        if k == 0:
                            pe.wait(bank.free)
                        Wh, Wl = wh[i][:, kk, wc], wl[i][:, kk, wc]
                        Ah, Al = A.hi[:, k, tc], A.lo[:, k, tc]
                        for q, (p0, p1) in enumerate(((Wh, Ah), (Wh, Al), (Wl, Ah)) if form == "A" else
                                                     ((Ah, Wh), (Ah, Wl), (Al, Wh))):
                            M = (wc.stop - wc.start) if form == "B" else A.n
                            end = k == K - 1 and q == 2
                            t = pe.do(lambda e, o_=bank.ap[:, 0:M], l_=p0, r_=p1, s_=(k == 0 and q == 0), e_=end:
                                      e.matmul(o_, l_, r_, start=s_, stop=e_),
                                      mark=end or (q == 2 and kk == 1 and bank is jobs[-1][0]))
                            if end:
                                toks.append(t)
                        t_used[n] = t
                for _ in range(background_per_chunk):
                    if background:
                        background.pop(0)()
                n += 1
            for job in jobs:
                job[1].free = [t_used[n - 1]]
            flush()
            on_group(g, [j[0] for j in jobs], toks)

    def rstd(src, dst, scale, *tokens):
        t = pool.do(lambda e: e.tensor_scalar(dst, src, scale, EPS, ALU.mult, ALU.add), *tokens)
        w = dst.shape[1]
        return pool.do(lambda e: e.tensor_tensor(dst, dst, half[:, 0:w], ALU.pow), t, t_half)

    def halves(src, A, k, cols, tokens, scale=None):
        hi, lo = A.hi[:, k, cols], A.lo[:, k, cols]
        if scale is None:
            t = act.do(lambda e: e.activation(hi, src, AF.Copy), tokens, A.free)
            t2 = dve.do(lambda e: e.tensor_tensor(lo, src, hi.bitcast(F32), ALU.subtract), t, tokens, A.free)
        else:
            t = act.do(lambda e: e.activation(hi, src, AF.Copy, scale=scale), tokens, A.free)
            t2 = dve.do(lambda e: e.scalar_tensor_tensor(lo, src, scale, hi.bitcast(F32), ALU.mult, ALU.subtract),
                        t, tokens, A.free)
        A.tok[k] = [t, t2]
        return t2

    def norm(src, toks, gain, A):
        nt = A.n // P
        last = {}
        for t in range(nt):
            b = t % 2
            buf = xn[b]
            t1 = act.do(lambda e, t=t, buf=buf: e.activation(buf[:, :], src[:, t, :], AF.Square,
                                                             accum_out=stat[:, t:t + 1]), toks[t], xn_free[b],
                        stat_free)
            t2 = rstd(stat[:, t:t + 1], stat[:, 8 + t:9 + t], 1.0 / D, t1, stat_free)
            t3 = dve.do(lambda e, t=t, buf=buf: e.tensor_scalar(buf[:, :], src[:, t, :], stat[:, 8 + t:9 + t], None,
                                                                ALU.mult), t1, t2, toks[t])
            for c in range(KD):
                if t == 0:
                    pe.wait(banks[c].free)
                last[c] = pe.do(lambda e, c=c, t=t, buf=buf: e.transpose(banks[c].ap[:, t * P:(t + 1) * P],
                                                                         buf[:, c * P:(c + 1) * P], ident),
                                t3, t_cst, mark=t == nt - 1 or c == KD - 1)
            xn_free[b] = [last[KD - 1]]
        stat_free[:] = [t3]
        for c in range(KD):
            banks[c].free = [halves(banks[c].ap[:, 0:A.n], A, c, slice(0, A.n), last[c], gain[:, c:c + 1])]

    stat_free = []

    def add_to_x(scale):
        def on_group(g, bk, toks):
            for t in range(NT):
                xs = x[:, t, g * 512:(g + 1) * 512]
                tk = dve.do(lambda e, xs=xs, b=bk[t]: e.scalar_tensor_tensor(xs, b.ap[:, :], scale, xs, ALU.mult,
                                                                             ALU.add), toks[t], xtok[t])
                bk[t].free = [tk]
                xtok[t] = [tk]
        return on_group

    def handover():
        toks = [q.now() for q in (pe, act, dve, pool)]
        for q in (act, dve, pool, sp):
            q.wait(*toks)

    def copy_out(engine, dst, src, *tokens):
        if engine is act:
            return act.do(lambda e: e.activation(dst, src, AF.Copy), *tokens)
        return engine.do(lambda e: e.tensor_copy(dst, src), *tokens)

    def head_norm(tmp, t, nh, hd, sq, ss, tok, sq_free):
        v = tmp[:, t, :].rearrange("p (h d) -> p h d", h=nh)
        s3 = sq[:, :].rearrange("p (h d) -> p h d", h=nh)
        t1 = dve.do(lambda e: e.tensor_tensor(sq[:, :], tmp[:, t, :], tmp[:, t, :], ALU.mult), tok, sq_free)
        r = ss[:, t, 0:nh]
        t2 = dve.do(lambda e: e.tensor_reduce(r, s3, AX, ALU.add), t1)
        xn_free[0] = [t2]
        t3 = rstd(r, r, 1.0 / hd, t2)
        return dve.do(lambda e: e.tensor_tensor(v, v, r.unsqueeze(2).to_broadcast([P, nh, hd]), ALU.mult), t3, t2)

    def turn(tmp, tt, blocks, bk, dsts, gains, nt, last_use):
        toks = []
        for c in range(blocks):
            bank = bk[c]
            pe.wait(bank.free)
            for t in range(nt):
                tk = pe.do(lambda e, c=c, t=t, bank=bank: e.transpose(bank.ap[:, t * P:(t + 1) * P],
                                                                      tmp[:, t, c * P:(c + 1) * P], ident),
                           tt[t], mark=t == nt - 1)
            last_use.append(tk)
            if gains is None:
                q = act if c % 2 else dve
                r = copy_out(q, dsts[c], bank.ap[:, 0:nt * P], tk)
            elif c % 2:
                r = act.do(lambda e, c=c, bank=bank: e.activation(dsts[c], bank.ap[:, 0:nt * P], AF.Copy,
                                                                  scale=gains[c]), tk)
            else:
                r = dve.do(lambda e, c=c, bank=bank: e.tensor_scalar(dsts[c], bank.ap[:, 0:nt * P], gains[c], None,
                                                                     ALU.mult), tk)
            bank.free = [r]
            toks.append(r)
        return toks

    def widths(lo, n):
        out_, o = [], 0
        for i in range(n):
            k0, k1 = lo(i)
            out_.append((k0, k1, o, (k1 - k0) * P))
            o += (k1 - k0) * P
        return out_, o

    def attend(st, tag, H, tiles, score, value, O, mode="softmax", bias=None, sink=None, scale=1.0, nk=NT,
               before=None, st2=None):
        spans, total = tiles
        Pb = [sb(f"{tag}P{i}", [P, total], F32, st) for i in range(2)]
        PT = [sb(f"{tag}PT{i}", [P, nk, S], F32, st2 or st) for i in range(2)]
        sm = [sb(f"{tag}sm{i}", [P, 24], F32, st) for i in range(2)]
        stick = mode == "stick"
        Qb = [sb(f"{tag}Q{i}", [P, total + NT], F32, st) for i in range(2)] if stick else None
        Zr = sb(f"{tag}Z", [P, 512], F32, st) if stick else None
        P_free, PT_free = [[], []], [[], []]
        ready, turned = {}, {}
        t_one = None
        if stick:
            t_one = [pool.do(lambda e: e.memset(Zr[:, :], 0.0))]
            t_one += [pool.do(lambda e, b=b: e.memset(Qb[b][:, :], 1.0)) for b in range(2)]

        def first_half(h):
            b = h % 2
            p, m = Pb[b], sm[b]
            mx, nm, den, es, rd = (m[:, 4 * i:4 * i + 4] for i in range(5))
            got = []
            for i, (k0, k1, o, W) in enumerate(spans):
                bank = banks[i]
                pe.wait(bank.free)
                tk = score(h, i, bank.ap[:, 0:W], k0, k1)
                pw = p[:, o:o + W]
                if stick:
                    dg = bank.ap[:, W - P:W]
                    t0 = dve.do(lambda e, dg=dg: e.tensor_tensor(dg, dg, mis("strict"), ALU.add), tk, t_cst)
                    kp_ = Qb[b][:, o + i:o + i + W]
                    t1 = act.do(lambda e, pw=pw, s=bank.ap[:, 0:W]: e.activation(pw, s, AF.Sigmoid), t0, P_free[b],
                                t_one)
                    t2 = act.do(lambda e, kp_=kp_, s=bank.ap[:, 0:W]: e.activation(kp_, s, AF.Sigmoid, scale=-1.0),
                                P_free[b], t_one)
                    bank.free = [t2]
                    got.append((t1, t2))
                elif bias is not None:
                    bt, btok = bias(h, i, W)
                    t1 = dve.do(lambda e, pw=pw, s=bank.ap[:, 0:W], bt=bt, i=i: e.tensor_tensor_reduce(
                        pw, s, bt, 1.0, FLOOR, ALU.add, ALU.max, mx[:, i:i + 1]), tk, btok, P_free[b])
                    bank.free = [t1]
                    got.append(t1)
                else:
                    t1 = dve.do(lambda e, s=bank.ap[:, 0:W], i=i: e.tensor_reduce(mx[:, i:i + 1], s, AX, ALU.max),
                                tk, P_free[b])
                    got.append(t1)
            if stick:
                ready[h] = got
                return
            if sink is not None:
                t2 = dve.do(lambda e: e.tensor_scalar(nm, mx, sink[:, h:h + 1], -1.0, ALU.max, ALU.mult), got)
            else:
                t2 = dve.do(lambda e: e.tensor_scalar(nm, mx, -scale, None, ALU.mult), got)
            for i, (k0, k1, o, W) in enumerate(spans):
                pw = p[:, o:o + W]
                src = pw if bias is not None else banks[i].ap[:, 0:W]
                t3 = act.do(lambda e, pw=pw, src=src, i=i: e.activation(pw, src, AF.Exp, bias=nm[:, i:i + 1],
                                                                        scale=scale, accum_out=den[:, i:i + 1]),
                            t2, P_free[b])
                if bias is None:
                    banks[i].free = [t3]
            if sink is not None:
                t3 = act.do(lambda e: e.activation(es, nm, AF.Exp, bias=sink[:, h:h + 1]), t2)
            ready[h] = t3

        def second_half(h):
            b = h % 2
            p, m = Pb[b], sm[b]
            den, es, rd = (m[:, 4 * i:4 * i + 4] for i in range(2, 5))
            toks = []
            if stick:
                for i, (k0, k1, o, W) in enumerate(spans):
                    q = Qb[b][:, o + i:o + i + W + 1]
                    t1, t2 = ready[h][i]
                    rev = Qb[b][:, o + i:o + i + W][:, ::-1]
                    t3 = dve.do(lambda e, rev=rev, W=W: e.tensor_tensor_scan(rev, rev, Zr[:, 0:W], 1.0, ALU.mult,
                                                                             ALU.add), t1, t2, t_one)
                    pw = p[:, o:o + W]
                    toks.append(dve.do(lambda e, pw=pw, q=q, W=W: e.tensor_tensor(pw, pw, q[:, 1:W + 1], ALU.mult), t3))
                ready[h] = toks
                return
            t = ready[h]
            if sink is not None:
                t = dve.do(lambda e: e.tensor_tensor(den, den, es, ALU.add), t)
            t = dve.do(lambda e: e.reciprocal(rd, den), t)
            for i, (k0, k1, o, W) in enumerate(spans):
                pw = p[:, o:o + W]
                toks.append(dve.do(lambda e, pw=pw, i=i: e.tensor_scalar(pw, pw, rd[:, i:i + 1], None, ALU.mult), t))
            ready[h] = toks

        def turn_head(h):
            b = h % 2
            cp = []
            for i, (k0, k1, o, W) in enumerate(spans):
                bank = banks[4 + i % 2]
                pe.wait(bank.free)
                nb = k1 - k0
                for j in range(nb):
                    tk = pe.do(lambda e, j=j, o=o, bank=bank: e.transpose(
                        bank.ap[:, j * P:(j + 1) * P], Pb[b][:, o + j * P:o + (j + 1) * P], ident),
                        ready[h][i], mark=j == nb - 1)
                dst = PT[b][:, k0:k1, i * P:(i + 1) * P]
                src = bank.ap[:, 0:W].rearrange("p (k q) -> p k q", k=nb)
                t = copy_out(dve if i % 2 else act, dst, src, tk, PT_free[b])
                bank.free = [t]
                cp.append(t)
            P_free[b] = [tk]
            turned[h] = cp

        def product(h):
            b = h % 2
            pe.wait(turned[h])
            PT_free[b] = [value(h, PT[b])]

        for s in range(H + 2):
            if s < H:
                if before is not None:
                    before(s)
                first_half(s)
            if 1 <= s <= H:
                turn_head(s - 1)
            if s >= 2:
                product(s - 2)
            if s < H:
                second_half(s)

    def causal_scores(qT, kT, qtok, ktok, kv_of, dup):
        def score(h, i, dst, k0, k1):
            r = slice(64 * (h % 2), 64 * (h % 2) + 64)
            kb = kv_of(h) if dup else h // 2
            return pe.do(lambda e: e.matmul(dst, qT[r, h // 2, i * P:(i + 1) * P], kT[r, kb, k0 * P:k1 * P],
                                            start=True, stop=True), qtok[h // 2], ktok[kb])
        return score

    def pair_values(V, O, base, spans, causal, vtok):
        def value(h, PTb):
            pair = h // 2
            bank = banks[6 + pair % 2]
            if h % 2 == 0:
                pe.wait(bank.free)
            pe.wait(vtok)
            r = slice(64 * (h % 2), 64 * (h % 2) + 64)
            if causal:
                for kt in range(NT):
                    t = pe.do(lambda e, kt=kt: e.matmul(bank.ap[r, kt * P:S], V(h, kt), PTb[:, kt, kt * P:S],
                                                        start=kt == 0, stop=kt == NT - 1), mark=kt == NT - 1)
            else:
                for i, (k0, k1, o, W) in enumerate(spans):
                    for kt in range(k0, k1):
                        t = pe.do(lambda e, kt=kt, i=i, k0=k0, k1=k1: e.matmul(
                            bank.ap[r, i * P:(i + 1) * P], V(h, kt), PTb[:, kt, i * P:(i + 1) * P],
                            start=kt == k0, stop=kt == k1 - 1), mark=i == NT - 1 and kt == k1 - 1)
            if h % 2 == 1:
                bank.free = [halves(bank.ap[:, :], O, base + pair, slice(0, S), t)]
            return t
        return value

    causal_tiles = widths(lambda i: (0, i + 1), NT)

    def even_mixer(st):
        handover()
        s_b = sem("s_evb")
        evb = sb("evb", [P, 8 * 256], F32, st)
        t_evb = sp.dma(evb[:, :], T["evb"], s_b)
        qs = sb("e_qs", [P, 1], F32, st)
        ta = sb("e_ta", [P, NT, 512], F32, st)
        tk_ = sb("e_tk", [P, NT, 256], F32, st)
        kd = sb("e_kd", [P, NT, 256], F32, st)
        vb = sb("e_vb", [P, NT, 512], F32, st)
        ss = sb("e_ss", [P, NT, 8], F32, st)
        sk = sb("e_sk", [P, NT, 2], F32, st)
        qaT = sb("e_qaT", [P, 4, S], F32, st)
        kaT = sb("e_kaT", [P, 2, S], F32, st)
        qbT = sb("e_qbT", [P, 4, S], F32, st)
        kbT = sb("e_kbT", [P, 4, S], F32, st)
        t_qs = dve.do(lambda e: e.tensor_scalar(qs[:, :], par("ev_q_gain"), 0.125, None, ALU.mult), t_cst)
        tok = {"q": [], "k": [], "vb": [], "qb": [], "kb": []}

        def on_group(g, bk, toks):
            if g == 0:
                tt = []
                for t in range(NT):
                    e1 = copy_out(act, ta[:, t, :], bk[t].ap[:, :], toks[t])
                    bk[t].free = [e1]
                    tt.append(head_norm(ta, t, 8, 64, xn[0][:, 0:512], ss, e1, xn_free[0]))
                later.append(lambda: tok["q"].extend(
                    turn(ta, tt, 4, bk, [qaT[:, c, :] for c in range(4)], [qs[:, :]] * 4, NT, [])))
                dve.wait(t_qs)
                act.wait(t_qs)
            elif g == 1:
                tt = []
                for t in range(NT):
                    e1 = copy_out(act, tk_[:, t, :], bk[t].ap[:, 0:256], toks[t])
                    bk[t].free = [e1]
                    sq = xn[1][:, 0:128]
                    k3 = tk_[:, t, 0:128].rearrange("p (h d) -> p h d", h=2)
                    t1 = dve.do(lambda e, t=t: e.tensor_tensor(sq, tk_[:, t, 0:128], tk_[:, t, 0:128], ALU.mult), e1,
                                xn_free[1])
                    r = sk[:, t, :]
                    t2 = dve.do(lambda e, r=r: e.tensor_reduce(r, sq.rearrange("p (h d) -> p h d", h=2), AX, ALU.add), t1)
                    xn_free[1] = [t2]
                    t3 = rstd(r, r, 1.0 / 64, t2)
                    kdv = kd[:, t, :].rearrange("p (h u d) -> p h u d", h=2, u=2)
                    for u in range(2):
                        t4 = dve.do(lambda e, r=r, u=u, kdv=kdv, k3=k3: e.tensor_tensor(
                            kdv[:, :, u, :], k3, r.unsqueeze(2).to_broadcast([P, 2, 64]), ALU.mult), t3)
                    tt.append(t4)
                later.append(lambda: tok["k"].extend(
                    turn(kd, tt, 2, bk, [kaT[:, c, :] for c in range(2)], [par("ev_k_gain")] * 2, NT, [])))
            elif g == 2:
                for t in range(NT):
                    e1 = copy_out(act if t % 2 else dve, vb[:, t, :], bk[t].ap[:, :], toks[t])
                    bk[t].free = [e1]
                    tok["vb"].append(e1)
            else:
                for c in range(4):
                    if g == 3:
                        e1 = act.do(lambda e, c=c: e.activation(qbT[:, c, :], bk[c].ap[:, :], AF.Copy, scale=0.125),
                                    toks[c])
                    else:
                        e1 = copy_out(dve, kbT[:, c, :], bk[c].ap[:, :], toks[c])
                    bk[c].free = [e1]
                    tok["qb" if g == 3 else "kb"].append(e1)

        gemm("in0", {"h": hT}, on_group)
        flush()
        band = widths(lambda i: (max(i - 1, 0), i + 1), NT)
        attend(st.sub(), "ea", 8, band, causal_scores(qaT, kaT, tok["q"], tok["k"], lambda h: h // 4, True),
                   pair_values(lambda h, kt: tk_[:, kt, 128 + 64 * (h // 4):192 + 64 * (h // 4)], hT, 0, band[0], False, None),
                   hT, bias=lambda h, i, W: (evb[:, 256 * (h + 1) - W:256 * (h + 1)], [t_evb]), sink=par("ev_sinks"))
        handover()
        attend(st.sub(), "eb", 8, causal_tiles, causal_scores(qbT, kbT, tok["qb"], tok["kb"], None, False),
                   pair_values(lambda h, kt: vb[:, kt, 64 * h:64 * h + 64], hT, 4, None, True, tok["vb"]),
                   hT, mode="stick")

    def odd_mixer(st):
        handover()
        qs = sb("o_qs", [P, 1], F32, st)
        tmp = [sb(f"o_t{i}", [P, NT, 512], F32, st) for i in range(2)]
        tmp_free = [[], []]
        v = sb("o_v", [P, NT, D], F32, st)
        ss = [sb(f"o_ss{i}", [P, NT, 8], F32, st) for i in range(2)]
        qT = sb("o_qT", [P, 8, S], F32, st)
        kT = sb("o_kT", [P, 8, S], F32, st)
        t_qs = dve.do(lambda e: e.tensor_scalar(qs[:, :], par("od_q_gain"), 0.125, None, ALU.mult), t_cst)
        act.wait(t_qs)
        dve.wait(t_qs)
        tok = {"q": [], "k": [], "v": []}

        def on_group(g, bk, toks):
            if g < 4:
                b = g % 2
                tt = []
                for t in range(NT):
                    e1 = copy_out(act, tmp[b][:, t, :], bk[t].ap[:, :], toks[t], tmp_free[b])
                    bk[t].free = [e1]
                    tt.append(head_norm(tmp[b], t, 8, 64, xn[0][:, 0:512], ss[b], e1, xn_free[0]))
                dst = qT if g < 2 else kT
                gain = qs[:, :] if g < 2 else par("od_k_gain")

                def go():
                    used = []
                    tok["q" if g < 2 else "k"].extend(
                        turn(tmp[b], tt, 4, bk, [dst[:, 4 * (g % 2) + c, :] for c in range(4)], [gain] * 4, NT, used))
                    tmp_free[b] = used
                later.append(go)
            else:
                for t in range(NT):
                    e1 = copy_out(act if t % 2 else dve, v[:, t, 512 * (g - 4):512 * (g - 3)], bk[t].ap[:, :], toks[t])
                    bk[t].free = [e1]
                    tok["v"].append(e1)

        gemm("in1", {"h": hT}, on_group)
        flush()
        handover()
        ob = [tmp[0][:, i, :] for i in range(4)]
        s_ob = [sem(f"s_ob{i}") for i in range(4)]
        t_ob, ob_free = {}, [[]] * 4

        def fetch(h):
            if h < 16:
                t_ob[h] = sp.dma(ob[h % 4], T["odb"][:, 512 * h:512 * (h + 1)], s_ob[h % 4], ob_free[h % 4])

        for h in range(3):
            fetch(h)

        def before(h):
            if h >= 1:
                ob_free[(h - 1) % 4] = [dve.now()]
            fetch(h + 3)

        attend(st.sub(), "oc", 16, causal_tiles, causal_scores(qT, kT, tok["q"], tok["k"], None, False),
                   pair_values(lambda h, kt: v[:, kt, 64 * h:64 * h + 64], hT, 0, None, True, tok["v"]),
                   hT, bias=lambda h, i, W: (ob[h % 4][:, 512 - W:512], [t_ob[h]]), before=before)

    def cross(st, l):
        handover()
        s_m = sem(f"s_mem{l}")
        mx_ = sb(f"c{l}m", [P, 2, D], F32, st)
        M = Act(sb(f"c{l}mh", [P, KD, MEM], F32R, st), sb(f"c{l}ml", [P, KD, MEM], F32R, st), MEM)
        tm = [sb(f"c{l}t{i}", [P, NT, 512], F32, st) for i in range(2)]
        tm_free = [[], []]
        v = sb(f"c{l}v", [P, 2, D], F32, st)
        ss = [sb(f"c{l}ss{i}", [P, NT, 2], F32, st) for i in range(2)]
        kT = sb(f"c{l}kT", [P, 8, MEM], F32, st)
        qT = sb(f"c{l}qT", [P, 8, S], F32, st)
        t_m = sp.dma(mx_[:, :, :], T["mem"][0].rearrange("(t p) d -> p t d", p=P), s_m)
        tok = {"q": [], "k": [], "v": []}
        gains = {n: par(f"xa_{n}_gain{l}") for n in "qk"}

        def heads(which, nt, dst, g, bk, toks):
            b = g % 2
            tt = []
            for t in range(nt):
                e1 = copy_out(act, tm[b][:, t, :], bk[t].ap[:, :], toks[t], tm_free[b])
                bk[t].free = [e1]
                tt.append(head_norm(tm[b], t, 2, 256, xn[0][:, 0:512], ss[b], e1, xn_free[0]))

            def go():
                used = []
                tok[which].extend(turn(tm[b], tt, 4, home, [dst[:, 4 * g + c, :] for c in range(4)],
                                       [gains[which][:, c % 2:c % 2 + 1] for c in range(4)], nt, used))
                tm_free[b] = used
            home = banks[4 * (banks.index(bk[0]) // 4):4 * (banks.index(bk[0]) // 4) + 4]
            later.append(go)

        def on_kv(g, bk, toks):
            if g < 2:
                heads("k", 2, kT, g, bk, toks)
            else:
                for t in range(2):
                    e1 = copy_out(act if t % 2 else dve, v[:, t, 512 * (g - 2):512 * (g - 1)], bk[t].ap[:, :], toks[t])
                    bk[t].free = [e1]
                    tok["v"].append(e1)

        norm(mx_, [[t_m]] * 2, par(f"xa_mem_norm{l}"), M)
        gemm(f"kv{l}", {"m": M}, on_kv)
        flush()
        norm(x, xtok, par(f"xa_norm{l}"), hT)
        gemm(f"xq{l}", {"h": hT}, lambda g, bk, toks: heads("q", 4, qT, g, bk, toks))
        flush()

        def score(h, i, dst, k0, k1):
            for c in range(2):
                t = pe.do(lambda e, c=c: e.matmul(dst, qT[:, 2 * h + c, i * P:(i + 1) * P], kT[:, 2 * h + c, :],
                                                  start=c == 0, stop=c == 1),
                          tok["q"][2 * h + c], tok["k"][2 * h + c], mark=c == 1)
            return t

        def value(h, PTb):
            pe.wait(tok["v"])
            for c in range(2):
                bank = banks[6 + c]
                pe.wait(bank.free)
                for kt in range(2):
                    t = pe.do(lambda e, kt=kt, c=c: e.matmul(
                        banks[6 + c].ap[:, :], v[:, kt, 256 * h + c * P:256 * h + (c + 1) * P], PTb[:, kt, :],
                        start=kt == 0, stop=kt == 1), mark=kt == 1)
                bank.free = [halves(bank.ap[:, :], hT, 2 * h + c, slice(0, S), t)]
            return t

        handover()
        attend(st.sub(), f"cx{l}", 4, widths(lambda i: (0, 2), NT), score, value, hT, scale=1.0 / 16, nk=2)

    def sparse_mixer(st):
        handover()
        a0 = st.at
        vals = sb("s_v", [P, NT, 256], F32, st)
        qT = sb("s_qT", [P, 8, S], F32, st)
        kT = sb("s_kT", [P, 4, S], F32, st)
        spans, total = causal_tiles
        coef = sb("s_coef", [P, 8], F32, st)
        la = sb("s_la", [P, 5, 8], F32, st)
        sel = sb("s_sel", [P, total], F32, st)
        sc = sb("s_sc", [P, total], F32, st)
        iw = sb("s_iw", [P, NT, 8], F32, st)
        m8 = sb("s_m8", [P, 24], F32, st)
        a1 = st.at
        a2 = a1 + 32768
        tmp_area = Area(a1)
        tok = {"q": [], "k": [], "iq": [], "ik": [], "v": []}

        lam = par("rg_lambda")
        t = pool.do(lambda e: e.tensor_scalar(la[:, 1, :], lam, -1.0, None, ALU.mult), t_cst)
        t = dve.do(lambda e: e.tensor_tensor(la[:, 0, :], la[:, 1, :], lam, ALU.max), t)
        t_e = act.do(lambda e: e.activation(la[:, 0, :], la[:, 0, :], AF.Exp, scale=-1.0), t)
        t = pool.do(lambda e: e.tensor_scalar(la[:, 2, :], la[:, 0, :], 2.0, None, ALU.add), t_e)
        t = dve.do(lambda e: e.reciprocal(la[:, 2, :], la[:, 2, :]), t)
        t = pool.do(lambda e: e.tensor_tensor(la[:, 2, :], la[:, 2, :], la[:, 0, :], ALU.mult), t)
        t = pool.do(lambda e: e.tensor_tensor(la[:, 3, :], la[:, 2, :], la[:, 2, :], ALU.mult), t)
        t = pool.do(lambda e: e.memset(la[:, 4, :], 1.0 / 19))
        for n in range(17, 0, -2):
            t = pool.do(lambda e: e.tensor_tensor(la[:, 4, :], la[:, 4, :], la[:, 3, :], ALU.mult), pool.now())
            t = pool.do(lambda e, n=n: e.tensor_scalar(la[:, 4, :], la[:, 4, :], 1.0 / n, None, ALU.add), t)
        t = pool.do(lambda e: e.tensor_tensor(la[:, 4, :], la[:, 4, :], la[:, 2, :], ALU.mult), t)
        t = pool.do(lambda e: e.tensor_scalar(la[:, 4, :], la[:, 4, :], 16.0, None, ALU.mult), t)
        t = pool.do(lambda e: e.tensor_scalar(la[:, 1, :], la[:, 1, :], 0.0, 8.0, ALU.max, ALU.mult), t)
        t = pool.do(lambda e: e.tensor_tensor(coef[:, :], la[:, 4, :], la[:, 1, :], ALU.add), t)
        t_coef = pool.do(lambda e: e.tensor_scalar(la[:, 0, :], coef[:, :], -1.0, None, ALU.mult), t)
        ncoef = la[:, 0, :]

        iqT = sb("s_iqT", [P, 4, S], F32, tmp_area)
        ikT = sb("s_ikT", [P, S], F32, tmp_area)
        tq = sb("s_tq", [P, NT, 512], F32, tmp_area)
        tq2 = sb("s_tq2", [P, NT, 512], F32, tmp_area)
        ti = sb("s_ti", [P, NT, 128], F32, tmp_area)
        rt = [sb(f"s_rt{i}", [P, 4, 64], F32, tmp_area) for i in range(2)]
        lng = sb("s_lng", [P, 2, 64], F32, tmp_area)
        bn = sb("s_bn", [P, NT, 10], F32, tmp_area)
        rl = [sb(f"s_rl{i}", [P, 512], F32, tmp_area) for i in range(3)]
        s_ln = sem("s_ln")
        sp.dma(lng[:, 0, :], T["idx_k_ln_g_2"].partition_broadcast(P), s_ln)
        t_ln = sp.dma(lng[:, 1, :], T["idx_k_ln_b_2"].partition_broadcast(P), s_ln)
        rt_free = [[], []]
        turns = [0]

        def rope(buf, t, nh, tok_):
            b = turns[0] % 2
            turns[0] += 1
            v3 = buf.rearrange("p (h d) -> p h d", d=64)
            x1, x2 = v3[:, :, 0:8], v3[:, :, 8:16]
            cs = mis("cos")[:, 8 * t:8 * t + 8].unsqueeze(1).to_broadcast([P, nh, 8])
            sn = mis("sin")[:, 8 * t:8 * t + 8].unsqueeze(1).to_broadcast([P, nh, 8])
            r = [rt[b][:, i, 0:8 * nh].rearrange("p (h d) -> p h d", d=8) for i in range(4)]
            pr = [pool.do(lambda e, o=o, a=a, c=c: e.tensor_tensor(o, a, c, ALU.mult), tok_, t_cst)
                  for o, a, c in ((r[0], x1, cs), (r[1], x2, sn), (r[2], x2, cs), (r[3], x1, sn))]
            pool.do(lambda e: e.tensor_tensor(x1, r[0], r[1], ALU.subtract), pr)
            return pool.do(lambda e: e.tensor_tensor(x2, r[2], r[3], ALU.add), pr)

        tq_free = []

        def on_idx(g, bk, toks):
            if g == 0:
                tt = []
                for t in range(NT):
                    e1 = copy_out(act, tq[:, t, :], bk[t].ap[:, :], toks[t])
                    bk[t].free = [e1]
                    tt.append(rope(tq[:, t, :], t, 8, e1))

                def go():
                    tok["iq"] = turn(tq, tt, 4, bk, [iqT[:, c, :] for c in range(4)], None, NT, tq_free)
                later.append(go)
                return
            tt = []
            for t in range(NT):
                e1 = copy_out(act, ti[:, t, 0:72], bk[t].ap[:, 0:72], toks[t])
                bk[t].free = [e1]
                k = ti[:, t, 0:64]
                w1 = pool.do(lambda e, t=t: e.tensor_scalar(iw[:, t, :], ti[:, t, 64:72], (8 ** -0.5) * (64 ** -0.5),
                                                            None, ALU.mult), e1)
                t1 = dve.do(lambda e, t=t, k=k: e.bn_stats(bn[:, t, 0:6], k), e1)
                t2 = dve.do(lambda e, t=t: e.bn_aggr(bn[:, t, 6:8], bn[:, t, 0:6]), t1)
                t3 = rstd(bn[:, t, 7:8], bn[:, t, 8:9], 1.0, t2)
                t4 = dve.do(lambda e, t=t, k=k: e.tensor_scalar(k, k, bn[:, t, 6:7], bn[:, t, 8:9], ALU.subtract,
                                                                ALU.mult), t3, t2)
                t5 = dve.do(lambda e, k=k: e.tensor_tensor(k, k, lng[:, 0, :], ALU.mult), t4, t_ln)
                t6 = dve.do(lambda e, k=k: e.tensor_tensor(k, k, lng[:, 1, :], ALU.add), t5)
                t7 = rope(k, t, 1, [t6, w1])
                tt.append(copy_out(pool, ti[:, t, 64:128], k, t7))

            def go():
                tok["ik"] = turn(ti, tt, 1, bk, [ikT[:, :]], None, NT, [])
            later.append(go)

        def on_qkv(g, bk, toks):
            tt = []
            buf = [tq2, tq, tq2][g]
            fr = [[], tq_free, tq_free2][g]
            for t in range(NT):
                e1 = copy_out(act, buf[:, t, :], bk[t].ap[:, :], toks[t], fr)
                bk[t].free = [e1]
                if g < 2:
                    tt.append(rope(buf[:, t, :], t, 8, e1))
                else:
                    r1 = rope(buf[:, t, 0:256], t, 4, e1)
                    tok["v"].append(copy_out(pool, vals[:, t, :], buf[:, t, 256:512], e1))
                    kv = tq[:, t, :].rearrange("p (h u d) -> p h u d", h=4, u=2)
                    k3 = buf[:, t, 0:256].rearrange("p (h d) -> p h d", h=4)
                    c1 = pool.do(lambda e, kv=kv, k3=k3: e.tensor_copy(kv[:, :, 0, :], k3), r1, tq_free3)
                    tt.append(pool.do(lambda e, kv=kv, k3=k3: e.tensor_copy(kv[:, :, 1, :], k3), c1))

            def go():
                if g < 2:
                    tok["q"].extend(turn(buf, tt, 4, bk, [qT[:, 4 * g + c, :] for c in range(4)], [0.125] * 4, NT,
                                         tq_free2 if g == 0 else tq_free3))
                else:
                    tok["k"] = turn(tq, tt, 4, bk, [kT[:, c, :] for c in range(4)], None, NT, [])
            later.append(go)
        tq_free2, tq_free3 = [], []

        norm(x, xtok, par("norm_mix_pre"), hT)
        gemm("idx", {"h": hT}, on_idx)
        gemm("qkv", {"h": hT}, on_qkv)
        flush()

        sctok = {}
        rl_free = [[], [], []]
        n = 0
        for h in range(8):
            r = slice(64 * (h % 2), 64 * (h % 2) + 64)
            for i in range(1, NT):
                _, _, o, W = spans[i]
                bank = banks[n % 4]
                rb = rl[n % 3]
                tk = pe.do(lambda e, r=r, h=h, i=i, W=W, bank=bank: e.matmul(
                    bank.ap[:, 0:W], iqT[r, h // 2, i * P:(i + 1) * P], ikT[r, 0:W], start=True, stop=True),
                    bank.free, tok["iq"][h // 2], tok["ik"])
                t1 = act.do(lambda e, rb=rb, W=W, bank=bank: e.activation(rb[:, 0:W], bank.ap[:, 0:W], AF.Relu), tk,
                            rl_free[n % 3])
                bank.free = [t1]
                s_, w_ = sc[:, o:o + W], iw[:, i, h:h + 1]
                if h == 0:
                    t2 = dve.do(lambda e, s_=s_, w_=w_, rb=rb, W=W: e.tensor_scalar(s_, rb[:, 0:W], w_, None, ALU.mult),
                                t1, pool.now())
                else:
                    t2 = dve.do(lambda e, s_=s_, w_=w_, rb=rb, W=W: e.scalar_tensor_tensor(
                        s_, rb[:, 0:W], w_, s_, ALU.mult, ALU.add), t1, sctok[i])
                sctok[i] = t2
                rl_free[n % 3] = [t2]
                n += 1
        handover()

        best = {0: dve.do(lambda e: e.tensor_copy(sel[:, 0:P], mis("causal")), t_cst)}

        def select(i):
            _, _, o, W = spans[i]
            s_, w_, m_ = sc[:, o:o + W], sel[:, o:o + W], m8[:, 8 * (i - 1):8 * i]
            dg = sc[:, o + W - P:o + W]

            def start():
                t = pool.do(lambda e: e.affine_select(out=dg, in_=dg, compare_op=ALU.is_ge, fill=FLOOR, base=0,
                                                      pattern=[[-1, P]], channel_multiplier=1), sctok[i])
                best[i] = dve.do(lambda e: e.tensor_copy(w_, s_), t)

            def round_():
                t = dve.do(lambda e: e.max(m_, w_), best[i])
                best[i] = dve.do(lambda e: e.match_replace(w_, m_, w_, TAKEN), t)

            def end():
                t = dve.do(lambda e: e.tensor_tensor(w_, w_, s_, ALU.is_equal), best[i])
                best[i] = dve.do(lambda e: e.tensor_scalar(w_, w_, NEG, None, ALU.mult), t)
            return [start] + [round_] * 16 + [end]

        three = [select(i) for i in range(1, NT)]
        for r in range(18):
            for s_ in three:
                background.append(s_[r])

        y_area = Area(a1)
        Y = Act(sb("s_Yh", [P, KD, S], F32R, y_area), sb("s_Yl", [P, KD, S], F32R, y_area), S)
        rn = Area(a2)
        wa = sb("s_wa", [P, 8, 64], F32, rn)
        wx = sb("s_wx", [P, 8, 64], F32, rn)
        s_g = sem("s_g")
        sp.dma(wa[:, :, :], T["wa_l"], s_g)
        t_g = sp.dma(wx[:, :, :], T["wx_l"], s_g)
        xp = sb("s_xp", [P, 2, S + 3], F32, rn)
        xc = sb("s_xc", [P, 2, S], F32, rn)
        gr = sb("s_gr", [P, 2, S], F32, rn)
        ra = sb("s_ra", [P, 2, S], F32, rn)
        ri = sb("s_ri", [P, 2, S], F32, rn)
        th = sb("s_th", [P, 2, S], F32, rn)
        t_pad = pool.do(lambda e: e.memset(xp[:, :, :], 0.0))
        fr = {"xp": [t_pad], "gr": [], "rest": []}

        def on_rnn(g, bk, toks):
            tc, tg = [], []
            for j in range(2):
                c = 2 * g + j
                e1 = copy_out(act, xp[:, j, 3:S + 3], bk[j].ap[:, :], toks[j], fr["xp"])
                bk[j].free = [e1]
                cw = lambda k, c=c: prm[:, PRM["conv_w"][0] + 8 * k + c:PRM["conv_w"][0] + 8 * k + c + 1]
                t1 = act.do(lambda e, j=j, c=c, cw=cw: e.activation(xc[:, j, :], xp[:, j, 0:S], AF.Identity,
                                                                    bias=par("conv_b")[:, c:c + 1], scale=cw(0)),
                            e1, fr["rest"])
                for k in range(1, 4):
                    t1 = dve.do(lambda e, j=j, k=k, cw=cw: e.scalar_tensor_tensor(
                        xc[:, j, :], xp[:, j, k:k + S], cw(k), xc[:, j, :], ALU.mult, ALU.add), t1)
                tc.append(t1)
            for j in range(2):
                e1 = act.do(lambda e, j=j: e.activation(gr[:, j, :], bk[2 + j].ap[:, :], AF.Gelu_apprx_tanh),
                            toks[2 + j], fr["gr"])
                bk[2 + j].free = [e1]
                tg.append(e1)
            fr["xp"] = list(tc)

            def go():
                ts, tz, tu = [], [], []
                for j in range(2):
                    c = 2 * g + j
                    for m, (w_, bias_, dst) in enumerate(((wa, "rg_b_a", ra), (wx, "rg_b_x", ri))):
                        bank = bk[2 * j + m]
                        pe.wait(bank.free)
                        for u in range(2):
                            r = slice(64 * u, 64 * u + 64)
                            tk = pe.do(lambda e, r=r, w_=w_, c=c, j=j, bank=bank: e.matmul(
                                bank.ap[r, :], w_[r, c, :], xc[r, j, :], start=True, stop=True), t_g, tc[j],
                                mark=u == 1)
                        t1 = act.do(lambda e, bank=bank, dst=dst, j=j, c=c, bias_=bias_: e.activation(
                            dst[:, j, :], bank.ap[:, :], AF.Sigmoid, bias=par(bias_)[:, c:c + 1]), tk, fr["rest"])
                        bank.free = [t1]
                        ts.append(t1)
                for j in range(2):
                    c = 2 * g + j
                    tz.append(act.do(lambda e, j=j, c=c: e.activation(th[:, j, :], ra[:, j, :], AF.Tanh,
                                                                      scale=coef[:, c:c + 1]), ts, t_coef, fr["rest"]))
                    ta_ = act.do(lambda e, j=j, c=c: e.activation(ra[:, j, :], ra[:, j, :], AF.Exp,
                                                                  scale=ncoef[:, c:c + 1]), ts, tz)
                    t1 = dve.do(lambda e, j=j: e.tensor_tensor(xc[:, j, :], xc[:, j, :], ri[:, j, :], ALU.mult), ts,
                                pe.now())
                    t2 = dve.do(lambda e, j=j: e.tensor_scalar(ri[:, j, :], th[:, j, :], 1.0, None, ALU.add), tz[j], t1)
                    t3 = dve.do(lambda e, j=j: e.reciprocal(ri[:, j, :], ri[:, j, :]), t2)
                    tu.append((dve.do(lambda e, j=j: e.tensor_tensor(th[:, j, :], th[:, j, :], ri[:, j, :], ALU.mult),
                                      t3), ta_))
                for j in range(2):
                    c = 2 * g + j
                    t1 = act.do(lambda e, j=j: e.activation(th[:, j, :], th[:, j, :], AF.Sqrt, scale=2.0), tu[j][0])
                    t2 = dve.do(lambda e, j=j: e.tensor_tensor(th[:, j, :], th[:, j, :], xc[:, j, :], ALU.mult), t1)
                    t3 = dve.do(lambda e, j=j: e.tensor_tensor_scan(ri[:, j, :], ra[:, j, :], th[:, j, :], 0.0, ALU.mult,
                                                                    ALU.add), t2, tu[j][1])
                    t4 = dve.do(lambda e, j=j: e.tensor_tensor(gr[:, j, :], gr[:, j, :], ri[:, j, :], ALU.mult), t3,
                                tg[j])
                    t5 = halves(gr[:, j, :], Y, c, slice(0, S), t4)
                fr["gr"] = [t5]
                fr["rest"] = [t5]
            later.append(go)

        gemm("rnn", {"h": hT}, on_rnn, 4)
        flush()
        handover()
        Mg = sb("s_mg", [P, 8, S], F32, Area(a2))
        GB = sb("s_gb", [P, 8, S], F32, Area(a1))
        gt = [xn[i][:, 0:S] for i in range(2)]
        gt_free = [xn_free[0], xn_free[1]]
        mtok = {}

        def on_ya(g, bk, toks):
            for j in range(2):
                c = 2 * g + j
                t1 = act.do(lambda e, j=j: e.activation(gt[j], bk[j].ap[:, :], AF.Sigmoid), toks[j], gt_free[j])
                bk[j].free = [t1]
                t2 = dve.do(lambda e, j=j, c=c: e.tensor_tensor(Mg[:, c, :], gt[j], bk[2 + j].ap[:, :], ALU.mult),
                            t1, toks[2 + j])
                bk[2 + j].free = [t2]
                gt_free[j] = [t2]
                xn_free[j] = [t2]
                mtok[c] = t2

        gtok = {}

        def on_gb(g, bk, toks):
            for c in range(4):
                t1 = act.do(lambda e, c=c: e.activation(GB[:, 4 * g + c, :], bk[c].ap[:, :], AF.Sigmoid), toks[c])
                bk[c].free = [t1]
                gtok[4 * g + c] = t1

        gemm("ya", {"h": hT, "y": Y}, on_ya, 2)
        gemm("gb", {"h": hT}, on_gb, 2)
        while background:
            background.pop(0)()
        handover()
        attend(Area(a2 + 16384), "sx", 16, causal_tiles, causal_scores(qT, kT, tok["q"], tok["k"], lambda h: h // 4, True),
                   pair_values(lambda h, kt: vals[:, kt, 64 * (h // 4):64 * (h // 4) + 64], hT, 0, None, True, tok["v"]),
                   hT, bias=lambda h, i, W: (sel[:, spans[i][2]:spans[i][2] + W], [best[i]]), st2=Area(a1 + 16384))
        handover()
        Z = Act(sb("s_Zh", [P, KD, S], F32R, Area(a1 + 16384)), sb("s_Zl", [P, KD, S], F32R, Area(a0 + 4096)), S)

        def on_yb(g, bk, toks):
            for c in range(4):
                k = 4 * g + c
                t1 = dve.do(lambda e, c=c, k=k: e.tensor_tensor(GB[:, k, :], GB[:, k, :], bk[c].ap[:, :], ALU.mult),
                            toks[c], gtok[k])
                bk[c].free = [t1]
                t2 = dve.do(lambda e, k=k: e.tensor_tensor(GB[:, k, :], GB[:, k, :], Mg[:, k, :], ALU.add), t1, mtok[k])
                halves(GB[:, k, :], Z, k, slice(0, S), t2)

        gemm("yb", {"h": hT}, on_yb)
        post_norm(Area(a2 + 16384), "wo", {"y": Z}, "s_", T["norm_mix_post_2"])

    def post_norm(area, name, acts, tag, gain):
        gb = sb(tag + "pg", [P, D], F32, area)
        s_p = sem(tag + "s_pg")
        t_p = sp.dma(gb[:, :], gain.partition_broadcast(P), s_p)
        held = []
        gemm(name, acts, lambda g, bk, toks: held.append((bk, toks)))
        def tile(t):
            b = t % 2
            two = [(held[g][0][t], held[g][1][t], slice(512 * g, 512 * g + 512)) for g in range(2)]
            t1 = [act.do(lambda e, k=k, c=c, g=g: e.activation(xn[b][:, c], k.ap[:, :], AF.Square,
                                                              accum_out=stat[:, 4 * g + t:4 * g + t + 1]),
                         tk, xn_free[b], stat_free) for g, (k, tk, c) in enumerate(two)]
            r = stat[:, 8 + t:9 + t]
            t2 = pool.do(lambda e: e.tensor_tensor(r, stat[:, t:t + 1], stat[:, 4 + t:5 + t], ALU.add), t1, stat_free)
            t2 = rstd(r, r, 1.0 / D, t2)
            t3 = [dve.do(lambda e, k=k, c=c: e.scalar_tensor_tensor(xn[b][:, c], k.ap[:, :], r, gb[:, c], ALU.mult,
                                                                    ALU.mult), t1, t2, t_p) for k, _, c in two]
            for k, _, _ in two:
                k.free = [t3[1]]
            t4 = dve.do(lambda e: e.tensor_tensor(x[:, t, :], x[:, t, :], xn[b][:, :], ALU.add), t3, xtok[t])
            xtok[t] = [t4]
            xn_free[b] = [t4]
            return t4

        for t in range(NT):
            t4 = tile(t)
        stat_free[:] = [t4]

    def ffn(up, down, tag, after):
        area = Area(base)
        handover()
        F = Act(sb(tag + "Fh", [P, KF, S], F32R, area), sb(tag + "Fl", [P, KF, S], F32R, area), S)
        sg = [sb(f"{tag}sg{i}", [P, S], F32, area) for i in range(2)]
        pr = [sb(f"{tag}pr{i}", [P, S], F32, area) for i in range(2)]
        sg_free, pr_free = [[], []], [[], []]

        def on_group(g, bk, toks):
            for j in range(2):
                t1 = act.do(lambda e, j=j: e.activation(sg[j][:, :], bk[j].ap[:, :], AF.Silu), toks[j], sg_free[j])
                bk[j].free = [t1]
                t2 = dve.do(lambda e, j=j: e.tensor_tensor(pr[j][:, :], sg[j][:, :], bk[2 + j].ap[:, :], ALU.mult),
                            t1, toks[2 + j], pr_free[j])
                bk[2 + j].free = [t2]
                sg_free[j] = [t2]
                pr_free[j] = [halves(pr[j][:, :], F, 2 * g + j, slice(0, S), t2)]

        gemm(up, {"h": hT}, on_group)
        after(area, down, {"f": F})

    def half_added(area, name, acts):
        gemm(name, acts, add_to_x(0.5))

    def whole():
        for l in range(2):
            norm(x, xtok, par(f"ffn1_norm{l}"), hT)
            ffn(f"f1u{l}", f"f1d{l}", f"f1{l}", half_added)
            if stop == f"f1{l}":
                return
            norm(x, xtok, par(f"mix_norm{l}"), hT)
            (even_mixer if l == 0 else odd_mixer)(Area(base))
            gemm(f"out{l}", {"h": hT}, add_to_x(1.0))
            if stop == f"mix{l}":
                return
            cross(Area(base), l)
            gemm(f"xo{l}", {"h": hT}, add_to_x(1.0))
            if stop == f"xa{l}":
                return
            norm(x, xtok, par(f"ffn2_norm{l}"), hT)
            ffn(f"f2u{l}", f"f2d{l}", f"f2{l}", half_added)
            if stop == f"f2{l}":
                return
        sparse_mixer(Area(base))
        if stop == "sp":
            return
        norm(x, xtok, par("norm_ffn_pre"), hT)
        ffn("f3u", "f3d", "f3", lambda area, name, acts: post_norm(area, name, acts, "f3", T["norm_ffn_post_2"]))

    whole()
    for t in range(NT):
        sp.dma(out[0, t * P:(t + 1) * P, :], x[:, t, :], s_st, xtok[t])
    sp.wait((s_st, s_st.count))

    with nc.Block() as block:
        block.sync(lambda e: sp.play(e))
        block.tensor(lambda e: pe.play(e))
        block.scalar(lambda e: act.play(e))
        block.vector(lambda e: dve.play(e))
        block.gpsimd(lambda e: pool.play(e))
    ctx.close()


def shape_tables():
    p = np.arange(P)[:, None]
    misc = np.zeros((P, NMISC), np.float32)
    f = np.arange(P)[None, :]
    misc[:, 0:128] = p == f
    misc[:, 128:256] = np.where(f < p, 0.0, NEG)
    misc[:, 256:384] = np.where(f <= p, 0.0, NEG)
    inv = (np.float32(500000.0) ** (-np.arange(8, dtype=np.float32) / np.float32(8))).astype(np.float32)
    ang = (np.arange(S, dtype=np.float32)[:, None] * inv[None, :]).astype(np.float32)
    for name, fn in (("cos", np.cos), ("sin", np.sin)):
        o = MISC[name][0]
        misc[:, o:o + 32] = fn(ang.astype(np.float64)).reshape(NT, P, 8).transpose(1, 0, 2).reshape(P, 32)
    d = p + 128 - np.arange(256)[None, :]
    evb = [np.where((d >= 0) & (d <= 127), -(2.0 ** -(h + 1)) * d, NEG) for h in range(8)]
    d = p + 384 - np.arange(512)[None, :]
    c = ((d >= 0) & (d <= 128)).astype(int) + ((d >= 0) & (d % 4 == 0)) + ((d >= 0) & (d % 16 == 0))
    odb = [np.where(c > 0, -np.float64(np.float32(2.0 ** (-8.0 * (h + 1) / 16))) * d
                    + np.log(np.maximum(c, 1)), NEG) for h in range(16)]
    return misc, np.concatenate(evb, 1).astype(np.float32), np.concatenate(odb, 1).astype(np.float32)


_DIRECT = ["x", "mem", "ffn1_w_gu", "ffn1_w_down", "ev_w_in", "ev_w_out", "od_w_in", "od_w_out", "xa_w_q", "xa_w_kv",
           "xa_w_o", "ffn2_w_gu", "ffn2_w_down", "w_in_2", "idx_k_ln_g_2", "idx_k_ln_b_2", "w_rnn_out_2",
           "w_att_out_2", "w_o_2", "norm_mix_post_2", "w_ffn_gate_2", "w_ffn_up_2", "w_ffn_down_2", "norm_ffn_post_2"]


def lay_out(inputs):
    a = {n: np.ascontiguousarray(inputs[n]) for n in _DIRECT}
    for n in ("idx_k_ln_g_2", "idx_k_ln_b_2", "norm_mix_post_2", "norm_ffn_post_2"):
        a[n] = a[n].reshape(-1)
    g = {n: np.asarray(v) for n, v in inputs.items() if n not in _DIRECT}

    def col(v):
        return v.reshape(-1, P).T

    def twice(v):
        return np.concatenate([v, v]).reshape(P, 1)

    parts = []
    for l in range(2):
        parts += [col(g[n][l]) for n in ("ffn1_norm", "mix_norm", "xa_norm", "xa_mem_norm", "ffn2_norm", "xa_q_gain",
                                         "xa_k_gain")]
    parts += [twice(g[n][0]) for n in ("ev_q_gain", "ev_k_gain", "od_q_gain", "od_k_gain")]
    parts.append(np.broadcast_to(g["ev_sinks"][0][None, :], (P, 8)))
    parts += [col(g[n + "_2"][0]) for n in ("norm_mix_pre", "norm_ffn_pre", "conv_b", "rg_b_a", "rg_b_x", "rg_lambda")]
    parts += [col(g["conv_w_2"][0][k]) for k in range(4)]
    a["prm"] = np.ascontiguousarray(np.concatenate(parts, axis=1))
    for n, s in (("wa_l", "rg_w_a_2"), ("wx_l", "rg_w_x_2")):
        a[n] = np.ascontiguousarray(g[s][0].reshape(8, 2, 64, 64).transpose(1, 2, 0, 3).reshape(P, 8, 64))
    a["misc"], a["evb"], a["odb"] = shape_tables()
    return a


def kernel(**inputs):
    import concourse.bacc as _bacc
    from concourse.bass_utils import run_bass_kernel_spmd as _run

    nc = _bacc.Bacc("TRN2", target_bir_lowering=False, num_devices=1)
    arrays, T = {}, {}
    for name, a in lay_out(inputs).items():
        arrays[f"in_{name}"] = a
        T[name] = nc.dram_tensor(f"in_{name}", a.shape, mybir.dt.from_np(a.dtype), kind="ExternalInput").ap()
    out = nc.dram_tensor("out_x", (1, S, D), F32, kind="ExternalOutput").ap()
    program(nc, T, out)
    r = _run(nc, [arrays], core_ids=[0])
    return r.results[0]["out_x"]
```

```python
from contextlib import ExitStack

import numpy as np

import concourse.bass as bass
from concourse import mybir

F32 = mybir.dt.float32
F32R = mybir.dt.float32r
ALU = mybir.AluOpType
AF = mybir.ActivationFunctionType
AX = mybir.AxisListType.X

P = 128
S = 512
NT = S // P
D = 1024
KD = D // P
FF = 2816
KF = FF // P
MEM = 256
EPS = 1e-6
NEG = -1.0e30
FLOOR = -3.0e38
TAKEN = -3.3e38
NRAW = 4
NW = 4
AHEAD = 3


class Sem:

    def __init__(self, handle):
        self.handle = handle
        self.count = 0


class Queue:

    def __init__(self, sem):
        self.sem = sem
        self.items = []
        self.met = {}

    def wait(self, *tokens):
        for t in tokens:
            if t is None:
                continue
            if isinstance(t, list):
                self.wait(*t)
                continue
            sem, value = t
            if self.met.get(sem, 0) < value:
                self.met[sem] = value
                self.items.append(lambda e, h=sem.handle, v=value: e.wait_ge(h, v))

    def do(self, fn, *tokens, mark=True):
        self.wait(*tokens)
        if not mark:
            self.items.append(fn)
            return None
        self.sem.count += 1
        self.items.append(lambda e, h=self.sem.handle: fn(e).then_inc(h, 1))
        return (self.sem, self.sem.count)

    def dma(self, out, in_, sem, *tokens):
        self.wait(*tokens)
        sem.count += 16
        self.items.append(lambda e, h=sem.handle: e.dma_start(out, in_).then_inc(h, 16))
        return (sem, sem.count)

    def now(self):
        return (self.sem, self.sem.count) if self.sem.count else None

    def play(self, engine):
        for item in self.items:
            item(engine)


class Bank:
    def __init__(self, ap):
        self.ap = ap
        self.free = []


class Area:

    def __init__(self, at):
        self.at = at

    def take(self, nc, name, shape, dt):
        n = 4 * int(np.prod(shape[1:]))
        t = nc.alloc_sbuf_tensor_at(name, shape, dt, offset=self.at)
        self.at += -(-n // 32) * 32
        return t

    def sub(self, skip=0):
        return Area(self.at + skip)


class Act:

    def __init__(self, hi, lo, n):
        self.hi, self.lo, self.n = hi, lo, n
        self.tok = {}
        self.free = []


def params_layout():
    names = []
    for l in range(2):
        names += [(f"ffn1_norm{l}", 8), (f"mix_norm{l}", 8), (f"xa_norm{l}", 8), (f"xa_mem_norm{l}", 8),
                  (f"ffn2_norm{l}", 8), (f"xa_q_gain{l}", 2), (f"xa_k_gain{l}", 2)]
    names += [("ev_q_gain", 1), ("ev_k_gain", 1), ("od_q_gain", 1), ("od_k_gain", 1), ("ev_sinks", 8),
              ("norm_mix_pre", 8), ("norm_ffn_pre", 8), ("conv_b", 8), ("rg_b_a", 8), ("rg_b_x", 8),
              ("rg_lambda", 8), ("conv_w", 32)]
    at, off = {}, 0
    for n, w in names:
        at[n] = (off, w)
        off += w
    return at, off


PRM, NPRM = params_layout()
MISC = {"ident": (0, 128), "strict": (128, 128), "causal": (256, 128), "cos": (384, 32), "sin": (416, 32)}
NMISC = 448


def program(nc, T, out, stop=None):
    ctx = ExitStack()

    def sb(name, shape, dt=F32, area=None):
        if area is None:
            return ctx.enter_context(nc.sbuf_tensor(name, shape, dt))
        return area.take(nc, name, shape, dt)

    def sem(name):
        return Sem(ctx.enter_context(nc.semaphore(name)))

    pe, act, dve, pool, sp = (Queue(sem("s_" + n)) for n in ("pe", "act", "dve", "pool", "sp"))
    s_st = sem("s_st")
    s_cst = sem("s_cst")
    banks = [Bank(ctx.enter_context(nc.psum_tensor(f"ps{i}", [P, 512], F32))) for i in range(8)]

    x = sb("x", [P, NT, D])
    hTh = sb("hTh", [P, KD, S], F32R)
    hTl = sb("hTl", [P, KD, S], F32R)
    hT = Act(hTh, hTl, S)
    raw = [sb(f"raw{i}", [P, 2, 512]) for i in range(NRAW)]
    wh = [sb(f"wh{i}", [P, 2, 512], F32R) for i in range(NW)]
    wl = [sb(f"wl{i}", [P, 2, 512], F32R) for i in range(NW)]
    s_raw = [sem(f"s_raw{i}") for i in range(NRAW)]
    xn = [sb(f"xn{i}", [P, D]) for i in range(2)]
    xn_free = [[], []]
    prm = sb("prm", [P, NPRM])
    misc = sb("misc", [P, NMISC])
    half = sb("half", [P, 64])
    stat = sb("stat", [P, 16])
    ident = misc[:, 0:128]
    base = -(-nc.sbuf_base // 64) * 64

    def par(name):
        o, w = PRM[name]
        return prm[:, o:o + w]

    def mis(name):
        o, w = MISC[name]
        return misc[:, o:o + w]

    t_cst = [sp.dma(prm[:, :], T["prm"], s_cst), sp.dma(misc[:, :], T["misc"], s_cst)][-1]
    s_x = [sem(f"s_x{t}") for t in range(NT)]
    xtok = [[sp.dma(x[:, t, :], T["x"][0, t * P:(t + 1) * P, :], s_x[t])] for t in range(NT)]
    t_half = pool.do(lambda e: e.memset(half[:, :], -0.5))

    def gate_up(name, wg, wu, a="h"):
        return (name, KD, [[(wg, c, 256, a, "A"), (wu, c, 256, a, "A")] for c in range(0, FF, 256)])

    def rows(name, w, K, widths, a="h", form="B", c0=0):
        groups = []
        for n in widths:
            groups.append([(w, c0, n, a, form)])
            c0 += n
        return (name, K, groups)

    GEMMS = []
    for l in range(2):
        wgu, wd = T["ffn1_w_gu"][l], T["ffn1_w_down"][l]
        GEMMS.append(gate_up(f"f1u{l}", wgu[:, 0:FF], wgu[:, FF:2 * FF]))
        GEMMS.append(rows(f"f1d{l}", wd, KF, [512, 512], "f"))
        if l == 0:
            w = T["ev_w_in"][0]
            GEMMS.append((f"in{l}", KD, [[(w, 0, 512, "h", "B")], [(w, 512, 256, "h", "B")], [(w, 1792, 512, "h", "B")],
                                         [(w, 768, 512, "h", "A")], [(w, 1280, 512, "h", "A")]]))
            GEMMS.append(rows(f"out{l}", T["ev_w_out"][0], KD, [512, 512]))
        else:
            w = T["od_w_in"][0]
            GEMMS.append(rows(f"in{l}", w, KD, [512] * 6))
            GEMMS.append(rows(f"out{l}", T["od_w_out"][0], KD, [512, 512]))
        GEMMS.append(rows(f"kv{l}", T["xa_w_kv"][l], KD, [512] * 4, "m"))
        GEMMS.append(rows(f"xq{l}", T["xa_w_q"][l], KD, [512] * 2))
        GEMMS.append(rows(f"xo{l}", T["xa_w_o"][l], KD, [512] * 2))
        wgu, wd = T["ffn2_w_gu"][l], T["ffn2_w_down"][l]
        GEMMS.append(gate_up(f"f2u{l}", wgu[:, 0:FF], wgu[:, FF:2 * FF]))
        GEMMS.append(rows(f"f2d{l}", wd, KF, [512, 512], "f"))
    w = T["w_in_2"][0]
    GEMMS.append(("idx", KD, [[(w, 3584, 512, "h", "B")], [(w, 4096, 72, "h", "B")]]))
    GEMMS.append(rows("qkv", w, KD, [512] * 3, c0=2048))
    GEMMS.append(("rnn", KD, [[(w, c, 256, "h", "A"), (w, 1024 + c, 256, "h", "A")] for c in range(0, 1024, 256)]))
    GEMMS.append(("ya", KD, [[seg] for c in range(0, 1024, 512)
                             for seg in ((w, 4168 + c, 512, "h", "A"), (T["w_rnn_out_2"][0], c, 512, "y", "A"))]))
    GEMMS.append(rows("gb", w, KD, [512] * 2, form="A", c0=5192))
    GEMMS.append(rows("yb", T["w_att_out_2"][0], KD, [512] * 2, form="A"))
    GEMMS.append(rows("wo", T["w_o_2"][0], KD, [512] * 2, "y"))
    GEMMS.append(gate_up("f3u", T["w_ffn_gate_2"][0], T["w_ffn_up_2"][0]))
    GEMMS.append(rows("f3d", T["w_ffn_down_2"][0], KF, [512, 512], "f"))

    stream = [(segs, kp) for _, K, groups in GEMMS for segs in groups for kp in range(K // 2)]
    first = {}
    n = 0
    for name, K, groups in GEMMS:
        first[name] = n
        n += len(groups) * K // 2
    spec = {g[0]: g for g in GEMMS}
    t_raw, t_hi, t_lo, t_used = {}, {}, {}, {}
    done = {"load": 0, "split": 0}

    def load(n):
        if n >= len(stream):
            return
        segs, kp = stream[n]
        r = n % NRAW
        old = n - NRAW
        o = 0
        for w, c, width, _, _ in segs:
            t_raw[n] = sp.dma(raw[r][:, :, o:o + width],
                              w[kp * 256:(kp + 1) * 256, c:c + width].rearrange("(c p) n -> p c n", p=P),
                              s_raw[r], t_hi.get(old), t_lo.get(old))
            o += width

    def split(n):
        if n >= len(stream):
            return
        W = sum(s[2] for s in stream[n][0])
        r, i = n % NRAW, n % NW
        src, hi, lo = raw[r][:, :, 0:W], wh[i][:, :, 0:W], wl[i][:, :, 0:W]
        t_hi[n] = act.do(lambda e: e.activation(hi, src, AF.Copy), t_raw[n], t_used.get(n - NW))
        t_lo[n] = dve.do(lambda e: e.tensor_tensor(lo, src, hi.bitcast(F32), ALU.subtract),
                         t_raw[n], t_hi[n], t_used.get(n - NW))

    def advance(n):
        while done["split"] <= n + AHEAD:
            while done["load"] < done["split"] + NRAW:
                load(done["load"])
                done["load"] += 1
            split(done["split"])
            done["split"] += 1

    later = []
    background = []
    urgent = []
    side = [0]

    def flush():
        while later:
            later.pop(0)()

    def take_half():
        side[0] ^= 1
        return banks[4 * side[0]:4 * side[0] + 4]

    def gemm(name, acts, on_group, background_per_chunk=0):
        _, K, groups = spec[name]
        n = first[name]
        for g, segs in enumerate(groups):
            bk = take_half()
            jobs, o, b = [], 0, 0
            for _, _, width, a, form in segs:
                A = acts[a]
                if form == "A":
                    for j in range(width // P):
                        jobs.append((bk[b], A, "A", slice(o + j * P, o + (j + 1) * P), slice(0, A.n)))
                        b += 1
                else:
                    for t in range(A.n // P):
                        jobs.append((bk[b], A, "B", slice(o, o + width), slice(t * P, (t + 1) * P)))
                        b += 1
                o += width
            toks = []
            blocks = [[kp] for kp in range(K // 2)]
            if g == len(groups) - 1:
                blocks[-2:] = [[K // 2 - 2, K // 2 - 1]]
            for block in blocks:
                advance(n)
                for u in range(len(block)):
                    pe.wait(t_hi[n + u], t_lo[n + u])
                ks = [(2 * kp + kk, n + kp - block[0], kk) for kp in block for kk in range(2)]
                order = [(k, job) for k in ks for job in jobs] if len(block) == 1 else \
                        [(k, job) for job in jobs for k in ks]
                for (k, m, kk), (bank, A, form, wc, tc) in order:
                    i = m % NW
                    pe.wait(A.tok[k])
                    if k == 0:
                        pe.wait(bank.free)
                    Wh, Wl = wh[i][:, kk, wc], wl[i][:, kk, wc]
                    Ah, Al = A.hi[:, k, tc], A.lo[:, k, tc]
                    for q, (p0, p1) in enumerate(((Wh, Ah), (Wh, Al), (Wl, Ah)) if form == "A" else
                                                 ((Ah, Wh), (Ah, Wl), (Al, Wh))):
                        M = (wc.stop - wc.start) if form == "B" else A.n
                        end = k == K - 1 and q == 2
                        t = pe.do(lambda e, o_=bank.ap[:, 0:M], l_=p0, r_=p1, s_=(k == 0 and q == 0), e_=end:
                                  e.matmul(o_, l_, r_, start=s_, stop=e_),
                                  mark=end or (q == 2 and kk == 1 and bank is jobs[-1][0]))
                        if end:
                            toks.append(t)
                    t_used[m] = t
                for _ in block:
                    if urgent:
                        urgent.pop(0)()
                    for _ in range(background_per_chunk):
                        if background:
                            background.pop(0)()
                n += len(block)
            for job in jobs:
                job[1].free = [t_used[n - 1]]
            flush()
            on_group(g, [j[0] for j in jobs], toks)

    def rstd(src, dst, scale, *tokens):
        t = pool.do(lambda e: e.tensor_scalar(dst, src, scale, EPS, ALU.mult, ALU.add), *tokens)
        w = dst.shape[1]
        return pool.do(lambda e: e.tensor_tensor(dst, dst, half[:, 0:w], ALU.pow), t, t_half)

    def halves(src, A, k, cols, tokens, scale=None):
        hi, lo = A.hi[:, k, cols], A.lo[:, k, cols]
        if scale is None:
            t = act.do(lambda e: e.activation(hi, src, AF.Copy), tokens, A.free)
            t2 = dve.do(lambda e: e.tensor_tensor(lo, src, hi.bitcast(F32), ALU.subtract), t, tokens, A.free)
        else:
            t = act.do(lambda e: e.activation(hi, src, AF.Copy, scale=scale), tokens, A.free)
            t2 = dve.do(lambda e: e.scalar_tensor_tensor(lo, src, scale, hi.bitcast(F32), ALU.mult, ALU.subtract),
                        t, tokens, A.free)
        A.tok[k] = [t, t2]
        return t2

    def norm(src, toks, gain, A):
        nt = A.n // P
        last = {}
        for t in range(nt):
            b = t % 2
            buf = xn[b]
            t1 = act.do(lambda e, t=t, buf=buf: e.activation(buf[:, :], src[:, t, :], AF.Square,
                                                             accum_out=stat[:, t:t + 1]), toks[t], xn_free[b],
                        stat_free)
            t2 = rstd(stat[:, t:t + 1], stat[:, 8 + t:9 + t], 1.0 / D, t1, stat_free)
            t3 = dve.do(lambda e, t=t, buf=buf: e.tensor_scalar(buf[:, :], src[:, t, :], stat[:, 8 + t:9 + t], None,
                                                                ALU.mult), t1, t2, toks[t])
            for c in range(KD):
                if t == 0:
                    pe.wait(banks[c].free)
                last[c] = pe.do(lambda e, c=c, t=t, buf=buf: e.transpose(banks[c].ap[:, t * P:(t + 1) * P],
                                                                         buf[:, c * P:(c + 1) * P], ident),
                                t3, t_cst, mark=t == nt - 1 or c == KD - 1)
            xn_free[b] = [last[KD - 1]]
        stat_free[:] = [t3]
        for c in range(KD):
            banks[c].free = [halves(banks[c].ap[:, 0:A.n], A, c, slice(0, A.n), last[c], gain[:, c:c + 1])]

    stat_free = []

    def add_to_x(scale):
        def on_group(g, bk, toks):
            for t in range(NT):
                xs = x[:, t, g * 512:(g + 1) * 512]
                tk = dve.do(lambda e, xs=xs, b=bk[t]: e.scalar_tensor_tensor(xs, b.ap[:, :], scale, xs, ALU.mult,
                                                                             ALU.add), toks[t], xtok[t])
                bk[t].free = [tk]
                xtok[t] = [tk]
        return on_group

    def handover():
        toks = [q.now() for q in (pe, act, dve, pool)]
        for q in (act, dve, pool):
            q.wait(*toks)

    def copy_out(engine, dst, src, *tokens):
        if engine is act:
            return act.do(lambda e: e.activation(dst, src, AF.Copy), *tokens)
        return engine.do(lambda e: e.tensor_copy(dst, src), *tokens)

    def head_norm(tmp, t, nh, hd, sq, ss, tok, sq_free):
        v = tmp[:, t, :].rearrange("p (h d) -> p h d", h=nh)
        s3 = sq[:, :].rearrange("p (h d) -> p h d", h=nh)
        t1 = dve.do(lambda e: e.tensor_tensor(sq[:, :], tmp[:, t, :], tmp[:, t, :], ALU.mult), tok, sq_free)
        r = ss[:, t, 0:nh]
        t2 = dve.do(lambda e: e.tensor_reduce(r, s3, AX, ALU.add), t1)
        xn_free[0] = [t2]
        t3 = rstd(r, r, 1.0 / hd, t2)
        return dve.do(lambda e: e.tensor_tensor(v, v, r.unsqueeze(2).to_broadcast([P, nh, hd]), ALU.mult), t3, t2)

    def turn(tmp, tt, blocks, bk, dsts, gains, nt, last_use):
        toks = []
        for c in range(blocks):
            bank = bk[c]
            pe.wait(bank.free)
            for t in range(nt):
                tk = pe.do(lambda e, c=c, t=t, bank=bank: e.transpose(bank.ap[:, t * P:(t + 1) * P],
                                                                      tmp[:, t, c * P:(c + 1) * P], ident),
                           tt[t], mark=t == nt - 1)
            last_use.append(tk)
            if gains is None:
                q = act if c % 2 else dve
                r = copy_out(q, dsts[c], bank.ap[:, 0:nt * P], tk)
            elif c % 2:
                r = act.do(lambda e, c=c, bank=bank: e.activation(dsts[c], bank.ap[:, 0:nt * P], AF.Copy,
                                                                  scale=gains[c]), tk)
            else:
                r = dve.do(lambda e, c=c, bank=bank: e.tensor_scalar(dsts[c], bank.ap[:, 0:nt * P], gains[c], None,
                                                                     ALU.mult), tk)
            bank.free = [r]
            toks.append(r)
        return toks

    def widths(lo, n):
        out_, o = [], 0
        for i in range(n):
            k0, k1 = lo(i)
            out_.append((k0, k1, o, (k1 - k0) * P))
            o += (k1 - k0) * P
        return out_, o

    def attend(st, tag, H, tiles, score, value, O, mode="softmax", bias=None, sink=None, scale=1.0, nk=NT,
               before=None, st2=None):
        spans, total = tiles
        Pb = [sb(f"{tag}P{i}", [P, total], F32, st) for i in range(2)]
        PT = [sb(f"{tag}PT{i}", [P, nk, S], F32, st2 or st) for i in range(2)]
        sm = [sb(f"{tag}sm{i}", [P, 24], F32, st) for i in range(2)]
        stick = mode == "stick"
        Qb = [sb(f"{tag}Q{i}", [P, total + NT], F32, st) for i in range(2)] if stick else None
        Zr = sb(f"{tag}Z", [P, 512], F32, st) if stick else None
        causal = total == 10 * P
        sgroups = [[0, 1], [2], [3]] if causal else [[0, 1], [2, 3]]
        groups = [[3], [2, 0], [1]] if causal else [[0, 1], [2, 3]]
        tbank = 6 - len(groups)
        place = {}
        for n, group in enumerate(sgroups):
            at = 0
            for i in group:
                place[i] = banks[n].ap[:, at:at + spans[i][3]]
                at += spans[i][3]
        P_free, PT_free = [[], []], [[], []]
        ready, turned = {}, {}
        t_one = None
        if stick:
            t_one = [pool.do(lambda e: e.memset(Zr[:, :], 0.0))]
            t_one += [pool.do(lambda e, b=b: e.memset(Qb[b][:, :], 1.0)) for b in range(2)]

        def first_half(h):
            b = h % 2
            p, m = Pb[b], sm[b]
            mx, nm, den, es, rd = (m[:, 4 * i:4 * i + 4] for i in range(5))
            got = [None] * NT
            for n, group in enumerate(sgroups):
                bank = banks[n]
                pe.wait(bank.free)
                for i in group:
                    k0, k1, o, W = spans[i]
                    tk = score(h, i, place[i], k0, k1)
                if stick:
                    for i in group:
                        dg = place[i][:, spans[i][3] - P:spans[i][3]]
                        t0 = dve.do(lambda e, dg=dg: e.tensor_tensor(dg, dg, mis("strict"), ALU.add), tk, t_cst)
                for i in group:
                    k0, k1, o, W = spans[i]
                    pw, src = p[:, o:o + W], place[i]
                    if stick:
                        kp_ = Qb[b][:, o + i:o + i + W]
                        t1 = act.do(lambda e, pw=pw, src=src: e.activation(pw, src, AF.Sigmoid), t0, P_free[b], t_one)
                        t2 = act.do(lambda e, kp_=kp_, src=src: e.activation(kp_, src, AF.Sigmoid, scale=-1.0),
                                    P_free[b], t_one)
                        got[i] = (t1, t2)
                    elif bias is not None:
                        bt, btok = bias(h, i, W)
                        t2 = got[i] = dve.do(lambda e, pw=pw, src=src, bt=bt, i=i: e.tensor_tensor_reduce(
                            pw, src, bt, 1.0, FLOOR, ALU.add, ALU.max, mx[:, i:i + 1]), tk, btok, P_free[b])
                    else:
                        t2 = got[i] = dve.do(lambda e, src=src, i=i: e.tensor_reduce(mx[:, i:i + 1], src, AX, ALU.max),
                                             tk, P_free[b])
                bank.free = [t2]
            if stick:
                ready[h] = got
                return
            if sink is not None:
                t2 = dve.do(lambda e: e.tensor_scalar(nm, mx, sink[:, h:h + 1], -1.0, ALU.max, ALU.mult), got)
            else:
                t2 = dve.do(lambda e: e.tensor_scalar(nm, mx, -scale, None, ALU.mult), got)
            ready[h] = t2

        def exps(h):
            b = h % 2
            p, m = Pb[b], sm[b]
            nm, den, es = (m[:, 4 * i:4 * i + 4] for i in range(1, 4))
            t2 = ready[h]
            for i, (k0, k1, o, W) in enumerate(spans):
                pw = p[:, o:o + W]
                src = pw if bias is not None else place[i]
                t3 = act.do(lambda e, pw=pw, src=src, i=i: e.activation(pw, src, AF.Exp, bias=nm[:, i:i + 1],
                                                                        scale=scale, accum_out=den[:, i:i + 1]),
                            t2, P_free[b])
                if bias is None:
                    banks[i // 2].free = [t3]
            if sink is not None:
                t3 = act.do(lambda e: e.activation(es, nm, AF.Exp, bias=sink[:, h:h + 1]), t2)
            ready[h] = t3

        def second_half(h):
            b = h % 2
            p, m = Pb[b], sm[b]
            den, es, rd = (m[:, 4 * i:4 * i + 4] for i in range(2, 5))
            toks = []
            if stick:
                for i, (k0, k1, o, W) in enumerate(spans):
                    q = Qb[b][:, o + i:o + i + W + 1]
                    t1, t2 = ready[h][i]
                    rev = Qb[b][:, o + i:o + i + W][:, ::-1]
                    t3 = dve.do(lambda e, rev=rev, W=W: e.tensor_tensor_scan(rev, rev, Zr[:, 0:W], 1.0, ALU.mult,
                                                                             ALU.add), t1, t2, t_one)
                    pw = p[:, o:o + W]
                    toks.append(dve.do(lambda e, pw=pw, q=q, W=W: e.tensor_tensor(pw, pw, q[:, 1:W + 1], ALU.mult), t3))
                ready[h] = toks
                return
            t = ready[h]
            if sink is not None:
                t = dve.do(lambda e: e.tensor_tensor(den, den, es, ALU.add), t)
            t = dve.do(lambda e: e.reciprocal(rd, den), t)
            for i, (k0, k1, o, W) in enumerate(spans):
                pw = p[:, o:o + W]
                toks.append(dve.do(lambda e, pw=pw, i=i: e.tensor_scalar(pw, pw, rd[:, i:i + 1], None, ALU.mult), t))
            ready[h] = toks

        def turn_head(h):
            b = h % 2
            cp = []
            for n, group in enumerate(groups):
                bank = banks[tbank + n]
                pe.wait(bank.free)
                at = 0
                for i in group:
                    k0, k1, o, W = spans[i]
                    for j in range(k1 - k0):
                        tk = pe.do(lambda e, j=j, o=o, at=at, bank=bank: e.transpose(
                            bank.ap[:, at + j * P:at + (j + 1) * P], Pb[b][:, o + j * P:o + (j + 1) * P], ident),
                            ready[h][i], mark=i == group[-1] and j == k1 - k0 - 1)
                    at += W
                at = 0
                for i in group:
                    k0, k1, o, W = spans[i]
                    t = copy_out(dve if stick or n % 2 else act, PT[b][:, k0:k1, i * P:(i + 1) * P],
                                 bank.ap[:, at:at + W].rearrange("p (k q) -> p k q", k=k1 - k0), tk, PT_free[b])
                    at += W
                bank.free = [t]
                cp.append(t)
            P_free[b] = [tk]
            turned[h] = cp

        def product(h):
            b = h % 2
            pe.wait(turned[h])
            t, finish = value(h, PT[b])
            PT_free[b] = [t]
            return finish

        finish = None
        for s in range(H + 3):
            if 1 <= s <= H:
                second_half(s - 1)
            if s < H:
                if before is not None:
                    before(s)
                first_half(s)
            if finish is not None:
                finish()
                finish = None
            if 1 <= s <= H:
                turn_head(s - 1)
            if s < H and not stick:
                exps(s)
            if 2 <= s < H + 2:
                finish = product(s - 2)

    def causal_scores(qT, kT, qtok, ktok, kv_of, dup):
        def score(h, i, dst, k0, k1):
            r = slice(64 * (h % 2), 64 * (h % 2) + 64)
            kb = kv_of(h) if dup else h // 2
            return pe.do(lambda e: e.matmul(dst, qT[r, h // 2, i * P:(i + 1) * P], kT[r, kb, k0 * P:k1 * P],
                                            start=True, stop=True), qtok[h // 2], ktok[kb])
        return score

    def pair_values(V, O, base, spans, causal, vtok):
        def value(h, PTb):
            pair = h // 2
            bank = banks[6 + pair % 2]
            if h % 2 == 0:
                pe.wait(bank.free)
            pe.wait(vtok)
            r = slice(64 * (h % 2), 64 * (h % 2) + 64)
            if causal:
                for kt in range(NT):
                    t = pe.do(lambda e, kt=kt: e.matmul(bank.ap[r, kt * P:S], V(h, kt), PTb[:, kt, kt * P:S],
                                                        start=kt == 0, stop=kt == NT - 1), mark=kt == NT - 1)
            else:
                for i, (k0, k1, o, W) in enumerate(spans):
                    for kt in range(k0, k1):
                        t = pe.do(lambda e, kt=kt, i=i, k0=k0, k1=k1: e.matmul(
                            bank.ap[r, i * P:(i + 1) * P], V(h, kt), PTb[:, kt, i * P:(i + 1) * P],
                            start=kt == k0, stop=kt == k1 - 1), mark=i == NT - 1 and kt == k1 - 1)

            def finish():
                bank.free = [halves(bank.ap[:, :], O, base + pair, slice(0, S), t)]
            return t, finish if h % 2 else None
        return value

    causal_tiles = widths(lambda i: (0, i + 1), NT)

    def even_mixer(st):
        handover()
        s_b = sem("s_evb")
        evb = sb("evb", [P, 8 * 256], F32, st)
        t_evb = pool.dma(evb[:, :], T["evb"], s_b)
        qs = sb("e_qs", [P, 1], F32, st)
        ta = sb("e_ta", [P, NT, 512], F32, st)
        tk_ = sb("e_tk", [P, NT, 256], F32, st)
        kd = sb("e_kd", [P, NT, 256], F32, st)
        vb = sb("e_vb", [P, NT, 512], F32, st)
        ss = sb("e_ss", [P, NT, 8], F32, st)
        sk = sb("e_sk", [P, NT, 2], F32, st)
        qaT = sb("e_qaT", [P, 4, S], F32, st)
        kaT = sb("e_kaT", [P, 2, S], F32, st)
        qbT = sb("e_qbT", [P, 4, S], F32, st)
        kbT = sb("e_kbT", [P, 4, S], F32, st)
        t_qs = dve.do(lambda e: e.tensor_scalar(qs[:, :], par("ev_q_gain"), 0.125, None, ALU.mult), t_cst)
        tok = {"q": [], "k": [], "vb": [], "qb": [], "kb": []}

        def on_group(g, bk, toks):
            if g == 0:
                tt = []
                for t in range(NT):
                    e1 = copy_out(act, ta[:, t, :], bk[t].ap[:, :], toks[t])
                    bk[t].free = [e1]
                    tt.append(head_norm(ta, t, 8, 64, xn[0][:, 0:512], ss, e1, xn_free[0]))
                later.append(lambda: tok["q"].extend(
                    turn(ta, tt, 4, bk, [qaT[:, c, :] for c in range(4)], [qs[:, :]] * 4, NT, [])))
                dve.wait(t_qs)
                act.wait(t_qs)
            elif g == 1:
                tt = []
                for t in range(NT):
                    e1 = copy_out(act, tk_[:, t, :], bk[t].ap[:, 0:256], toks[t])
                    bk[t].free = [e1]
                    sq = xn[1][:, 0:128]
                    k3 = tk_[:, t, 0:128].rearrange("p (h d) -> p h d", h=2)
                    t1 = dve.do(lambda e, t=t: e.tensor_tensor(sq, tk_[:, t, 0:128], tk_[:, t, 0:128], ALU.mult), e1,
                                xn_free[1])
                    r = sk[:, t, :]
                    t2 = dve.do(lambda e, r=r: e.tensor_reduce(r, sq.rearrange("p (h d) -> p h d", h=2), AX, ALU.add), t1)
                    xn_free[1] = [t2]
                    t3 = rstd(r, r, 1.0 / 64, t2)
                    kdv = kd[:, t, :].rearrange("p (h u d) -> p h u d", h=2, u=2)
                    for u in range(2):
                        t4 = dve.do(lambda e, r=r, u=u, kdv=kdv, k3=k3: e.tensor_tensor(
                            kdv[:, :, u, :], k3, r.unsqueeze(2).to_broadcast([P, 2, 64]), ALU.mult), t3)
                    tt.append(t4)
                later.append(lambda: tok["k"].extend(
                    turn(kd, tt, 2, bk, [kaT[:, c, :] for c in range(2)], [par("ev_k_gain")] * 2, NT, [])))
            elif g == 2:
                for t in range(NT):
                    e1 = copy_out(act if t % 2 else dve, vb[:, t, :], bk[t].ap[:, :], toks[t])
                    bk[t].free = [e1]
                    tok["vb"].append(e1)
            else:
                for c in range(4):
                    if g == 3:
                        e1 = act.do(lambda e, c=c: e.activation(qbT[:, c, :], bk[c].ap[:, :], AF.Copy, scale=0.125),
                                    toks[c])
                    else:
                        e1 = copy_out(dve, kbT[:, c, :], bk[c].ap[:, :], toks[c])
                    bk[c].free = [e1]
                    tok["qb" if g == 3 else "kb"].append(e1)

        gemm("in0", {"h": hT}, on_group)
        flush()
        band = widths(lambda i: (max(i - 1, 0), i + 1), NT)
        attend(st.sub(), "ea", 8, band, causal_scores(qaT, kaT, tok["q"], tok["k"], lambda h: h // 4, True),
                   pair_values(lambda h, kt: tk_[:, kt, 128 + 64 * (h // 4):192 + 64 * (h // 4)], hT, 0, band[0], False, None),
                   hT, bias=lambda h, i, W: (evb[:, 256 * (h + 1) - W:256 * (h + 1)], [t_evb]), sink=par("ev_sinks"))
        handover()
        attend(st.sub(), "eb", 8, causal_tiles, causal_scores(qbT, kbT, tok["qb"], tok["kb"], None, False),
                   pair_values(lambda h, kt: vb[:, kt, 64 * h:64 * h + 64], hT, 4, None, True, tok["vb"]),
                   hT, mode="stick")

    def odd_mixer(st):
        handover()
        qs = sb("o_qs", [P, 1], F32, st)
        tmp = [sb(f"o_t{i}", [P, NT, 512], F32, st) for i in range(2)]
        tmp_free = [[], []]
        v = sb("o_v", [P, NT, D], F32, st)
        ss = [sb(f"o_ss{i}", [P, NT, 8], F32, st) for i in range(2)]
        qT = sb("o_qT", [P, 8, S], F32, st)
        kT = sb("o_kT", [P, 8, S], F32, st)
        t_qs = dve.do(lambda e: e.tensor_scalar(qs[:, :], par("od_q_gain"), 0.125, None, ALU.mult), t_cst)
        act.wait(t_qs)
        dve.wait(t_qs)
        tok = {"q": [], "k": [], "v": []}

        def on_group(g, bk, toks):
            if g < 4:
                b = g % 2
                tt = []
                for t in range(NT):
                    e1 = copy_out(act, tmp[b][:, t, :], bk[t].ap[:, :], toks[t], tmp_free[b])
                    bk[t].free = [e1]
                    tt.append(head_norm(tmp[b], t, 8, 64, xn[0][:, 0:512], ss[b], e1, xn_free[0]))
                dst = qT if g < 2 else kT
                gain = qs[:, :] if g < 2 else par("od_k_gain")

                def go():
                    used = []
                    tok["q" if g < 2 else "k"].extend(
                        turn(tmp[b], tt, 4, bk, [dst[:, 4 * (g % 2) + c, :] for c in range(4)], [gain] * 4, NT, used))
                    tmp_free[b] = used
                later.append(go)
            else:
                for t in range(NT):
                    e1 = copy_out(act if t % 2 else dve, v[:, t, 512 * (g - 4):512 * (g - 3)], bk[t].ap[:, :], toks[t])
                    bk[t].free = [e1]
                    tok["v"].append(e1)

        gemm("in1", {"h": hT}, on_group)
        flush()
        handover()
        ob = [tmp[0][:, i, :] for i in range(4)]
        s_ob = [sem(f"s_ob{i}") for i in range(4)]
        t_ob, ob_free = {}, [[]] * 4

        def fetch(h):
            if h < 16:
                t_ob[h] = pool.dma(ob[h % 4], T["odb"][:, 512 * h:512 * (h + 1)], s_ob[h % 4], ob_free[h % 4])

        for h in range(3):
            fetch(h)

        def before(h):
            if h >= 1:
                ob_free[(h - 1) % 4] = [dve.now()]
            fetch(h + 3)

        attend(st.sub(), "oc", 16, causal_tiles, causal_scores(qT, kT, tok["q"], tok["k"], None, False),
                   pair_values(lambda h, kt: v[:, kt, 64 * h:64 * h + 64], hT, 0, None, True, tok["v"]),
                   hT, bias=lambda h, i, W: (ob[h % 4][:, 512 - W:512], [t_ob[h]]), before=before)

    def cross(st, l):
        handover()
        s_m = sem(f"s_mem{l}")
        mx_ = sb(f"c{l}m", [P, 2, D], F32, st)
        M = Act(sb(f"c{l}mh", [P, KD, MEM], F32R, st), sb(f"c{l}ml", [P, KD, MEM], F32R, st), MEM)
        tm = [sb(f"c{l}t{i}", [P, NT, 512], F32, st) for i in range(2)]
        tm_free = [[], []]
        v = sb(f"c{l}v", [P, 2, D], F32, st)
        ss = [sb(f"c{l}ss{i}", [P, NT, 2], F32, st) for i in range(2)]
        kT = sb(f"c{l}kT", [P, 8, MEM], F32, st)
        qT = sb(f"c{l}qT", [P, 8, S], F32, st)
        t_m = pool.dma(mx_[:, :, :], T["mem"][0].rearrange("(t p) d -> p t d", p=P), s_m)
        tok = {"q": [], "k": [], "v": []}
        gains = {n: par(f"xa_{n}_gain{l}") for n in "qk"}

        def heads(which, nt, dst, g, bk, toks):
            b = g % 2
            tt = []
            for t in range(nt):
                e1 = copy_out(act, tm[b][:, t, :], bk[t].ap[:, :], toks[t], tm_free[b])
                bk[t].free = [e1]
                tt.append(head_norm(tm[b], t, 2, 256, xn[0][:, 0:512], ss[b], e1, xn_free[0]))

            def go():
                used = []
                tok[which].extend(turn(tm[b], tt, 4, home, [dst[:, 4 * g + c, :] for c in range(4)],
                                       [gains[which][:, c % 2:c % 2 + 1] for c in range(4)], nt, used))
                tm_free[b] = used
            home = banks[4 * (banks.index(bk[0]) // 4):4 * (banks.index(bk[0]) // 4) + 4]
            later.append(go)

        def on_kv(g, bk, toks):
            if g < 2:
                heads("k", 2, kT, g, bk, toks)
            else:
                for t in range(2):
                    e1 = copy_out(act if t % 2 else dve, v[:, t, 512 * (g - 2):512 * (g - 1)], bk[t].ap[:, :], toks[t])
                    bk[t].free = [e1]
                    tok["v"].append(e1)

        norm(mx_, [[t_m]] * 2, par(f"xa_mem_norm{l}"), M)
        gemm(f"kv{l}", {"m": M}, on_kv)
        flush()
        norm(x, xtok, par(f"xa_norm{l}"), hT)
        gemm(f"xq{l}", {"h": hT}, lambda g, bk, toks: heads("q", 4, qT, g, bk, toks))
        flush()

        def score(h, i, dst, k0, k1):
            for c in range(2):
                t = pe.do(lambda e, c=c: e.matmul(dst, qT[:, 2 * h + c, i * P:(i + 1) * P], kT[:, 2 * h + c, :],
                                                  start=c == 0, stop=c == 1),
                          tok["q"][2 * h + c], tok["k"][2 * h + c], mark=c == 1)
            return t

        def value(h, PTb):
            pe.wait(tok["v"])
            done_ = []
            for c in range(2):
                bank = banks[6 + c]
                pe.wait(bank.free)
                for kt in range(2):
                    t = pe.do(lambda e, kt=kt, c=c: e.matmul(
                        banks[6 + c].ap[:, :], v[:, kt, 256 * h + c * P:256 * h + (c + 1) * P], PTb[:, kt, :],
                        start=kt == 0, stop=kt == 1), mark=kt == 1)
                done_.append(t)

            def finish():
                for c in range(2):
                    banks[6 + c].free = [halves(banks[6 + c].ap[:, :], hT, 2 * h + c, slice(0, S), done_[c])]
            return t, finish

        handover()
        attend(st.sub(), f"cx{l}", 4, widths(lambda i: (0, 2), NT), score, value, hT, scale=1.0 / 16, nk=2)

    def sparse_mixer(st):
        handover()
        a0 = st.at
        vals = sb("s_v", [P, NT, 256], F32, st)
        qT = sb("s_qT", [P, 8, S], F32, st)
        kT = sb("s_kT", [P, 4, S], F32, st)
        spans, total = causal_tiles
        coef = sb("s_coef", [P, 8], F32, st)
        la = sb("s_la", [P, 5, 8], F32, st)
        sel = sb("s_sel", [P, total], F32, st)
        sc = sb("s_sc", [P, total], F32, st)
        iw = sb("s_iw", [P, NT, 8], F32, st)
        m8 = sb("s_m8", [P, 24], F32, st)
        a1 = st.at
        a2 = a1 + 32768
        tmp_area = Area(a1)
        tok = {"q": [], "k": [], "iq": [], "ik": [], "v": []}

        lam = par("rg_lambda")
        t = pool.do(lambda e: e.tensor_scalar(la[:, 1, :], lam, -1.0, None, ALU.mult), t_cst)
        t = dve.do(lambda e: e.tensor_tensor(la[:, 0, :], la[:, 1, :], lam, ALU.max), t)
        t_e = act.do(lambda e: e.activation(la[:, 0, :], la[:, 0, :], AF.Exp, scale=-1.0), t)
        t = pool.do(lambda e: e.tensor_scalar(la[:, 2, :], la[:, 0, :], 2.0, None, ALU.add), t_e)
        t = dve.do(lambda e: e.reciprocal(la[:, 2, :], la[:, 2, :]), t)
        t = pool.do(lambda e: e.tensor_tensor(la[:, 2, :], la[:, 2, :], la[:, 0, :], ALU.mult), t)
        t = pool.do(lambda e: e.tensor_tensor(la[:, 3, :], la[:, 2, :], la[:, 2, :], ALU.mult), t)
        t = pool.do(lambda e: e.memset(la[:, 4, :], 1.0 / 19))
        for n in range(17, 0, -2):
            t = pool.do(lambda e: e.tensor_tensor(la[:, 4, :], la[:, 4, :], la[:, 3, :], ALU.mult), pool.now())
            t = pool.do(lambda e, n=n: e.tensor_scalar(la[:, 4, :], la[:, 4, :], 1.0 / n, None, ALU.add), t)
        t = pool.do(lambda e: e.tensor_tensor(la[:, 4, :], la[:, 4, :], la[:, 2, :], ALU.mult), t)
        t = pool.do(lambda e: e.tensor_scalar(la[:, 4, :], la[:, 4, :], 16.0, None, ALU.mult), t)
        t = pool.do(lambda e: e.tensor_scalar(la[:, 1, :], la[:, 1, :], 0.0, 8.0, ALU.max, ALU.mult), t)
        t = pool.do(lambda e: e.tensor_tensor(coef[:, :], la[:, 4, :], la[:, 1, :], ALU.add), t)
        t_coef = pool.do(lambda e: e.tensor_scalar(la[:, 0, :], coef[:, :], -1.0, None, ALU.mult), t)
        ncoef = la[:, 0, :]

        iqT = sb("s_iqT", [P, 4, S], F32, tmp_area)
        ikT = sb("s_ikT", [P, S], F32, tmp_area)
        tq = sb("s_tq", [P, NT, 512], F32, tmp_area)
        tq2 = sb("s_tq2", [P, NT, 512], F32, tmp_area)
        ti = sb("s_ti", [P, NT, 128], F32, tmp_area)
        rt = [sb(f"s_rt{i}", [P, 4, 64], F32, tmp_area) for i in range(2)]
        lng = sb("s_lng", [P, 2, 64], F32, tmp_area)
        bn = sb("s_bn", [P, NT, 10], F32, tmp_area)
        rl = [xn[0][:, 0:512], xn[0][:, 512:1024], xn[1][:, 0:512]]
        s_ln = sem("s_ln")
        pool.dma(lng[:, 0, :], T["idx_k_ln_g_2"].partition_broadcast(P), s_ln)
        t_ln = pool.dma(lng[:, 1, :], T["idx_k_ln_b_2"].partition_broadcast(P), s_ln)
        rt_free = [[], []]
        turns = [0]

        def rope(buf, t, nh, tok_):
            b = turns[0] % 2
            turns[0] += 1
            v3 = buf.rearrange("p (h d) -> p h d", d=64)
            x1, x2 = v3[:, :, 0:8], v3[:, :, 8:16]
            cs = mis("cos")[:, 8 * t:8 * t + 8].unsqueeze(1).to_broadcast([P, nh, 8])
            sn = mis("sin")[:, 8 * t:8 * t + 8].unsqueeze(1).to_broadcast([P, nh, 8])
            r = [rt[b][:, i, 0:8 * nh].rearrange("p (h d) -> p h d", d=8) for i in range(4)]
            pr = [pool.do(lambda e, o=o, a=a, c=c: e.tensor_tensor(o, a, c, ALU.mult), tok_, t_cst)
                  for o, a, c in ((r[0], x1, cs), (r[1], x2, sn), (r[2], x2, cs), (r[3], x1, sn))]
            pool.do(lambda e: e.tensor_tensor(x1, r[0], r[1], ALU.subtract), pr)
            return pool.do(lambda e: e.tensor_tensor(x2, r[2], r[3], ALU.add), pr)

        tq_free = []

        def on_idx(g, bk, toks):
            if g == 0:
                tt = []
                for t in range(NT):
                    e1 = copy_out(act, tq[:, t, :], bk[t].ap[:, :], toks[t])
                    bk[t].free = [e1]
                    tt.append(rope(tq[:, t, :], t, 8, e1))

                def go():
                    tok["iq"] = turn(tq, tt, 4, bk, [iqT[:, c, :] for c in range(4)], None, NT, tq_free)
                later.append(go)
                return
            tt = []
            for t in range(NT):
                e1 = copy_out(act, ti[:, t, 0:72], bk[t].ap[:, 0:72], toks[t])
                bk[t].free = [e1]
                k = ti[:, t, 0:64]
                w1 = pool.do(lambda e, t=t: e.tensor_scalar(iw[:, t, :], ti[:, t, 64:72], (8 ** -0.5) * (64 ** -0.5),
                                                            None, ALU.mult), e1)
                t1 = dve.do(lambda e, t=t, k=k: e.bn_stats(bn[:, t, 0:6], k), e1)
                t2 = dve.do(lambda e, t=t: e.bn_aggr(bn[:, t, 6:8], bn[:, t, 0:6]), t1)
                t3 = rstd(bn[:, t, 7:8], bn[:, t, 8:9], 1.0, t2)
                t4 = dve.do(lambda e, t=t, k=k: e.tensor_scalar(k, k, bn[:, t, 6:7], bn[:, t, 8:9], ALU.subtract,
                                                                ALU.mult), t3, t2)
                t5 = dve.do(lambda e, k=k: e.tensor_tensor(k, k, lng[:, 0, :], ALU.mult), t4, t_ln)
                t6 = dve.do(lambda e, k=k: e.tensor_tensor(k, k, lng[:, 1, :], ALU.add), t5)
                t7 = rope(k, t, 1, [t6, w1])
                tt.append(copy_out(pool, ti[:, t, 64:128], k, t7))

            def go():
                tok["ik"] = turn(ti, tt, 1, bk, [ikT[:, :]], None, NT, [])
            later.append(go)

        def on_qkv(g, bk, toks):
            tt = []
            buf = [tq2, tq, tq2][g]
            fr = [[], tq_free, tq_free2][g]
            for t in range(NT):
                e1 = copy_out(act, buf[:, t, :], bk[t].ap[:, :], toks[t], fr)
                bk[t].free = [e1]
                if g < 2:
                    tt.append(rope(buf[:, t, :], t, 8, e1))
                else:
                    r1 = rope(buf[:, t, 0:256], t, 4, e1)
                    tok["v"].append(copy_out(pool, vals[:, t, :], buf[:, t, 256:512], e1))
                    kv = tq[:, t, :].rearrange("p (h u d) -> p h u d", h=4, u=2)
                    k3 = buf[:, t, 0:256].rearrange("p (h d) -> p h d", h=4)
                    c1 = pool.do(lambda e, kv=kv, k3=k3: e.tensor_copy(kv[:, :, 0, :], k3), r1, tq_free3)
                    tt.append(pool.do(lambda e, kv=kv, k3=k3: e.tensor_copy(kv[:, :, 1, :], k3), c1))

            def go():
                if g < 2:
                    tok["q"].extend(turn(buf, tt, 4, bk, [qT[:, 4 * g + c, :] for c in range(4)], [0.125] * 4, NT,
                                         tq_free2 if g == 0 else tq_free3))
                else:
                    four[:] = bk
                    tok["k"] = turn(tq, tt, 4, bk, [kT[:, c, :] for c in range(4)], None, NT, [])
            later.append(go)
        tq_free2, tq_free3, four = [], [], []

        norm(x, xtok, par("norm_mix_pre"), hT)
        gemm("idx", {"h": hT}, on_idx)
        gemm("qkv", {"h": hT}, on_qkv)
        sctok, best = {}, {}

        def index_scores():
            rl_free = [list(xn_free[0]), list(xn_free[0]), list(xn_free[1])]
            n = 0
            for h in range(8):
                r = slice(64 * (h % 2), 64 * (h % 2) + 64)
                for i in range(1, NT):
                    _, _, o, W = spans[i]
                    bank = four[n % 4]
                    rb = rl[n % 3]
                    tk = pe.do(lambda e, r=r, h=h, i=i, W=W, bank=bank: e.matmul(
                        bank.ap[:, 0:W], iqT[r, h // 2, i * P:(i + 1) * P], ikT[r, 0:W], start=True, stop=True),
                        bank.free, tok["iq"][h // 2], tok["ik"])
                    t1 = act.do(lambda e, rb=rb, W=W, bank=bank: e.activation(rb[:, 0:W], bank.ap[:, 0:W], AF.Relu), tk,
                                rl_free[n % 3])
                    bank.free = [t1]
                    s_, w_ = sc[:, o:o + W], iw[:, i, h:h + 1]
                    if h == 0:
                        t2 = dve.do(lambda e, s_=s_, w_=w_, rb=rb, W=W: e.tensor_scalar(s_, rb[:, 0:W], w_, None, ALU.mult),
                                    t1, pool.now())
                    else:
                        t2 = dve.do(lambda e, s_=s_, w_=w_, rb=rb, W=W: e.scalar_tensor_tensor(
                            s_, rb[:, 0:W], w_, s_, ALU.mult, ALU.add), t1, sctok[i])
                    sctok[i] = t2
                    rl_free[n % 3] = [t2]
                    n += 1
            xn_free[0], xn_free[1] = rl_free[0] + rl_free[1], rl_free[2]
            handover()
            best[0] = dve.do(lambda e: e.tensor_copy(sel[:, 0:P], mis("causal")), t_cst)
            three = [select(i) for i in range(1, NT)]
            for r in range(18):
                for s_ in three:
                    background.append(s_[r])

        later.append(index_scores)

        def select(i):
            _, _, o, W = spans[i]
            s_, w_, m_ = sc[:, o:o + W], sel[:, o:o + W], m8[:, 8 * (i - 1):8 * i]
            dg = sc[:, o + W - P:o + W]

            def start():
                t = pool.do(lambda e: e.affine_select(out=dg, in_=dg, compare_op=ALU.is_ge, fill=FLOOR, base=0,
                                                      pattern=[[-1, P]], channel_multiplier=1), sctok[i])
                best[i] = dve.do(lambda e: e.tensor_copy(w_, s_), t)

            def round_():
                t = dve.do(lambda e: e.max(m_, w_), best[i])
                best[i] = dve.do(lambda e: e.match_replace(w_, m_, w_, TAKEN), t)

            def end():
                t = dve.do(lambda e: e.tensor_tensor(w_, w_, s_, ALU.is_equal), best[i])
                best[i] = dve.do(lambda e: e.tensor_scalar(w_, w_, NEG, None, ALU.mult), t)
            return [start] + [round_] * 16 + [end]

        y_area = Area(a1)
        Y = Act(sb("s_Yh", [P, KD, S], F32R, y_area), sb("s_Yl", [P, KD, S], F32R, y_area), S)
        rn = Area(a2)
        wa = sb("s_wa", [P, 8, P], F32, rn)
        wx = sb("s_wx", [P, 8, P], F32, rn)
        s_g = sem("s_g")
        pool.dma(wa[:, :, :], T["wa_l"], s_g)
        t_g = pool.dma(wx[:, :, :], T["wx_l"], s_g)
        xp = sb("s_xp", [P, 2, S + 3], F32, rn)
        xc = sb("s_xc", [P, 2, S], F32, rn)
        gr = xn[1][:, :].rearrange("p (j s) -> p j s", j=2)
        ra = sb("s_ra", [P, 2, S], F32, rn)
        ri = sb("s_ri", [P, 2, S], F32, rn)
        th = sb("s_th", [P, 2, S], F32, rn)
        t_pad = pool.do(lambda e: e.memset(xp[:, :, :], 0.0))
        fr = {"xp": [t_pad], "gr": [], "rest": []}

        def on_rnn(g, bk, toks):
            tc, tg = [], []
            for j in range(2):
                c = 2 * g + j
                e1 = copy_out(act, xp[:, j, 3:S + 3], bk[j].ap[:, :], toks[j], fr["xp"])
                bk[j].free = [e1]
                cw = lambda k, c=c: prm[:, PRM["conv_w"][0] + 8 * k + c:PRM["conv_w"][0] + 8 * k + c + 1]
                t1 = act.do(lambda e, j=j, c=c, cw=cw: e.activation(xc[:, j, :], xp[:, j, 0:S], AF.Identity,
                                                                    bias=par("conv_b")[:, c:c + 1], scale=cw(0)),
                            e1, fr["rest"])
                for k in range(1, 4):
                    t1 = dve.do(lambda e, j=j, k=k, cw=cw: e.scalar_tensor_tensor(
                        xc[:, j, :], xp[:, j, k:k + S], cw(k), xc[:, j, :], ALU.mult, ALU.add), t1)
                tc.append(t1)
            for j in range(2):
                e1 = act.do(lambda e, j=j: e.activation(gr[:, j, :], bk[2 + j].ap[:, :], AF.Gelu_apprx_tanh),
                            toks[2 + j], fr["gr"])
                bk[2 + j].free = [e1]
                tg.append(e1)
            fr["xp"] = list(tc)

            ts, tz, tu = [], [], []

            def gates():
                for j in range(2):
                    c = 2 * g + j
                    for m, (w_, bias_, dst) in enumerate(((wa, "rg_b_a", ra), (wx, "rg_b_x", ri))):
                        bank = bk[2 * j + m]
                        pe.wait(bank.free)
                        tk = pe.do(lambda e, w_=w_, c=c, j=j, bank=bank: e.matmul(
                            bank.ap[:, :], w_[:, c, :], xc[:, j, :], start=True, stop=True), t_g, tc[j])
                        t1 = act.do(lambda e, bank=bank, dst=dst, j=j, c=c, bias_=bias_: e.activation(
                            dst[:, j, :], bank.ap[:, :], AF.Sigmoid, bias=par(bias_)[:, c:c + 1]), tk, fr["rest"])
                        bank.free = [t1]
                        ts.append(t1)

            def rates():
                for j in range(2):
                    c = 2 * g + j
                    tz.append(act.do(lambda e, j=j, c=c: e.activation(th[:, j, :], ra[:, j, :], AF.Tanh,
                                                                      scale=coef[:, c:c + 1]), ts, t_coef, fr["rest"]))
                    ta_ = act.do(lambda e, j=j, c=c: e.activation(ra[:, j, :], ra[:, j, :], AF.Exp,
                                                                  scale=ncoef[:, c:c + 1]), ts, tz)
                    t1 = pool.do(lambda e, j=j: e.tensor_tensor(xc[:, j, :], xc[:, j, :], ri[:, j, :], ALU.mult), ts,
                                 pe.now())
                    t2 = pool.do(lambda e, j=j: e.tensor_tensor(ri[:, j, :], ra[:, j, :], ra[:, j, :], ALU.mult), t1,
                                 ta_)
                    tu.append((dve.do(lambda e, j=j: e.scalar_tensor_tensor(
                        th[:, j, :], ri[:, j, :], 1.0, th[:, j, :], ALU.add, ALU.mult), t2, tz[j]), ta_))

            def scan():
                for j in range(2):
                    c = 2 * g + j
                    t1 = act.do(lambda e, j=j: e.activation(th[:, j, :], th[:, j, :], AF.Sqrt), tu[j][0])
                    t2 = dve.do(lambda e, j=j: e.tensor_tensor(th[:, j, :], th[:, j, :], xc[:, j, :], ALU.mult), t1, tu[j][0])
                    t3 = dve.do(lambda e, j=j: e.tensor_tensor_scan(ri[:, j, :], ra[:, j, :], th[:, j, :], 0.0, ALU.mult,
                                                                    ALU.add), t2, tu[j][1])
                    t4 = dve.do(lambda e, j=j: e.tensor_tensor(gr[:, j, :], gr[:, j, :], ri[:, j, :], ALU.mult), t3,
                                tg[j])
                    t5 = halves(gr[:, j, :], Y, c, slice(0, S), t4)
                fr["gr"] = [t5]
                fr["rest"] = [t5]

            urgent.extend([gates, rates, scan])

        gemm("rnn", {"h": hT}, on_rnn, 1)
        mg_area, gb_area = Area(a2), Area(a1)
        Mg = sb("s_mg", [P, 8, S], F32, mg_area)
        GB = sb("s_gb", [P, 8, S], F32, gb_area)
        gt = [xn[i // 2][:, S * (i % 2):S * (i % 2) + S] for i in range(4)]
        gt_free = [xn_free[i // 2] for i in range(4)]
        gt_tok = {}
        mtok = {}

        def on_ya(g, bk, toks):
            for j in range(4):
                if g % 2 == 0:
                    gt_tok[j] = act.do(lambda e, j=j: e.activation(gt[j], bk[j].ap[:, :], AF.Sigmoid), toks[j],
                                       gt_free[j], fr["gr"])
                    bk[j].free = [gt_tok[j]]
                else:
                    if g == 1 and j == 0:
                        handover()
                    c = 4 * (g // 2) + j
                    mtok[c] = dve.do(lambda e, j=j, c=c: e.tensor_tensor(Mg[:, c, :], gt[j], bk[j].ap[:, :], ALU.mult),
                                     gt_tok[j], toks[j])
                    bk[j].free = [mtok[c]]
                    gt_free[j] = [mtok[c]]
                    xn_free[j // 2] = [mtok[c]]

        gtok = {}

        def on_gb(g, bk, toks):
            for c in range(4):
                t1 = act.do(lambda e, c=c: e.activation(GB[:, 4 * g + c, :], bk[c].ap[:, :], AF.Sigmoid), toks[c])
                bk[c].free = [t1]
                gtok[4 * g + c] = t1

        gemm("ya", {"h": hT, "y": Y}, on_ya, 2)
        handover()
        gemm("gb", {"h": hT}, on_gb, 1)
        while background:
            background.pop(0)()
        handover()
        attend(Area(a2 + 16384), "sx", 16, causal_tiles, causal_scores(qT, kT, tok["q"], tok["k"], lambda h: h // 4, True),
                   pair_values(lambda h, kt: vals[:, kt, 64 * (h // 4):64 * (h // 4) + 64], hT, 0, None, True, tok["v"]),
                   hT, bias=lambda h, i, W: (sel[:, spans[i][2]:spans[i][2] + W], [best[i]]), st2=Area(a1 + 16384))
        handover()
        Z = Act(sb("s_Zh", [P, KD, S], F32R, Area(a1 + 16384)), sb("s_Zl", [P, KD, S], F32R, Area(a0 + 4096)), S)

        def on_yb(g, bk, toks):
            for c in range(4):
                k = 4 * g + c
                t1 = dve.do(lambda e, c=c, k=k: e.tensor_tensor(GB[:, k, :], GB[:, k, :], bk[c].ap[:, :], ALU.mult),
                            toks[c], gtok[k])
                bk[c].free = [t1]
                t2 = dve.do(lambda e, k=k: e.tensor_tensor(GB[:, k, :], GB[:, k, :], Mg[:, k, :], ALU.add), t1, mtok[k])
                halves(GB[:, k, :], Z, k, slice(0, S), t2)

        gemm("yb", {"h": hT}, on_yb)
        post_norm(Area(a2 + 16384), "wo", {"y": Z}, "s_", T["norm_mix_post_2"])

    def post_norm(area, name, acts, tag, gain):
        gb = sb(tag + "pg", [P, D], F32, area)
        s_p = sem(tag + "s_pg")
        t_p = pool.dma(gb[:, :], gain.partition_broadcast(P), s_p)
        held = []
        gemm(name, acts, lambda g, bk, toks: held.append((bk, toks)))
        def tile(t):
            b = t % 2
            two = [(held[g][0][t], held[g][1][t], slice(512 * g, 512 * g + 512)) for g in range(2)]
            t1 = [act.do(lambda e, k=k, c=c, g=g: e.activation(xn[b][:, c], k.ap[:, :], AF.Square,
                                                              accum_out=stat[:, 4 * g + t:4 * g + t + 1]),
                         tk, xn_free[b], stat_free) for g, (k, tk, c) in enumerate(two)]
            r = stat[:, 8 + t:9 + t]
            t2 = pool.do(lambda e: e.tensor_tensor(r, stat[:, t:t + 1], stat[:, 4 + t:5 + t], ALU.add), t1, stat_free)
            t2 = rstd(r, r, 1.0 / D, t2)
            t3 = [dve.do(lambda e, k=k, c=c: e.scalar_tensor_tensor(xn[b][:, c], k.ap[:, :], r, gb[:, c], ALU.mult,
                                                                    ALU.mult), t1, t2, t_p) for k, _, c in two]
            for k, _, _ in two:
                k.free = [t3[1]]
            t4 = dve.do(lambda e: e.tensor_tensor(x[:, t, :], x[:, t, :], xn[b][:, :], ALU.add), t3, xtok[t])
            xtok[t] = [t4]
            xn_free[b] = [t4]
            return t4

        for t in range(NT):
            t4 = tile(t)
        stat_free[:] = [t4]

    def ffn(up, down, tag, after):
        area = Area(base)
        handover()
        F = Act(sb(tag + "Fh", [P, KF, S], F32R, area), sb(tag + "Fl", [P, KF, S], F32R, area), S)
        sg = [sb(f"{tag}sg{i}", [P, S], F32, area) for i in range(2)]
        pr = [sb(f"{tag}pr{i}", [P, S], F32, area) for i in range(2)]
        sg_free, pr_free = [[], []], [[], []]

        def on_group(g, bk, toks):
            for j in range(2):
                t1 = act.do(lambda e, j=j: e.activation(sg[j][:, :], bk[j].ap[:, :], AF.Silu), toks[j], sg_free[j])
                bk[j].free = [t1]
                t2 = dve.do(lambda e, j=j: e.tensor_tensor(pr[j][:, :], sg[j][:, :], bk[2 + j].ap[:, :], ALU.mult),
                            t1, toks[2 + j], pr_free[j])
                bk[2 + j].free = [t2]
                sg_free[j] = [t2]
                pr_free[j] = [halves(pr[j][:, :], F, 2 * g + j, slice(0, S), t2)]

        gemm(up, {"h": hT}, on_group)
        after(area, down, {"f": F})

    def half_added(area, name, acts):
        gemm(name, acts, add_to_x(0.5))

    def whole():
        for l in range(2):
            norm(x, xtok, par(f"ffn1_norm{l}"), hT)
            ffn(f"f1u{l}", f"f1d{l}", f"f1{l}", half_added)
            if stop == f"f1{l}":
                return
            norm(x, xtok, par(f"mix_norm{l}"), hT)
            (even_mixer if l == 0 else odd_mixer)(Area(base))
            gemm(f"out{l}", {"h": hT}, add_to_x(1.0))
            if stop == f"mix{l}":
                return
            cross(Area(base), l)
            gemm(f"xo{l}", {"h": hT}, add_to_x(1.0))
            if stop == f"xa{l}":
                return
            norm(x, xtok, par(f"ffn2_norm{l}"), hT)
            ffn(f"f2u{l}", f"f2d{l}", f"f2{l}", half_added)
            if stop == f"f2{l}":
                return
        sparse_mixer(Area(base))
        if stop == "sp":
            return
        norm(x, xtok, par("norm_ffn_pre"), hT)
        ffn("f3u", "f3d", "f3", lambda area, name, acts: post_norm(area, name, acts, "f3", T["norm_ffn_post_2"]))

    whole()
    for t in range(NT):
        sp.dma(out[0, t * P:(t + 1) * P, :], x[:, t, :], s_st, xtok[t])
    sp.wait((s_st, s_st.count))

    with nc.Block() as block:
        block.sync(lambda e: sp.play(e))
        block.tensor(lambda e: pe.play(e))
        block.scalar(lambda e: act.play(e))
        block.vector(lambda e: dve.play(e))
        block.gpsimd(lambda e: pool.play(e))
    ctx.close()


def shape_tables():
    p = np.arange(P)[:, None]
    misc = np.zeros((P, NMISC), np.float32)
    f = np.arange(P)[None, :]
    misc[:, 0:128] = p == f
    misc[:, 128:256] = np.where(f < p, 0.0, NEG)
    misc[:, 256:384] = np.where(f <= p, 0.0, NEG)
    inv = (np.float32(500000.0) ** (-np.arange(8, dtype=np.float32) / np.float32(8))).astype(np.float32)
    ang = (np.arange(S, dtype=np.float32)[:, None] * inv[None, :]).astype(np.float32)
    for name, fn in (("cos", np.cos), ("sin", np.sin)):
        o = MISC[name][0]
        misc[:, o:o + 32] = fn(ang.astype(np.float64)).reshape(NT, P, 8).transpose(1, 0, 2).reshape(P, 32)
    d = p + 128 - np.arange(256)[None, :]
    evb = [np.where((d >= 0) & (d <= 127), -(2.0 ** -(h + 1)) * d, NEG) for h in range(8)]
    d = p + 384 - np.arange(512)[None, :]
    c = ((d >= 0) & (d <= 128)).astype(int) + ((d >= 0) & (d % 4 == 0)) + ((d >= 0) & (d % 16 == 0))
    odb = [np.where(c > 0, -np.float64(np.float32(2.0 ** (-8.0 * (h + 1) / 16))) * d
                    + np.log(np.maximum(c, 1)), NEG) for h in range(16)]
    return misc, np.concatenate(evb, 1).astype(np.float32), np.concatenate(odb, 1).astype(np.float32)


_DIRECT = ["x", "mem", "ffn1_w_gu", "ffn1_w_down", "ev_w_in", "ev_w_out", "od_w_in", "od_w_out", "xa_w_q", "xa_w_kv",
           "xa_w_o", "ffn2_w_gu", "ffn2_w_down", "w_in_2", "idx_k_ln_g_2", "idx_k_ln_b_2", "w_rnn_out_2",
           "w_att_out_2", "w_o_2", "norm_mix_post_2", "w_ffn_gate_2", "w_ffn_up_2", "w_ffn_down_2", "norm_ffn_post_2"]


def lay_out(inputs):
    a = {n: np.ascontiguousarray(inputs[n]) for n in _DIRECT}
    for n in ("idx_k_ln_g_2", "idx_k_ln_b_2", "norm_mix_post_2", "norm_ffn_post_2"):
        a[n] = a[n].reshape(-1)
    g = {n: np.asarray(v) for n, v in inputs.items() if n not in _DIRECT}

    def col(v):
        return v.reshape(-1, P).T

    def twice(v):
        return np.concatenate([v, v]).reshape(P, 1)

    parts = []
    for l in range(2):
        parts += [col(g[n][l]) for n in ("ffn1_norm", "mix_norm", "xa_norm", "xa_mem_norm", "ffn2_norm", "xa_q_gain",
                                         "xa_k_gain")]
    parts += [twice(g[n][0]) for n in ("ev_q_gain", "ev_k_gain", "od_q_gain", "od_k_gain")]
    parts.append(np.broadcast_to(g["ev_sinks"][0][None, :], (P, 8)))
    parts += [col(g[n + "_2"][0]) for n in ("norm_mix_pre", "norm_ffn_pre", "conv_b", "rg_b_a", "rg_b_x", "rg_lambda")]
    parts += [col(g["conv_w_2"][0][k]) for k in range(4)]
    a["prm"] = np.ascontiguousarray(np.concatenate(parts, axis=1))
    for n, s in (("wa_l", "rg_w_a_2"), ("wx_l", "rg_w_x_2")):
        w = np.zeros((2, 64, 8, 2, 64), np.float32)
        for u in range(2):
            w[u, :, :, u, :] = g[s][0][u::2].transpose(1, 0, 2)
        a[n] = w.reshape(P, 8, P)
    a["misc"], a["evb"], a["odb"] = shape_tables()
    return a


def kernel(**inputs):
    import concourse.bacc as _bacc
    from concourse.bass_utils import run_bass_kernel_spmd as _run

    nc = _bacc.Bacc("TRN2", target_bir_lowering=False, num_devices=1)
    arrays, T = {}, {}
    for name, a in lay_out(inputs).items():
        arrays[f"in_{name}"] = a
        T[name] = nc.dram_tensor(f"in_{name}", a.shape, mybir.dt.from_np(a.dtype), kind="ExternalInput").ap()
    out = nc.dram_tensor("out_x", (1, S, D), F32, kind="ExternalOutput").ap()
    program(nc, T, out)
    r = _run(nc, [arrays], core_ids=[0])
    return r.results[0]["out_x"]
```

```python
from contextlib import ExitStack

import numpy as np

import concourse.bass as bass
from concourse import mybir

F32 = mybir.dt.float32
F32R = mybir.dt.float32r
ALU = mybir.AluOpType
AF = mybir.ActivationFunctionType
AX = mybir.AxisListType.X

P = 128
S = 512
NT = S // P
D = 1024
KD = D // P
FF = 2816
KF = FF // P
MEM = 256
EPS = 1e-6
NEG = -1.0e30
FLOOR = -3.0e38
TAKEN = -3.3e38
NRAW = 4
NW = 4
AHEAD = 3


class Sem:

    def __init__(self, handle):
        self.handle = handle
        self.count = 0


class Queue:

    def __init__(self, sem):
        self.sem = sem
        self.items = []
        self.met = {}

    def wait(self, *tokens):
        for t in tokens:
            if t is None:
                continue
            if isinstance(t, list):
                self.wait(*t)
                continue
            sem, value = t
            if self.met.get(sem, 0) < value:
                self.met[sem] = value
                self.items.append(lambda e, h=sem.handle, v=value: e.wait_ge(h, v))

    def do(self, fn, *tokens, mark=True):
        self.wait(*tokens)
        if not mark:
            self.items.append(fn)
            return None
        self.sem.count += 1
        self.items.append(lambda e, h=self.sem.handle: fn(e).then_inc(h, 1))
        return (self.sem, self.sem.count)

    def dma(self, out, in_, sem, *tokens):
        self.wait(*tokens)
        sem.count += 16
        self.items.append(lambda e, h=sem.handle: e.dma_start(out, in_).then_inc(h, 16))
        return (sem, sem.count)

    def now(self):
        return (self.sem, self.sem.count) if self.sem.count else None

    def play(self, engine):
        for item in self.items:
            item(engine)


class Bank:
    def __init__(self, ap):
        self.ap = ap
        self.free = []


class Area:

    def __init__(self, at):
        self.at = at

    def take(self, nc, name, shape, dt):
        n = 4 * int(np.prod(shape[1:]))
        t = nc.alloc_sbuf_tensor_at(name, shape, dt, offset=self.at)
        self.at += -(-n // 32) * 32
        return t

    def sub(self, skip=0):
        return Area(self.at + skip)


class Act:

    def __init__(self, hi, lo, n):
        self.hi, self.lo, self.n = hi, lo, n
        self.tok = {}
        self.free = []


def params_layout():
    names = []
    for l in range(2):
        names += [(f"ffn1_norm{l}", 8), (f"mix_norm{l}", 8), (f"xa_norm{l}", 8), (f"xa_mem_norm{l}", 8),
                  (f"ffn2_norm{l}", 8), (f"xa_q_gain{l}", 2), (f"xa_k_gain{l}", 2)]
    names += [("ev_q_gain", 1), ("ev_k_gain", 1), ("od_q_gain", 1), ("od_k_gain", 1), ("ev_sinks", 8),
              ("norm_mix_pre", 8), ("norm_ffn_pre", 8), ("conv_b", 8), ("rg_b_a", 8), ("rg_b_x", 8),
              ("rg_lambda", 8), ("conv_w", 32)]
    at, off = {}, 0
    for n, w in names:
        at[n] = (off, w)
        off += w
    return at, off


PRM, NPRM = params_layout()
MISC = {"ident": (0, 128), "strict": (128, 128), "causal": (256, 128), "cos": (384, 32), "sin": (416, 32)}
NMISC = 448


def program(nc, T, out, stop=None):
    ctx = ExitStack()

    def sb(name, shape, dt=F32, area=None):
        if area is None:
            return ctx.enter_context(nc.sbuf_tensor(name, shape, dt))
        return area.take(nc, name, shape, dt)

    def sem(name):
        return Sem(ctx.enter_context(nc.semaphore(name)))

    pe, act, dve, pool, sp = (Queue(sem("s_" + n)) for n in ("pe", "act", "dve", "pool", "sp"))
    s_st = sem("s_st")
    s_cst = sem("s_cst")
    banks = [Bank(ctx.enter_context(nc.psum_tensor(f"ps{i}", [P, 512], F32))) for i in range(8)]

    x = sb("x", [P, NT, D])
    hTh = sb("hTh", [P, KD, S], F32R)
    hTl = sb("hTl", [P, KD, S], F32R)
    hT = Act(hTh, hTl, S)
    raw = [sb(f"raw{i}", [P, 2, 512]) for i in range(NRAW)]
    wh = [sb(f"wh{i}", [P, 2, 512], F32R) for i in range(NW)]
    wl = [sb(f"wl{i}", [P, 2, 512], F32R) for i in range(NW)]
    s_raw = [sem(f"s_raw{i}") for i in range(NRAW)]
    xn = [sb(f"xn{i}", [P, D]) for i in range(2)]
    xn_free = [[], []]
    prm = sb("prm", [P, NPRM])
    misc = sb("misc", [P, NMISC])
    half = sb("half", [P, 64])
    stat = sb("stat", [P, 16])
    coef = sb("coef", [P, 8])
    la = sb("la", [P, 5, 8])
    ident = misc[:, 0:128]
    base = -(-nc.sbuf_base // 64) * 64

    def par(name):
        o, w = PRM[name]
        return prm[:, o:o + w]

    def mis(name):
        o, w = MISC[name]
        return misc[:, o:o + w]

    s_x = [sem(f"s_x{t}") for t in range(NT)]
    xtok = [[sp.dma(x[:, t, :], T["x"][0, t * P:(t + 1) * P, :], s_x[t])] for t in range(2)]
    t_cst = [sp.dma(prm[:, :], T["prm"], s_cst), sp.dma(misc[:, :], T["misc"], s_cst)][-1]
    xtok += [[sp.dma(x[:, t, :], T["x"][0, t * P:(t + 1) * P, :], s_x[t])] for t in range(2, NT)]
    t_half = pool.do(lambda e: e.memset(half[:, :], -0.5))

    def gate_up(name, wg, wu, a="h"):
        return (name, KD, [[(wg, c, 256, a, "A"), (wu, c, 256, a, "A")] for c in range(0, FF, 256)])

    def rows(name, w, K, widths, a="h", form="B", c0=0):
        groups = []
        for n in widths:
            groups.append([(w, c0, n, a, form)])
            c0 += n
        return (name, K, groups)

    GEMMS = []
    for l in range(2):
        wgu, wd = T["ffn1_w_gu"][l], T["ffn1_w_down"][l]
        GEMMS.append(gate_up(f"f1u{l}", wgu[:, 0:FF], wgu[:, FF:2 * FF]))
        GEMMS.append(rows(f"f1d{l}", wd, KF, [512, 512], "f"))
        if l == 0:
            w = T["ev_w_in"][0]
            GEMMS.append((f"in{l}", KD, [[(w, 0, 512, "h", "B")], [(w, 512, 256, "h", "B")], [(w, 1792, 512, "h", "B")],
                                         [(w, 768, 512, "h", "A")], [(w, 1280, 512, "h", "A")]]))
            GEMMS.append(rows(f"out{l}", T["ev_w_out"][0], KD, [512, 512]))
        else:
            w = T["od_w_in"][0]
            GEMMS.append(rows(f"in{l}", w, KD, [512] * 6))
            GEMMS.append(rows(f"out{l}", T["od_w_out"][0], KD, [512, 512]))
        GEMMS.append((f"kv{l}", KD, [[(T["xa_w_kv"][l], c, 512, "m", "B")] for c in (1024, 1536, 0, 512)]))
        GEMMS.append(rows(f"xq{l}", T["xa_w_q"][l], KD, [512] * 2))
        GEMMS.append(rows(f"xo{l}", T["xa_w_o"][l], KD, [512] * 2))
        wgu, wd = T["ffn2_w_gu"][l], T["ffn2_w_down"][l]
        GEMMS.append(gate_up(f"f2u{l}", wgu[:, 0:FF], wgu[:, FF:2 * FF]))
        GEMMS.append(rows(f"f2d{l}", wd, KF, [512, 512], "f"))
    w = T["w_in_2"][0]
    GEMMS.append(("idx", KD, [[(w, 3584, 512, "h", "B")], [(w, 4096, 72, "h", "B")]]))
    GEMMS.append(rows("qkv", w, KD, [512] * 3, c0=2048))
    GEMMS.append(("rnn", KD, [[(w, c, 256, "h", "A"), (w, 1024 + c, 256, "h", "A")] for c in range(0, 1024, 256)]))
    GEMMS.append(("ya", KD, [[seg] for c in range(0, 1024, 512)
                             for seg in ((w, 4168 + c, 512, "h", "A"), (T["w_rnn_out_2"][0], c, 512, "y", "A"))]))
    GEMMS.append(rows("gb", w, KD, [512] * 2, form="A", c0=5192))
    GEMMS.append(rows("yb", T["w_att_out_2"][0], KD, [512] * 2, form="A"))
    GEMMS.append(rows("wo", T["w_o_2"][0], KD, [512] * 2, "y"))
    GEMMS.append(gate_up("f3u", T["w_ffn_gate_2"][0], T["w_ffn_up_2"][0]))
    GEMMS.append(rows("f3d", T["w_ffn_down_2"][0], KF, [512, 512], "f"))

    stream = [(segs, kp) for _, K, groups in GEMMS for segs in groups for kp in range(K // 2)]
    first = {}
    n = 0
    for name, K, groups in GEMMS:
        first[name] = n
        n += len(groups) * K // 2
    spec = {g[0]: g for g in GEMMS}
    t_raw, t_hi, t_lo, t_used = {}, {}, {}, {}
    done = {"load": 0, "split": 0}

    def load(n):
        if n >= len(stream):
            return
        segs, kp = stream[n]
        r = n % NRAW
        old = n - NRAW
        o = 0
        for w, c, width, _, _ in segs:
            t_raw[n] = sp.dma(raw[r][:, :, o:o + width],
                              w[kp * 256:(kp + 1) * 256, c:c + width].rearrange("(c p) n -> p c n", p=P),
                              s_raw[r], t_hi.get(old), t_lo.get(old))
            o += width

    def split(n):
        if n >= len(stream):
            return
        W = sum(s[2] for s in stream[n][0])
        r, i = n % NRAW, n % NW
        src, hi, lo = raw[r][:, :, 0:W], wh[i][:, :, 0:W], wl[i][:, :, 0:W]
        t_hi[n] = act.do(lambda e: e.activation(hi, src, AF.Copy), t_raw[n], t_used.get(n - NW))
        t_lo[n] = dve.do(lambda e: e.tensor_tensor(lo, src, hi.bitcast(F32), ALU.subtract),
                         t_raw[n], t_hi[n], t_used.get(n - NW))

    def advance(n):
        while done["split"] <= n + AHEAD:
            while done["load"] < done["split"] + NRAW:
                load(done["load"])
                done["load"] += 1
            split(done["split"])
            done["split"] += 1

    later = []
    background = []
    urgent = []
    side = [0]

    def flush():
        while later:
            later.pop(0)()

    def drain():
        while urgent:
            urgent.pop(0)()
        flush()

    def take_half():
        side[0] ^= 1
        return banks[4 * side[0]:4 * side[0] + 4]

    def gemm(name, acts, on_group, background_per_chunk=0):
        _, K, groups = spec[name]
        n = first[name]
        for g, segs in enumerate(groups):
            bk = take_half()
            jobs, o, b = [], 0, 0
            for _, _, width, a, form in segs:
                A = acts[a]
                if form == "A":
                    for j in range(width // P):
                        jobs.append((bk[b], A, "A", slice(o + j * P, o + (j + 1) * P), slice(0, A.n)))
                        b += 1
                else:
                    for t in range(A.n // P):
                        jobs.append((bk[b], A, "B", slice(o, o + width), slice(t * P, (t + 1) * P)))
                        b += 1
                o += width
            toks = []
            blocks = [[kp] for kp in range(K // 2)]
            if g == len(groups) - 1:
                blocks[-2:] = [[K // 2 - 2, K // 2 - 1]]
            for block in blocks:
                advance(n)
                for u in range(len(block)):
                    pe.wait(t_hi[n + u], t_lo[n + u])
                ks = [(2 * kp + kk, n + kp - block[0], kk) for kp in block for kk in range(2)]
                order = [(k, job) for k in ks for job in jobs] if len(block) == 1 else \
                        [(k, job) for job in jobs for k in ks]
                for (k, m, kk), (bank, A, form, wc, tc) in order:
                    i = m % NW
                    pe.wait(A.tok[k])
                    if k == 0:
                        pe.wait(bank.free)
                    Wh, Wl = wh[i][:, kk, wc], wl[i][:, kk, wc]
                    Ah, Al = A.hi[:, k, tc], A.lo[:, k, tc]
                    for q, (p0, p1) in enumerate(((Wh, Ah), (Wh, Al), (Wl, Ah)) if form == "A" else
                                                 ((Ah, Wh), (Ah, Wl), (Al, Wh))):
                        M = (wc.stop - wc.start) if form == "B" else A.n
                        end = k == K - 1 and q == 2
                        t = pe.do(lambda e, o_=bank.ap[:, 0:M], l_=p0, r_=p1, s_=(k == 0 and q == 0), e_=end:
                                  e.matmul(o_, l_, r_, start=s_, stop=e_),
                                  mark=end or (q == 2 and kk == 1 and bank is jobs[-1][0]))
                        if end:
                            toks.append(t)
                    t_used[m] = t
                for _ in block:
                    if urgent:
                        urgent.pop(0)()
                    for _ in range(background_per_chunk):
                        if background:
                            background.pop(0)()
                n += len(block)
            for job in jobs:
                job[1].free = [t_used[n - 1]]
            flush()
            on_group(g, [j[0] for j in jobs], toks)

    def rstd(src, dst, scale, *tokens):
        t = pool.do(lambda e: e.tensor_scalar(dst, src, scale, EPS, ALU.mult, ALU.add), *tokens)
        w = dst.shape[1]
        return pool.do(lambda e: e.tensor_tensor(dst, dst, half[:, 0:w], ALU.pow), t, t_half)

    def halves(src, A, k, cols, tokens, scale=None):
        hi, lo = A.hi[:, k, cols], A.lo[:, k, cols]
        if scale is None:
            t = act.do(lambda e: e.activation(hi, src, AF.Copy), tokens, A.free)
            t2 = dve.do(lambda e: e.tensor_tensor(lo, src, hi.bitcast(F32), ALU.subtract), t, tokens, A.free)
        else:
            t = act.do(lambda e: e.activation(hi, src, AF.Copy, scale=scale), tokens, A.free)
            t2 = dve.do(lambda e: e.scalar_tensor_tensor(lo, src, scale, hi.bitcast(F32), ALU.mult, ALU.subtract),
                        t, tokens, A.free)
        A.tok[k] = [t, t2]
        return t2

    def norm_steps(gain, A, junk=None, before=None):
        rate, last, squares = {}, {}, []

        scaled, turned = {}, []

        def scale(t):
            if t >= 2 and t - 2 not in turned:
                turn_tile(t - 2)
            buf = xn[t % 2]
            scaled[t] = dve.do(lambda e: e.tensor_scalar(buf[:, :], x[:, t, :], stat[:, 8 + t:9 + t], None, ALU.mult),
                               rate[t], xtok[t], xn_free[t % 2])

        def turn_tile(t):
            turned.append(t)
            buf = xn[t % 2]
            for c in order:
                if t == 0:
                    pe.wait(banks[c].free)
                last[c] = pe.do(lambda e, c=c: e.transpose(
                    banks[c].ap[:, t * P:(t + 1) * P], buf[:, c * P:(c + 1) * P], ident), scaled[t], t_cst,
                    mark=t == NT - 1 or c == order[-1])
            xn_free[t % 2] = [last[order[-1]]]

        order = []

        def tile(t):
            if t == 0:
                order.extend([4 * (1 - side[0]) + i for i in range(4)] + [4 * side[0] + i for i in range(4)])
            dst = xn[t % 2] if junk is None else junk
            if junk is None and t >= 1:
                scale(t - 1)
                if t >= 2:
                    turn_tile(t - 2)
            t1 = act.do(lambda e: e.activation(dst[:, :], x[:, t, :], AF.Square, accum_out=stat[:, t:t + 1]), xtok[t],
                        xn_free[t % 2] if junk is None else squares, stat_free)
            squares[:] = [t1]
            rate[t] = [t1, rstd(stat[:, t:t + 1], stat[:, 8 + t:9 + t], 1.0 / D, t1, stat_free)]
            if junk is not None and t >= 1:
                scale(t - 1)

        def finish():
            scale(NT - 1)
            turn_tile(NT - 2)
            turn_tile(NT - 1)
            stat_free[:] = [scaled[NT - 1]]
            if before is not None:
                before()
            for c in range(KD):
                banks[c].free = [halves(banks[c].ap[:, 0:A.n], A, c, slice(0, A.n), last[c], gain[:, c:c + 1])]

        return tile, finish

    def norm(gain, A, before=None):
        tile, finish = norm_steps(gain, A, None, before)
        for t in range(NT):
            tile(t)
        finish()

    stat_free = []

    def pair_rates(p, src, buf, junk, toks, c0):
        got = []
        for t in (2 * p, 2 * p + 1):
            b, r0, r1 = buf(t), stat[:, c0 + t:c0 + t + 1], stat[:, 8 + c0 + t:9 + c0 + t]
            t1 = act.do(lambda e, t=t, r0=r0: e.activation(junk(t), src(t), AF.Square, accum_out=r0), toks[t],
                        xn_free[t % 2], stat_free)
            t2 = rstd(r0, r1, 1.0 / D, t1, stat_free)
            got.append(dve.do(lambda e, t=t, b=b, r1=r1: e.tensor_scalar(b, src(t), r1, None, ALU.mult), t1, t2,
                              toks[t]))
        return got

    def pair_turn(p, buf, got, gain, A, four):
        cols = slice(256 * p, 256 * p + 256)
        for j in range(4):
            bank = four[j]
            pe.wait(bank.free)
            for u in range(2):
                c = 2 * j + u
                for i, t in enumerate((2 * p, 2 * p + 1)):
                    tk = pe.do(lambda e, c=c, u=u, i=i, t=t, bank=bank: e.transpose(
                        bank.ap[:, 256 * u + i * P:256 * u + (i + 1) * P], buf(t)[:, c * P:(c + 1) * P], ident),
                        got[i], t_cst, mark=u == 1 and i == 1)
            his = [act.do(lambda e, u=u, c=2 * j + u, bank=bank: e.activation(
                A.hi[:, c, cols], bank.ap[:, 256 * u:256 * u + 256], AF.Copy, scale=gain[:, c:c + 1]), tk, A.free)
                for u in range(2)]
            for u in range(2):
                c = 2 * j + u
                lo = dve.do(lambda e, u=u, c=c, bank=bank: e.scalar_tensor_tensor(
                    A.lo[:, c, cols], bank.ap[:, 256 * u:256 * u + 256], gain[:, c:c + 1],
                    A.hi[:, c, cols].bitcast(F32), ALU.mult, ALU.subtract), his, A.free)
                A.tok[c] = (A.tok[c] if p else []) + his + [lo]
            bank.free = [lo]
        for t in (0, 1):
            xn_free[t] = [tk]
        stat_free[:] = got

    def add_to_x(scale, then=None):
        def on_group(g, bk, toks):
            for t in range(NT):
                xs = x[:, t, g * 512:(g + 1) * 512]
                tk = dve.do(lambda e, xs=xs, b=bk[t]: e.scalar_tensor_tensor(xs, b.ap[:, :], scale, xs, ALU.mult,
                                                                             ALU.add), toks[t], xtok[t])
                bk[t].free = [tk]
                xtok[t] = [tk]
                if g == 1 and then is not None:
                    then[0](t)
            if g == 1 and then is not None:
                then[1]()
        return on_group

    def handover():
        toks = [q.now() for q in (pe, act, dve, pool)]
        for q in (act, dve, pool):
            q.wait(*toks)

    def copy_out(engine, dst, src, *tokens):
        if engine is act:
            return act.do(lambda e: e.activation(dst, src, AF.Copy), *tokens)
        return engine.do(lambda e: e.tensor_copy(dst, src), *tokens)

    def head_rates(tmp, nt, nh, hd, width, ss, bk, toks, free):
        got = []
        for t in range(nt):
            sq = xn[t % 2][:, 0:nh * hd]
            e1 = copy_out(act, tmp[:, t, 0:width], bk[t].ap[:, 0:width], toks[t], free)
            e2 = act.do(lambda e, t=t, sq=sq: e.activation(sq, bk[t].ap[:, 0:nh * hd], AF.Square), toks[t],
                        xn_free[t % 2])
            bk[t].free = [e2]
            r = ss[:, t, 0:nh]
            t2 = dve.do(lambda e, r=r, sq=sq: e.tensor_reduce(r, sq.rearrange("p (h d) -> p h d", h=nh), AX, ALU.add),
                        e2)
            xn_free[t % 2] = [t2]
            got.append([e1, rstd(r, r, 1.0 / hd, t2)])
        return got

    def head_scale(tmp, got, nh, hd, ss, dst=None):
        tt = []
        for t, tok_ in enumerate(got):
            v = tmp[:, t, 0:nh * hd].rearrange("p (h d) -> p h d", h=nh)
            r = ss[:, t, 0:nh].unsqueeze(2).to_broadcast([P, nh, hd])
            for o in [v] if dst is None else dst(t):
                tk = dve.do(lambda e, o=o, v=v, r=r: e.tensor_tensor(o, v, r, ALU.mult), tok_)
            tt.append(tk)
        return tt

    def turn(tmp, tt, blocks, bk, dsts, gains, nt, last_use):
        toks = []
        for c in range(blocks):
            bank = bk[c]
            pe.wait(bank.free)
            for t in range(nt):
                tk = pe.do(lambda e, c=c, t=t, bank=bank: e.transpose(bank.ap[:, t * P:(t + 1) * P],
                                                                      tmp[:, t, c * P:(c + 1) * P], ident),
                           tt[t], mark=t == nt - 1)
            last_use.append(tk)
            if gains is None:
                q = act if c % 2 else dve
                r = copy_out(q, dsts[c], bank.ap[:, 0:nt * P], tk)
            elif c % 2:
                r = act.do(lambda e, c=c, bank=bank: e.activation(dsts[c], bank.ap[:, 0:nt * P], AF.Copy,
                                                                  scale=gains[c]), tk)
            else:
                r = dve.do(lambda e, c=c, bank=bank: e.tensor_scalar(dsts[c], bank.ap[:, 0:nt * P], gains[c], None,
                                                                     ALU.mult), tk)
            bank.free = [r]
            toks.append(r)
        return toks

    def widths(lo, n):
        out_, o = [], 0
        for i in range(n):
            k0, k1 = lo(i)
            out_.append((k0, k1, o, (k1 - k0) * P))
            o += (k1 - k0) * P
        return out_, o

    def attend(st, tag, H, tiles, score, value, O, mode="softmax", bias=None, sink=None, scale=1.0, nk=NT,
               before=None, st2=None):
        spans, total = tiles
        Pb = [sb(f"{tag}P{i}", [P, total], F32, st) for i in range(2)]
        PT = [sb(f"{tag}PT{i}", [P, nk, S], F32, st2 or st) for i in range(2)]
        sm = [sb(f"{tag}sm{i}", [P, 24], F32, st) for i in range(2)]
        stick = mode == "stick"
        Qb = [sb(f"{tag}Q{i}", [P, total + NT], F32, st) for i in range(2)] if stick else None
        Zr = sb(f"{tag}Z", [P, 512], F32, st) if stick else None
        causal = total == 10 * P
        sgroups = [[0, 1], [2], [3]] if causal else [[0, 1], [2, 3]]
        groups = [[3], [2, 0], [1]] if causal else [[0, 1], [2, 3]]
        tbank = 6 - len(groups)
        places = [{}, {}]
        for b in range(2):
            for n, group in enumerate(sgroups):
                at = 0
                for i in group:
                    places[b][i] = banks[n if causal else 2 * b + n].ap[:, at:at + spans[i][3]]
                    at += spans[i][3]
        P_free, PT_free = [[], []], [[], []]
        ready, turned = {}, {}
        t_one = None
        if stick:
            t_one = [pool.do(lambda e: e.memset(Zr[:, :], 0.0))]
            t_one += [pool.do(lambda e, b=b: e.memset(Qb[b][:, :], 1.0)) for b in range(2)]

        def first_half(h):
            b = h % 2
            p, m, place = Pb[b], sm[b], places[b]
            mx, nm, den, es, rd = (m[:, 4 * i:4 * i + 4] for i in range(5))
            got = [None] * NT
            for n, group in enumerate(sgroups):
                bank = banks[n if causal else 2 * b + n]
                pe.wait(bank.free)
                for i in group:
                    k0, k1, o, W = spans[i]
                    tk = score(h, i, place[i], k0, k1)
                if stick:
                    for i in group:
                        dg = place[i][:, spans[i][3] - P:spans[i][3]]
                        t0 = dve.do(lambda e, dg=dg: e.tensor_tensor(dg, dg, mis("strict"), ALU.add), tk, t_cst)
                for i in group:
                    k0, k1, o, W = spans[i]
                    pw, src = p[:, o:o + W], place[i]
                    if stick:
                        kp_ = Qb[b][:, o + i:o + i + W]
                        t1 = act.do(lambda e, pw=pw, src=src: e.activation(pw, src, AF.Sigmoid), t0, P_free[b], t_one)
                        t2 = act.do(lambda e, kp_=kp_, src=src: e.activation(kp_, src, AF.Sigmoid, scale=-1.0),
                                    P_free[b], t_one)
                        got[i] = (t1, t2)
                    elif bias is not None:
                        bt, btok = bias(h, i, W)
                        t2 = got[i] = dve.do(lambda e, pw=pw, src=src, bt=bt, i=i: e.tensor_tensor_reduce(
                            pw, src, bt, 1.0, FLOOR, ALU.add, ALU.max, mx[:, i:i + 1]), tk, btok, P_free[b])
                    else:
                        t2 = got[i] = dve.do(lambda e, src=src, i=i: e.tensor_reduce(mx[:, i:i + 1], src, AX, ALU.max),
                                             tk, P_free[b])
                bank.free = [t2]
            if stick:
                ready[h] = got
                return
            if sink is not None:
                t2 = dve.do(lambda e: e.tensor_scalar(nm, mx, sink[:, h:h + 1], -1.0, ALU.max, ALU.mult), got)
            else:
                t2 = dve.do(lambda e: e.tensor_scalar(nm, mx, -scale, None, ALU.mult), got)
            ready[h] = t2

        def exps(h):
            b = h % 2
            p, m, place = Pb[b], sm[b], places[b]
            nm, den, es = (m[:, 4 * i:4 * i + 4] for i in range(1, 4))
            t2 = ready[h]
            for i, (k0, k1, o, W) in enumerate(spans):
                pw = p[:, o:o + W]
                src = pw if bias is not None else place[i]
                t3 = act.do(lambda e, pw=pw, src=src, i=i: e.activation(pw, src, AF.Exp, bias=nm[:, i:i + 1],
                                                                        scale=scale, accum_out=den[:, i:i + 1]),
                            t2, P_free[b])
                if bias is None:
                    banks[2 * b + i // 2].free = [t3]
            if sink is not None:
                t3 = act.do(lambda e: e.activation(es, nm, AF.Exp, bias=sink[:, h:h + 1]), t2)
            ready[h] = t3

        def second_half(h):
            b = h % 2
            p, m, place = Pb[b], sm[b], places[b]
            den, es, rd = (m[:, 4 * i:4 * i + 4] for i in range(2, 5))
            toks = []
            if stick:
                for i, (k0, k1, o, W) in enumerate(spans):
                    q = Qb[b][:, o + i:o + i + W + 1]
                    t1, t2 = ready[h][i]
                    rev = Qb[b][:, o + i:o + i + W][:, ::-1]
                    t3 = dve.do(lambda e, rev=rev, W=W: e.tensor_tensor_scan(rev, rev, Zr[:, 0:W], 1.0, ALU.mult,
                                                                             ALU.add), t1, t2, t_one)
                    pw = p[:, o:o + W]
                    toks.append(dve.do(lambda e, pw=pw, q=q, W=W: e.tensor_tensor(pw, pw, q[:, 1:W + 1], ALU.mult), t3))
                ready[h] = toks
                return
            t = ready[h]
            if sink is not None:
                t = dve.do(lambda e: e.tensor_tensor(den, den, es, ALU.add), t)
            t = dve.do(lambda e: e.reciprocal(rd, den), t)
            for i, (k0, k1, o, W) in enumerate(spans):
                pw = p[:, o:o + W]
                toks.append(dve.do(lambda e, pw=pw, i=i: e.tensor_scalar(pw, pw, rd[:, i:i + 1], None, ALU.mult), t))
            ready[h] = toks

        def turn_head(h):
            b = h % 2
            cp = []
            for n, group in enumerate(groups):
                bank = banks[tbank + n]
                pe.wait(bank.free)
                at = 0
                for i in group:
                    k0, k1, o, W = spans[i]
                    for j in range(k1 - k0):
                        tk = pe.do(lambda e, j=j, o=o, at=at, bank=bank: e.transpose(
                            bank.ap[:, at + j * P:at + (j + 1) * P], Pb[b][:, o + j * P:o + (j + 1) * P], ident),
                            ready[h][i], mark=i == group[-1] and j == k1 - k0 - 1)
                    at += W
                at = 0
                for i in group:
                    k0, k1, o, W = spans[i]
                    t = copy_out(dve if stick or n % 2 else act, PT[b][:, k0:k1, i * P:(i + 1) * P],
                                 bank.ap[:, at:at + W].rearrange("p (k q) -> p k q", k=k1 - k0), tk, PT_free[b])
                    at += W
                bank.free = [t]
                cp.append(t)
            P_free[b] = [tk]
            turned[h] = cp

        def product(h):
            b = h % 2
            pe.wait(turned[h])
            t, finish = value(h, PT[b])
            PT_free[b] = [t]
            return finish

        finish = None
        for s in range(H + 3):
            if 1 <= s <= H and (causal or bias is None):
                second_half(s - 1)
            if s < H:
                if before is not None:
                    before(s)
                first_half(s)
            if 1 <= s <= H and not (causal or bias is None):
                second_half(s - 1)
            if finish is not None:
                finish()
                finish = None
            if s < H and not stick:
                exps(s)
            if 2 <= s < H + 2 and bias is not None:
                finish = product(s - 2)
            if 1 <= s <= H:
                turn_head(s - 1)
            if 2 <= s < H + 2 and bias is None:
                finish = product(s - 2)

    def causal_scores(qT, kT, qtok, ktok, kv_of, dup):
        def score(h, i, dst, k0, k1):
            r = slice(64 * (h % 2), 64 * (h % 2) + 64)
            kb = kv_of(h) if dup else h // 2
            return pe.do(lambda e: e.matmul(dst, qT[r, h // 2, i * P:(i + 1) * P], kT[r, kb, k0 * P:k1 * P],
                                            start=True, stop=True), qtok[h // 2], ktok[kb])
        return score

    def pair_values(V, O, base, spans, causal, vtok):
        def value(h, PTb):
            pair = h // 2
            bank = banks[6 + pair % 2]
            if h % 2 == 0:
                pe.wait(bank.free)
            pe.wait(vtok)
            r = slice(64 * (h % 2), 64 * (h % 2) + 64)
            if causal:
                for kt in range(NT):
                    t = pe.do(lambda e, kt=kt: e.matmul(bank.ap[r, kt * P:S], V(h, kt), PTb[:, kt, kt * P:S],
                                                        start=kt == 0, stop=kt == NT - 1), mark=kt == NT - 1)
            else:
                for i, (k0, k1, o, W) in enumerate(spans):
                    for kt in range(k0, k1):
                        t = pe.do(lambda e, kt=kt, i=i, k0=k0, k1=k1: e.matmul(
                            bank.ap[r, i * P:(i + 1) * P], V(h, kt), PTb[:, kt, i * P:(i + 1) * P],
                            start=kt == k0, stop=kt == k1 - 1), mark=i == NT - 1 and kt == k1 - 1)

            def finish():
                bank.free = [halves(bank.ap[:, :], O, base + pair, slice(0, S), t)]
            return t, finish if h % 2 else None
        return value

    causal_tiles = widths(lambda i: (0, i + 1), NT)

    t_coef = []
    ncoef = la[:, 0, :]

    def recurrence_rates():
        lam = par("rg_lambda")
        t = pool.do(lambda e: e.tensor_scalar(la[:, 1, :], lam, -1.0, None, ALU.mult), t_cst)
        t = dve.do(lambda e: e.tensor_tensor(la[:, 0, :], la[:, 1, :], lam, ALU.max), t)
        t_e = act.do(lambda e: e.activation(la[:, 0, :], la[:, 0, :], AF.Exp, scale=-1.0), t)
        t = pool.do(lambda e: e.tensor_scalar(la[:, 2, :], la[:, 0, :], 2.0, None, ALU.add), t_e)
        t = dve.do(lambda e: e.reciprocal(la[:, 2, :], la[:, 2, :]), t)
        t = pool.do(lambda e: e.tensor_tensor(la[:, 2, :], la[:, 2, :], la[:, 0, :], ALU.mult), t)
        t = pool.do(lambda e: e.tensor_tensor(la[:, 3, :], la[:, 2, :], la[:, 2, :], ALU.mult), t)
        t = pool.do(lambda e: e.memset(la[:, 4, :], 1.0 / 19))
        for n in range(17, 0, -2):
            t = pool.do(lambda e: e.tensor_tensor(la[:, 4, :], la[:, 4, :], la[:, 3, :], ALU.mult), pool.now())
            t = pool.do(lambda e, n=n: e.tensor_scalar(la[:, 4, :], la[:, 4, :], 1.0 / n, None, ALU.add), t)
        t = pool.do(lambda e: e.tensor_tensor(la[:, 4, :], la[:, 4, :], la[:, 2, :], ALU.mult), t)
        t = pool.do(lambda e: e.tensor_scalar(la[:, 4, :], la[:, 4, :], 16.0, None, ALU.mult), t)
        t = pool.do(lambda e: e.tensor_scalar(la[:, 1, :], la[:, 1, :], 0.0, 8.0, ALU.max, ALU.mult), t)
        t = pool.do(lambda e: e.tensor_tensor(coef[:, :], la[:, 4, :], la[:, 1, :], ALU.add), t)
        t_coef.append(pool.do(lambda e: e.tensor_scalar(la[:, 0, :], coef[:, :], -1.0, None, ALU.mult), t))

    def even_mixer(st):
        handover()
        s_b = sem("s_evb")
        evb = sb("evb", [P, 8 * 256], F32, st)
        t_evb = pool.dma(evb[:, :], T["evb"], s_b)
        qs = sb("e_qs", [P, 1], F32, st)
        ta = sb("e_ta", [P, NT, 512], F32, st)
        tk_ = sb("e_tk", [P, NT, 256], F32, st)
        kd = sb("e_kd", [P, NT, 256], F32, st)
        vb = sb("e_vb", [P, NT, 512], F32, st)
        ss = sb("e_ss", [P, NT, 8], F32, st)
        sk = sb("e_sk", [P, NT, 2], F32, st)
        qaT = sb("e_qaT", [P, 4, S], F32, st)
        kaT = sb("e_kaT", [P, 2, S], F32, st)
        qbT = sb("e_qbT", [P, 4, S], F32, st)
        kbT = sb("e_kbT", [P, 4, S], F32, st)
        t_qs = dve.do(lambda e: e.tensor_scalar(qs[:, :], par("ev_q_gain"), 0.125, None, ALU.mult), t_cst)
        tok = {"q": [], "k": [], "vb": [], "qb": [], "kb": []}

        def on_group(g, bk, toks):
            if g == 0:
                got = head_rates(ta, NT, 8, 64, 512, ss, bk, toks, [])
                tt = []
                dve.wait(t_qs)
                act.wait(t_qs)
                urgent.append(lambda: tt.extend(head_scale(ta, got, 8, 64, ss)))
                urgent.append(lambda: tok["q"].extend(
                    turn(ta, tt, 4, bk, [qaT[:, c, :] for c in range(4)], [qs[:, :]] * 4, NT, [])))
            elif g == 1:
                got = head_rates(tk_, NT, 2, 64, 256, sk, bk, toks, [])
                tt = []

                def twice(t):
                    kdv = kd[:, t, :].rearrange("p (h u d) -> p h u d", h=2, u=2)
                    return [kdv[:, :, u, :] for u in range(2)]

                urgent.append(lambda: tt.extend(head_scale(tk_, got, 2, 64, sk, twice)))
                urgent.append(lambda: tok["k"].extend(
                    turn(kd, tt, 2, bk, [kaT[:, c, :] for c in range(2)], [par("ev_k_gain")] * 2, NT, [])))
            elif g == 2:
                for t in range(NT):
                    e1 = copy_out(act if t % 2 else dve, vb[:, t, :], bk[t].ap[:, :], toks[t])
                    bk[t].free = [e1]
                    tok["vb"].append(e1)
            else:
                for c in range(4):
                    if g == 3:
                        e1 = act.do(lambda e, c=c: e.activation(qbT[:, c, :], bk[c].ap[:, :], AF.Copy, scale=0.125),
                                    toks[c])
                    else:
                        e1 = copy_out(dve, kbT[:, c, :], bk[c].ap[:, :], toks[c])
                    bk[c].free = [e1]
                    tok["qb" if g == 3 else "kb"].append(e1)

        gemm("in0", {"h": hT}, on_group)
        drain()
        band = widths(lambda i: (max(i - 1, 0), i + 1), NT)
        attend(st.sub(), "ea", 8, band, causal_scores(qaT, kaT, tok["q"], tok["k"], lambda h: h // 4, True),
                   pair_values(lambda h, kt: tk_[:, kt, 128 + 64 * (h // 4):192 + 64 * (h // 4)], hT, 0, band[0], False, None),
                   hT, bias=lambda h, i, W: (evb[:, 256 * (h + 1) - W:256 * (h + 1)], [t_evb]), sink=par("ev_sinks"))
        handover()
        attend(st.sub(), "eb", 8, causal_tiles, causal_scores(qbT, kbT, tok["qb"], tok["kb"], None, False),
                   pair_values(lambda h, kt: vb[:, kt, 64 * h:64 * h + 64], hT, 4, None, True, tok["vb"]),
                   hT, mode="stick")

    def odd_mixer(st):
        handover()
        qs = sb("o_qs", [P, 1], F32, st)
        tmp = [sb(f"o_t{i}", [P, NT, 512], F32, st) for i in range(2)]
        tmp_free = [[], []]
        v = sb("o_v", [P, NT, D], F32, st)
        ss = [sb(f"o_ss{i}", [P, NT, 8], F32, st) for i in range(2)]
        qT = sb("o_qT", [P, 8, S], F32, st)
        kT = sb("o_kT", [P, 8, S], F32, st)
        t_qs = dve.do(lambda e: e.tensor_scalar(qs[:, :], par("od_q_gain"), 0.125, None, ALU.mult), t_cst)
        act.wait(t_qs)
        dve.wait(t_qs)
        tok = {"q": [], "k": [], "v": []}

        def on_group(g, bk, toks):
            if g < 4:
                b = g % 2
                got = head_rates(tmp[b], NT, 8, 64, 512, ss[b], bk, toks, tmp_free[b])
                tt = []
                dst = qT if g < 2 else kT
                gain = qs[:, :] if g < 2 else par("od_k_gain")

                def go():
                    used = []
                    tok["q" if g < 2 else "k"].extend(
                        turn(tmp[b], tt, 4, bk, [dst[:, 4 * (g % 2) + c, :] for c in range(4)], [gain] * 4, NT, used))
                    tmp_free[b] = used

                urgent.append(lambda: tt.extend(head_scale(tmp[b], got, 8, 64, ss[b])))
                urgent.append(go)
            else:
                for t in range(NT):
                    e1 = copy_out(act if t % 2 else dve, v[:, t, 512 * (g - 4):512 * (g - 3)], bk[t].ap[:, :], toks[t])
                    bk[t].free = [e1]
                    tok["v"].append(e1)

        gemm("in1", {"h": hT}, on_group)
        drain()
        ob = [tmp[0][:, i, :] for i in range(4)]
        s_ob = [sem(f"s_ob{i}") for i in range(4)]
        t_ob, ob_free = {}, [tmp_free[0]] * 4

        def fetch(h):
            if h < 16:
                t_ob[h] = pool.dma(ob[h % 4], T["odb"][:, 512 * h:512 * (h + 1)], s_ob[h % 4], ob_free[h % 4])

        for h in range(3):
            fetch(h)

        def before(h):
            if h >= 1:
                ob_free[(h - 1) % 4] = [dve.now()]
            fetch(h + 3)

        attend(st.sub(), "oc", 16, causal_tiles, causal_scores(qT, kT, tok["q"], tok["k"], None, False),
                   pair_values(lambda h, kt: v[:, kt, 64 * h:64 * h + 64], hT, 0, None, True, tok["v"]),
                   hT, bias=lambda h, i, W: (ob[h % 4][:, 512 - W:512], [t_ob[h]]), before=before)

    def cross_memory(st, l):
        handover()
        s_m = [sem(f"s_mem{l}{t}") for t in range(2)]
        M = Act(sb(f"c{l}mh", [P, KD, MEM], F32R, st), sb(f"c{l}ml", [P, KD, MEM], F32R, st), MEM)
        junk = sb(f"c{l}j", [P, 2, D], F32, st.sub())
        t_m = [pool.dma(xn[t][:, :], T["mem"][0][t * P:(t + 1) * P, :], s_m[t], xn_free[t]) for t in range(2)]
        got = []
        tile = lambda t: xn[t][:, :]

        def turn_():
            at = 4 * (1 - side[0])
            pair_turn(0, tile, got, par(f"xa_mem_norm{l}"), M, banks[at:at + 4])

        urgent.append(lambda: got.extend(pair_rates(0, tile, tile, lambda t: junk[:, t, :], t_m, 4)))
        urgent.extend([lambda: None] * 3 + [turn_])
        return st, M

    def cross(st, M, l):
        tm = [sb(f"c{l}t{i}", [P, NT, 512], F32, st) for i in range(2)]
        tm_free = [[], []]
        v = sb(f"c{l}v", [P, 2, D], F32, st)
        ss = [sb(f"c{l}ss{i}", [P, NT, 2], F32, st) for i in range(2)]
        kT = sb(f"c{l}kT", [P, 8, MEM], F32, st)
        qT = sb(f"c{l}qT", [P, 8, S], F32, st)
        tok = {"q": [], "k": [], "v": []}
        gains = {n: par(f"xa_{n}_gain{l}") for n in "qk"}

        def heads(which, nt, dst, g, bk, toks):
            b = g % 2
            got = head_rates(tm[b], nt, 2, 256, 512, ss[b], bk, toks, tm_free[b])
            tt = []

            def go():
                used = []
                tok[which].extend(turn(tm[b], tt, 4, home, [dst[:, 4 * g + c, :] for c in range(4)],
                                       [gains[which][:, c % 2:c % 2 + 1] for c in range(4)], nt, used))
                tm_free[b] = used
            home = banks[4 * (banks.index(bk[0]) // 4):4 * (banks.index(bk[0]) // 4) + 4]
            urgent.append(lambda: tt.extend(head_scale(tm[b], got, 2, 256, ss[b])))
            urgent.append(go)

        def on_kv(g, bk, toks):
            if g >= 2:
                heads("k", 2, kT, g - 2, bk, toks)
            else:
                for t in range(2):
                    e1 = copy_out(act if t % 2 else dve, v[:, t, 512 * g:512 * (g + 1)], bk[t].ap[:, :], toks[t])
                    bk[t].free = [e1]
                    tok["v"].append(e1)

        got = [[], []]
        four = [banks[i] for i in (2, 3, 6, 7)]
        for p in range(2):
            urgent.append(lambda p=p: got[p].extend(pair_rates(
                p, lambda t: x[:, t, :], lambda t: xn[t % 2][:, :], lambda t: xn[t % 2][:, :], xtok, 0)))
            urgent.append(lambda: None)
            urgent.append(lambda p=p: pair_turn(p, lambda t: xn[t % 2][:, :], got[p], par(f"xa_norm{l}"), hT, four))
        gemm(f"kv{l}", {"m": M}, on_kv)
        gemm(f"xq{l}", {"h": hT}, lambda g, bk, toks: heads("q", 4, qT, g, bk, toks))
        drain()

        def score(h, i, dst, k0, k1):
            for c in range(2):
                t = pe.do(lambda e, c=c: e.matmul(dst, qT[:, 2 * h + c, i * P:(i + 1) * P], kT[:, 2 * h + c, :],
                                                  start=c == 0, stop=c == 1),
                          tok["q"][2 * h + c], tok["k"][2 * h + c], mark=c == 1)
            return t

        def value(h, PTb):
            pe.wait(tok["v"])
            done_ = []
            for c in range(2):
                bank = banks[6 + c]
                pe.wait(bank.free)
                for kt in range(2):
                    t = pe.do(lambda e, kt=kt, c=c: e.matmul(
                        banks[6 + c].ap[:, :], v[:, kt, 256 * h + c * P:256 * h + (c + 1) * P], PTb[:, kt, :],
                        start=kt == 0, stop=kt == 1), mark=kt == 1)
                done_.append(t)

            def finish():
                for c in range(2):
                    banks[6 + c].free = [halves(banks[6 + c].ap[:, :], hT, 2 * h + c, slice(0, S), done_[c])]
            return t, finish

        junk = sb(f"c{l}jk", [P, D], F32, st)
        attend(st.sub(), f"cx{l}", 4, widths(lambda i: (0, 2), NT), score, value, hT, scale=1.0 / 16, nk=2)
        return junk

    def sparse_mixer(st):
        handover()
        a0 = st.at
        vals = sb("s_v", [P, NT, 256], F32, st)
        qT = sb("s_qT", [P, 8, S], F32, st)
        kT = sb("s_kT", [P, 4, S], F32, st)
        spans, total = causal_tiles
        sel = sb("s_sel", [P, total], F32, st)
        sc = sb("s_sc", [P, total], F32, st)
        iw = sb("s_iw", [P, NT, 8], F32, st)
        m8 = sb("s_m8", [P, 24], F32, st)
        a1 = st.at
        a2 = a1 + 32768
        tmp_area = Area(a1)
        tok = {"q": [], "k": [], "iq": [], "ik": [], "v": []}

        iqT = sb("s_iqT", [P, 4, S], F32, tmp_area)
        ikT = sb("s_ikT", [P, S], F32, tmp_area)
        tq = sb("s_tq", [P, NT, 512], F32, tmp_area)
        tq2 = sb("s_tq2", [P, NT, 512], F32, tmp_area)
        ti = sb("s_ti", [P, NT, 128], F32, tmp_area)
        rt = [sb(f"s_rt{i}", [P, 4, 64], F32, tmp_area) for i in range(2)]
        lng = sb("s_lng", [P, 2, 64], F32, tmp_area)
        bn = sb("s_bn", [P, NT, 10], F32, tmp_area)
        rl = [xn[0][:, 0:512], xn[0][:, 512:1024], xn[1][:, 0:512]]
        s_ln = sem("s_ln")
        pool.dma(lng[:, 0, :], T["idx_k_ln_g_2"].partition_broadcast(P), s_ln)
        t_ln = pool.dma(lng[:, 1, :], T["idx_k_ln_b_2"].partition_broadcast(P), s_ln)
        rt_free = [[], []]
        turns = [0]

        def rope(buf, t, nh, tok_):
            b = turns[0] % 2
            turns[0] += 1
            v3 = buf.rearrange("p (h d) -> p h d", d=64)
            x1, x2 = v3[:, :, 0:8], v3[:, :, 8:16]
            cs = mis("cos")[:, 8 * t:8 * t + 8].unsqueeze(1).to_broadcast([P, nh, 8])
            sn = mis("sin")[:, 8 * t:8 * t + 8].unsqueeze(1).to_broadcast([P, nh, 8])
            r = [rt[b][:, i, 0:8 * nh].rearrange("p (h d) -> p h d", d=8) for i in range(4)]
            pr = [pool.do(lambda e, o=o, a=a, c=c: e.tensor_tensor(o, a, c, ALU.mult), tok_, t_cst)
                  for o, a, c in ((r[0], x1, cs), (r[1], x2, sn), (r[2], x2, cs), (r[3], x1, sn))]
            pool.do(lambda e: e.tensor_tensor(x1, r[0], r[1], ALU.subtract), pr)
            return pool.do(lambda e: e.tensor_tensor(x2, r[2], r[3], ALU.add), pr)

        tq_free = []

        def on_idx(g, bk, toks):
            if g == 0:
                tt = []
                for t in range(NT):
                    e1 = copy_out(act, tq[:, t, :], bk[t].ap[:, :], toks[t])
                    bk[t].free = [e1]
                    tt.append(rope(tq[:, t, :], t, 8, e1))

                def go():
                    tok["iq"] = turn(tq, tt, 4, bk, [iqT[:, c, :] for c in range(4)], None, NT, tq_free)
                later.append(go)
                return
            tt = []
            for t in range(NT):
                e1 = copy_out(act, ti[:, t, 0:72], bk[t].ap[:, 0:72], toks[t])
                bk[t].free = [e1]
                k = ti[:, t, 0:64]
                w1 = pool.do(lambda e, t=t: e.tensor_scalar(iw[:, t, :], ti[:, t, 64:72], (8 ** -0.5) * (64 ** -0.5),
                                                            None, ALU.mult), e1)
                t1 = dve.do(lambda e, t=t, k=k: e.bn_stats(bn[:, t, 0:6], k), e1)
                t2 = dve.do(lambda e, t=t: e.bn_aggr(bn[:, t, 6:8], bn[:, t, 0:6]), t1)
                t3 = rstd(bn[:, t, 7:8], bn[:, t, 8:9], 1.0, t2)
                t4 = dve.do(lambda e, t=t, k=k: e.tensor_scalar(k, k, bn[:, t, 6:7], bn[:, t, 8:9], ALU.subtract,
                                                                ALU.mult), t3, t2)
                t5 = dve.do(lambda e, k=k: e.tensor_tensor(k, k, lng[:, 0, :], ALU.mult), t4, t_ln)
                t6 = dve.do(lambda e, k=k: e.tensor_tensor(k, k, lng[:, 1, :], ALU.add), t5)
                t7 = rope(k, t, 1, [t6, w1])
                tt.append(copy_out(pool, ti[:, t, 64:128], k, t7))

            def go():
                tok["ik"] = turn(ti, tt, 1, bk, [ikT[:, :]], None, NT, [])
            later.append(go)

        def on_qkv(g, bk, toks):
            tt = []
            buf = [tq2, tq, tq2][g]
            fr = [[], tq_free, tq_free2][g]
            for t in range(NT):
                e1 = copy_out(act, buf[:, t, :], bk[t].ap[:, :], toks[t], fr)
                bk[t].free = [e1]
                if g < 2:
                    tt.append(rope(buf[:, t, :], t, 8, e1))
                else:
                    r1 = rope(buf[:, t, 0:256], t, 4, e1)
                    tok["v"].append(copy_out(pool, vals[:, t, :], buf[:, t, 256:512], e1))
                    kv = tq[:, t, :].rearrange("p (h u d) -> p h u d", h=4, u=2)
                    k3 = buf[:, t, 0:256].rearrange("p (h d) -> p h d", h=4)
                    c1 = pool.do(lambda e, kv=kv, k3=k3: e.tensor_copy(kv[:, :, 0, :], k3), r1, tq_free3)
                    tt.append(pool.do(lambda e, kv=kv, k3=k3: e.tensor_copy(kv[:, :, 1, :], k3), c1))

            def go():
                if g < 2:
                    tok["q"].extend(turn(buf, tt, 4, bk, [qT[:, 4 * g + c, :] for c in range(4)], [0.125] * 4, NT,
                                         tq_free2 if g == 0 else tq_free3))
                else:
                    four[:] = bk
                    tok["k"] = turn(tq, tt, 4, bk, [kT[:, c, :] for c in range(4)], None, NT, [])
            later.append(go)
        tq_free2, tq_free3, four = [], [], []

        gemm("idx", {"h": hT}, on_idx)
        gemm("qkv", {"h": hT}, on_qkv)
        sctok, best = {}, {}

        def index_scores():
            rl_free = [list(xn_free[0]), list(xn_free[0]), list(xn_free[1])]
            n = 0
            for h in range(8):
                r = slice(64 * (h % 2), 64 * (h % 2) + 64)
                for i in range(1, NT):
                    _, _, o, W = spans[i]
                    bank = four[n % 4]
                    rb = rl[n % 3]
                    tk = pe.do(lambda e, r=r, h=h, i=i, W=W, bank=bank: e.matmul(
                        bank.ap[:, 0:W], iqT[r, h // 2, i * P:(i + 1) * P], ikT[r, 0:W], start=True, stop=True),
                        bank.free, tok["iq"][h // 2], tok["ik"])
                    t1 = act.do(lambda e, rb=rb, W=W, bank=bank: e.activation(rb[:, 0:W], bank.ap[:, 0:W], AF.Relu), tk,
                                rl_free[n % 3])
                    bank.free = [t1]
                    s_, w_ = sc[:, o:o + W], iw[:, i, h:h + 1]
                    if h == 0:
                        t2 = dve.do(lambda e, s_=s_, w_=w_, rb=rb, W=W: e.tensor_scalar(s_, rb[:, 0:W], w_, None, ALU.mult),
                                    t1, pool.now())
                    else:
                        t2 = dve.do(lambda e, s_=s_, w_=w_, rb=rb, W=W: e.scalar_tensor_tensor(
                            s_, rb[:, 0:W], w_, s_, ALU.mult, ALU.add), t1, sctok[i])
                    sctok[i] = t2
                    rl_free[n % 3] = [t2]
                    n += 1
            xn_free[0], xn_free[1] = rl_free[0] + rl_free[1], rl_free[2]
            handover()
            best[0] = dve.do(lambda e: e.tensor_copy(sel[:, 0:P], mis("causal")), t_cst)
            three = [select(i) for i in range(1, NT)]
            for r in range(18):
                for s_ in three:
                    background.append(s_[r])

        later.append(index_scores)

        def select(i):
            _, _, o, W = spans[i]
            s_, w_, m_ = sc[:, o:o + W], sel[:, o:o + W], m8[:, 8 * (i - 1):8 * i]
            dg = sc[:, o + W - P:o + W]

            def start():
                t = pool.do(lambda e: e.affine_select(out=dg, in_=dg, compare_op=ALU.is_ge, fill=FLOOR, base=0,
                                                      pattern=[[-1, P]], channel_multiplier=1), sctok[i])
                best[i] = dve.do(lambda e: e.tensor_copy(w_, s_), t)

            def round_():
                t = dve.do(lambda e: e.max(m_, w_), best[i])
                best[i] = dve.do(lambda e: e.match_replace(w_, m_, w_, TAKEN), t)

            def end():
                t = dve.do(lambda e: e.tensor_tensor(w_, w_, s_, ALU.is_equal), best[i])
                best[i] = dve.do(lambda e: e.tensor_scalar(w_, w_, NEG, None, ALU.mult), t)
            return [start] + [round_] * 16 + [end]

        y_area = Area(a1)
        Y = Act(sb("s_Yh", [P, KD, S], F32R, y_area), sb("s_Yl", [P, KD, S], F32R, y_area), S)
        rn = Area(a2)
        wa = sb("s_wa", [P, 8, P], F32, rn)
        wx = sb("s_wx", [P, 8, P], F32, rn)
        s_g = sem("s_g")
        pool.dma(wa[:, :, :], T["wa_l"], s_g)
        t_g = pool.dma(wx[:, :, :], T["wx_l"], s_g)
        xp = sb("s_xp", [P, 2, S + 3], F32, rn)
        xc = sb("s_xc", [P, 2, S], F32, rn)
        gr = xn[1][:, :].rearrange("p (j s) -> p j s", j=2)
        ra = sb("s_ra", [P, 2, S], F32, rn)
        ri = sb("s_ri", [P, 2, S], F32, rn)
        th = sb("s_th", [P, 2, S], F32, rn)
        t_pad = pool.do(lambda e: e.memset(xp[:, :, :], 0.0))
        fr = {"xp": [t_pad], "gr": [], "rest": []}

        def on_rnn(g, bk, toks):
            tc, tg = [], []
            for j in range(2):
                c = 2 * g + j
                e1 = copy_out(act, xp[:, j, 3:S + 3], bk[j].ap[:, :], toks[j], fr["xp"])
                bk[j].free = [e1]
                cw = lambda k, c=c: prm[:, PRM["conv_w"][0] + 8 * k + c:PRM["conv_w"][0] + 8 * k + c + 1]
                t1 = act.do(lambda e, j=j, c=c, cw=cw: e.activation(xc[:, j, :], xp[:, j, 0:S], AF.Identity,
                                                                    bias=par("conv_b")[:, c:c + 1], scale=cw(0)),
                            e1, fr["rest"])
                for k in range(1, 4):
                    t1 = dve.do(lambda e, j=j, k=k, cw=cw: e.scalar_tensor_tensor(
                        xc[:, j, :], xp[:, j, k:k + S], cw(k), xc[:, j, :], ALU.mult, ALU.add), t1)
                tc.append(t1)
            for j in range(2):
                e1 = act.do(lambda e, j=j: e.activation(gr[:, j, :], bk[2 + j].ap[:, :], AF.Gelu_apprx_tanh),
                            toks[2 + j], fr["gr"])
                bk[2 + j].free = [e1]
                tg.append(e1)
            fr["xp"] = list(tc)

            ts, tz, tu = [], [], []

            def gates():
                for j in range(2):
                    c = 2 * g + j
                    for m, (w_, bias_, dst) in enumerate(((wa, "rg_b_a", ra), (wx, "rg_b_x", ri))):
                        bank = bk[2 * j + m]
                        pe.wait(bank.free)
                        tk = pe.do(lambda e, w_=w_, c=c, j=j, bank=bank: e.matmul(
                            bank.ap[:, :], w_[:, c, :], xc[:, j, :], start=True, stop=True), t_g, tc[j])
                        t1 = act.do(lambda e, bank=bank, dst=dst, j=j, c=c, bias_=bias_: e.activation(
                            dst[:, j, :], bank.ap[:, :], AF.Sigmoid, bias=par(bias_)[:, c:c + 1]), tk, fr["rest"])
                        bank.free = [t1]
                        ts.append(t1)

            def rates():
                for j in range(2):
                    c = 2 * g + j
                    tz.append(act.do(lambda e, j=j, c=c: e.activation(th[:, j, :], ra[:, j, :], AF.Tanh,
                                                                      scale=coef[:, c:c + 1]), ts, t_coef, fr["rest"]))
                    ta_ = act.do(lambda e, j=j, c=c: e.activation(ra[:, j, :], ra[:, j, :], AF.Exp,
                                                                  scale=ncoef[:, c:c + 1]), ts, tz)
                    t1 = pool.do(lambda e, j=j: e.tensor_tensor(xc[:, j, :], xc[:, j, :], ri[:, j, :], ALU.mult), ts,
                                 pe.now())
                    t2 = pool.do(lambda e, j=j: e.tensor_tensor(ri[:, j, :], ra[:, j, :], ra[:, j, :], ALU.mult), t1,
                                 ta_)
                    tu.append((dve.do(lambda e, j=j: e.scalar_tensor_tensor(
                        th[:, j, :], ri[:, j, :], 1.0, th[:, j, :], ALU.add, ALU.mult), t2, tz[j]), ta_))

            def scan():
                for j in range(2):
                    c = 2 * g + j
                    t1 = act.do(lambda e, j=j: e.activation(th[:, j, :], th[:, j, :], AF.Sqrt), tu[j][0])
                    t2 = dve.do(lambda e, j=j: e.tensor_tensor(th[:, j, :], th[:, j, :], xc[:, j, :], ALU.mult), t1, tu[j][0])
                    t3 = dve.do(lambda e, j=j: e.tensor_tensor_scan(ri[:, j, :], ra[:, j, :], th[:, j, :], 0.0, ALU.mult,
                                                                    ALU.add), t2, tu[j][1])
                    t4 = dve.do(lambda e, j=j: e.tensor_tensor(gr[:, j, :], gr[:, j, :], ri[:, j, :], ALU.mult), t3,
                                tg[j])
                    t5 = halves(gr[:, j, :], Y, c, slice(0, S), t4)
                fr["gr"] = [t5]
                fr["rest"] = [t5]

            urgent.extend([lambda: None, gates, rates, scan])

        gemm("rnn", {"h": hT}, on_rnn, 1)
        mg_area, gb_area = Area(a2), Area(a1)
        Mg = sb("s_mg", [P, 8, S], F32, mg_area)
        GB = sb("s_gb", [P, 8, S], F32, gb_area)
        gt = [xn[i // 2][:, S * (i % 2):S * (i % 2) + S] for i in range(4)]
        gt_free = [xn_free[i // 2] for i in range(4)]
        gt_tok = {}
        mtok = {}

        def on_ya(g, bk, toks):
            for j in range(4):
                if g % 2 == 0:
                    gt_tok[j] = act.do(lambda e, j=j: e.activation(gt[j], bk[j].ap[:, :], AF.Sigmoid), toks[j],
                                       gt_free[j], fr["gr"])
                    bk[j].free = [gt_tok[j]]
                else:
                    if g == 1 and j == 0:
                        handover()
                    c = 4 * (g // 2) + j
                    mtok[c] = dve.do(lambda e, j=j, c=c: e.tensor_tensor(Mg[:, c, :], gt[j], bk[j].ap[:, :], ALU.mult),
                                     gt_tok[j], toks[j])
                    bk[j].free = [mtok[c]]
                    gt_free[j] = [mtok[c]]
                    xn_free[j // 2] = [mtok[c]]

        gtok = {}

        def on_gb(g, bk, toks):
            for c in range(4):
                t1 = act.do(lambda e, c=c: e.activation(GB[:, 4 * g + c, :], bk[c].ap[:, :], AF.Sigmoid), toks[c])
                bk[c].free = [t1]
                gtok[4 * g + c] = t1

        gemm("ya", {"h": hT, "y": Y}, on_ya, 2)
        drain()
        handover()
        gemm("gb", {"h": hT}, on_gb, 1)
        while background:
            background.pop(0)()
        handover()
        attend(Area(a2 + 16384), "sx", 16, causal_tiles, causal_scores(qT, kT, tok["q"], tok["k"], lambda h: h // 4, True),
                   pair_values(lambda h, kt: vals[:, kt, 64 * (h // 4):64 * (h // 4) + 64], hT, 0, None, True, tok["v"]),
                   hT, bias=lambda h, i, W: (sel[:, spans[i][2]:spans[i][2] + W], [best[i]]), st2=Area(a1 + 16384))
        handover()
        Z = Act(sb("s_Zh", [P, KD, S], F32R, Area(a1 + 16384)), sb("s_Zl", [P, KD, S], F32R, Area(a0 + 4096)), S)

        def on_yb(g, bk, toks):
            for c in range(4):
                k = 4 * g + c
                t1 = dve.do(lambda e, c=c, k=k: e.tensor_tensor(GB[:, k, :], GB[:, k, :], bk[c].ap[:, :], ALU.mult),
                            toks[c], gtok[k])
                bk[c].free = [t1]
                t2 = dve.do(lambda e, k=k: e.tensor_tensor(GB[:, k, :], GB[:, k, :], Mg[:, k, :], ALU.add), t1, mtok[k])
                halves(GB[:, k, :], Z, k, slice(0, S), t2)

        gemm("yb", {"h": hT}, on_yb)
        post_norm(Area(a2 + 16384), "wo", {"y": Z}, "s_", T["norm_mix_post_2"])

    def post_norm(area, name, acts, tag, gain):
        gb = sb(tag + "pg", [P, D], F32, area)
        s_p = sem(tag + "s_pg")
        t_p = pool.dma(gb[:, :], gain.partition_broadcast(P), s_p)
        held = []
        gemm(name, acts, lambda g, bk, toks: held.append((bk, toks)))
        def tile(t):
            b = t % 2
            two = [(held[g][0][t], held[g][1][t], slice(512 * g, 512 * g + 512)) for g in range(2)]
            t1 = [act.do(lambda e, k=k, c=c, g=g: e.activation(xn[b][:, c], k.ap[:, :], AF.Square,
                                                              accum_out=stat[:, 4 * g + t:4 * g + t + 1]),
                         tk, xn_free[b], stat_free) for g, (k, tk, c) in enumerate(two)]
            r = stat[:, 8 + t:9 + t]
            t2 = pool.do(lambda e: e.tensor_tensor(r, stat[:, t:t + 1], stat[:, 4 + t:5 + t], ALU.add), t1, stat_free)
            t2 = rstd(r, r, 1.0 / D, t2)
            t3 = [dve.do(lambda e, k=k, c=c: e.scalar_tensor_tensor(xn[b][:, c], k.ap[:, :], r, gb[:, c], ALU.mult,
                                                                    ALU.mult), t1, t2, t_p) for k, _, c in two]
            for k, _, _ in two:
                k.free = [t3[1]]
            t4 = dve.do(lambda e: e.tensor_tensor(x[:, t, :], x[:, t, :], xn[b][:, :], ALU.add), t3, xtok[t])
            xtok[t] = [t4]
            xn_free[b] = [t4]
            return t4

        for t in range(NT):
            t4 = tile(t)
        stat_free[:] = [t4]

    def ffn(up, down, tag, after):
        area = Area(base)
        handover()
        F = Act(sb(tag + "Fh", [P, KF, S], F32R, area), sb(tag + "Fl", [P, KF, S], F32R, area), S)
        sg = [sb(f"{tag}sg{i}", [P, S], F32, area) for i in range(2)]
        pr = [sb(f"{tag}pr{i}", [P, S], F32, area) for i in range(2)]
        sg_free, pr_free = [[], []], [[], []]

        def on_group(g, bk, toks):
            for j in range(2):
                t1 = act.do(lambda e, j=j: e.activation(sg[j][:, :], bk[j].ap[:, :], AF.Silu), toks[j], sg_free[j])
                bk[j].free = [t1]
                t2 = dve.do(lambda e, j=j: e.tensor_tensor(pr[j][:, :], sg[j][:, :], bk[2 + j].ap[:, :], ALU.mult),
                            t1, toks[2 + j], pr_free[j])
                bk[2 + j].free = [t2]
                sg_free[j] = [t2]
                pr_free[j] = [halves(pr[j][:, :], F, 2 * g + j, slice(0, S), t2)]

        gemm(up, {"h": hT}, on_group)
        after(area, down, {"f": F})

    def half_added(gain):
        def after(area, name, acts):
            junk = sb(name + "jk", [P, D], F32, area)
            gemm(name, acts, add_to_x(0.5, norm_steps(par(gain), hT, junk)))
        return after

    def whole():
        norm(par("ffn1_norm0"), hT, lambda: advance(-2))
        recurrence_rates()
        for l in range(2):
            ffn(f"f1u{l}", f"f1d{l}", f"f1{l}", half_added(f"mix_norm{l}"))
            if stop == f"f1{l}":
                return
            (even_mixer if l == 0 else odd_mixer)(Area(base))
            memory = cross_memory(Area(base), l)
            gemm(f"out{l}", {"h": hT}, add_to_x(1.0))
            if stop == f"mix{l}":
                return
            junk = cross(*memory, l)
            gemm(f"xo{l}", {"h": hT}, add_to_x(1.0, norm_steps(par(f"ffn2_norm{l}"), hT, junk)))
            if stop == f"xa{l}":
                return
            ffn(f"f2u{l}", f"f2d{l}", f"f2{l}", half_added("norm_mix_pre" if l else "ffn1_norm1"))
            if stop == f"f2{l}":
                return
        sparse_mixer(Area(base))
        if stop == "sp":
            return
        norm(par("norm_ffn_pre"), hT)
        ffn("f3u", "f3d", "f3", lambda area, name, acts: post_norm(area, name, acts, "f3", T["norm_ffn_post_2"]))

    whole()
    for t in range(NT):
        sp.dma(out[0, t * P:(t + 1) * P, :], x[:, t, :], s_st, xtok[t])
    sp.wait((s_st, s_st.count))

    with nc.Block() as block:
        block.sync(lambda e: sp.play(e))
        block.tensor(lambda e: pe.play(e))
        block.scalar(lambda e: act.play(e))
        block.vector(lambda e: dve.play(e))
        block.gpsimd(lambda e: pool.play(e))
    ctx.close()


def shape_tables():
    p = np.arange(P)[:, None]
    misc = np.zeros((P, NMISC), np.float32)
    f = np.arange(P)[None, :]
    misc[:, 0:128] = p == f
    misc[:, 128:256] = np.where(f < p, 0.0, NEG)
    misc[:, 256:384] = np.where(f <= p, 0.0, NEG)
    inv = (np.float32(500000.0) ** (-np.arange(8, dtype=np.float32) / np.float32(8))).astype(np.float32)
    ang = (np.arange(S, dtype=np.float32)[:, None] * inv[None, :]).astype(np.float32)
    for name, fn in (("cos", np.cos), ("sin", np.sin)):
        o = MISC[name][0]
        misc[:, o:o + 32] = fn(ang.astype(np.float64)).reshape(NT, P, 8).transpose(1, 0, 2).reshape(P, 32)
    d = p + 128 - np.arange(256)[None, :]
    evb = [np.where((d >= 0) & (d <= 127), -(2.0 ** -(h + 1)) * d, NEG) for h in range(8)]
    d = p + 384 - np.arange(512)[None, :]
    c = ((d >= 0) & (d <= 128)).astype(int) + ((d >= 0) & (d % 4 == 0)) + ((d >= 0) & (d % 16 == 0))
    odb = [np.where(c > 0, -np.float64(np.float32(2.0 ** (-8.0 * (h + 1) / 16))) * d
                    + np.log(np.maximum(c, 1)), NEG) for h in range(16)]
    return misc, np.concatenate(evb, 1).astype(np.float32), np.concatenate(odb, 1).astype(np.float32)


_DIRECT = ["x", "mem", "ffn1_w_gu", "ffn1_w_down", "ev_w_in", "ev_w_out", "od_w_in", "od_w_out", "xa_w_q", "xa_w_kv",
           "xa_w_o", "ffn2_w_gu", "ffn2_w_down", "w_in_2", "idx_k_ln_g_2", "idx_k_ln_b_2", "w_rnn_out_2",
           "w_att_out_2", "w_o_2", "norm_mix_post_2", "w_ffn_gate_2", "w_ffn_up_2", "w_ffn_down_2", "norm_ffn_post_2"]


def lay_out(inputs):
    a = {n: np.ascontiguousarray(inputs[n]) for n in _DIRECT}
    for n in ("idx_k_ln_g_2", "idx_k_ln_b_2", "norm_mix_post_2", "norm_ffn_post_2"):
        a[n] = a[n].reshape(-1)
    g = {n: np.asarray(v) for n, v in inputs.items() if n not in _DIRECT}

    def col(v):
        return v.reshape(-1, P).T

    def twice(v):
        return np.concatenate([v, v]).reshape(P, 1)

    parts = []
    for l in range(2):
        parts += [col(g[n][l]) for n in ("ffn1_norm", "mix_norm", "xa_norm", "xa_mem_norm", "ffn2_norm", "xa_q_gain",
                                         "xa_k_gain")]
    parts += [twice(g[n][0]) for n in ("ev_q_gain", "ev_k_gain", "od_q_gain", "od_k_gain")]
    parts.append(np.broadcast_to(g["ev_sinks"][0][None, :], (P, 8)))
    parts += [col(g[n + "_2"][0]) for n in ("norm_mix_pre", "norm_ffn_pre", "conv_b", "rg_b_a", "rg_b_x", "rg_lambda")]
    parts += [col(g["conv_w_2"][0][k]) for k in range(4)]
    a["prm"] = np.ascontiguousarray(np.concatenate(parts, axis=1))
    for n, s in (("wa_l", "rg_w_a_2"), ("wx_l", "rg_w_x_2")):
        w = np.zeros((2, 64, 8, 2, 64), np.float32)
        for u in range(2):
            w[u, :, :, u, :] = g[s][0][u::2].transpose(1, 0, 2)
        a[n] = w.reshape(P, 8, P)
    a["misc"], a["evb"], a["odb"] = shape_tables()
    return a


def kernel(**inputs):
    import concourse.bacc as _bacc
    from concourse.bass_utils import run_bass_kernel_spmd as _run

    nc = _bacc.Bacc("TRN2", target_bir_lowering=False, num_devices=1)
    arrays, T = {}, {}
    for name, a in lay_out(inputs).items():
        arrays[f"in_{name}"] = a
        T[name] = nc.dram_tensor(f"in_{name}", a.shape, mybir.dt.from_np(a.dtype), kind="ExternalInput").ap()
    out = nc.dram_tensor("out_x", (1, S, D), F32, kind="ExternalOutput").ap()
    program(nc, T, out)
    r = _run(nc, [arrays], core_ids=[0])
    return r.results[0]["out_x"]
```
